# Optimizing a Trainium2 kernel written in Bass

```python
import math
import jax, jax.numpy as jnp
from jax import lax
import numpy as np

D_MODEL = 1024
BATCH = 1
SEQ = 512
DEPTH = 1
DEC_BATCH = 8
DEC_SEQ = 1
PAST_LEN = 1024
PAGE_SIZE = 128

LRU_WIDTH = D_MODEL // 2
LRU_BLOCKS = 8
LRU_BLOCK = LRU_WIDTH // LRU_BLOCKS
CONV_WIDTH = 4
LRU_C = 8.0
N_HEADS = 8
N_KV_HEADS = 2
HEAD_DIM = 64
Q_PER_KV = N_HEADS // N_KV_HEADS
ATTN_WIDTH = N_HEADS * HEAD_DIM
KV_WIDTH = N_KV_HEADS * HEAD_DIM
WINDOW = 128
BLOCK = 128
MIX_WIDTH = LRU_WIDTH + ATTN_WIDTH
IN_WIDTH = 2 * LRU_WIDTH + ATTN_WIDTH + 2 * KV_WIDTH
SPLITS = (LRU_WIDTH, 2 * LRU_WIDTH, 2 * LRU_WIDTH + ATTN_WIDTH, 2 * LRU_WIDTH + ATTN_WIDTH + KV_WIDTH)
N_GROUPS = 4
EXPERTS_PER_GROUP = 8
N_EXPERTS = N_GROUPS * EXPERTS_PER_GROUP
TOP_K = 2
D_EXPERT = D_MODEL // 4
DEEPNORM_ALPHA = (2.0 * DEPTH) ** 0.25
DEEPNORM_BETA = (8.0 * DEPTH) ** -0.25
LN_EPS = 1e-5
RMS_EPS = 1e-6

kernel_name = 'hymba_rglru_swa_sink_hier_moe_deepnorm_step'

def layer_norm(x, g, b):
    xf = x.astype(jnp.float32)
    mu = jnp.mean(xf, -1, keepdims=True)
    var = jnp.mean(jnp.square(xf - mu), -1, keepdims=True)
    return ((xf - mu) * lax.rsqrt(var + LN_EPS) * g + b).astype(x.dtype)

def rms_norm(x, g):
    xf = x.astype(jnp.float32)
    return (xf * lax.rsqrt(jnp.mean(xf * xf, -1, keepdims=True) + RMS_EPS) * g).astype(x.dtype)

def ada_modulation(c, w_ada, b_ada):
    m = jax.nn.silu(c) @ w_ada + b_ada
    return [t[:, None, :] for t in jnp.split(m, 6, axis=-1)]

def causal_conv(u, ctx, w, b):
    T = u.shape[1]
    up = jnp.concatenate([ctx.astype(u.dtype), u], axis=1)
    out = b + sum(w[k] * up[:, k:k + T] for k in range(CONV_WIDTH))
    return out, up[:, -(CONV_WIDTH - 1):]

def block_diag(x, w, b):
    xb = x.reshape(x.shape[:-1] + (LRU_BLOCKS, LRU_BLOCK))
    return (jnp.einsum('btnd,nde->btne', xb, w) + b).reshape(x.shape)

def rg_lru(x, h0, w_a, b_a, w_x, b_x, lam):
    xf = x.astype(jnp.float32)
    r = jax.nn.sigmoid(block_diag(xf, w_a, b_a))
    i = jax.nn.sigmoid(block_diag(xf, w_x, b_x))
    log_a = -LRU_C * r * jax.nn.softplus(-lam.astype(jnp.float32))
    a = jnp.exp(log_a)
    bterm = jnp.sqrt(-jnp.expm1(2.0 * log_a)) * (i * xf)

    def combine(e1, e2):
        a1, b1 = e1
        a2, b2 = e2
        return a1 * a2, a2 * b1 + b2

    A, Bc = lax.associative_scan(combine, (a, bterm), axis=1)
    h = A * h0.astype(jnp.float32)[:, None, :] + Bc
    return h, h[:, -1]

def sink_softmax(s, mask, sinks):
    s = jnp.where(mask, s, -jnp.inf)
    sk = sinks.astype(jnp.float32).reshape(N_KV_HEADS, Q_PER_KV)[:, :, None, None]
    sk = jnp.broadcast_to(sk, s.shape[:-1] + (1,))
    p = jax.nn.softmax(jnp.concatenate([s, sk], axis=-1), axis=-1)
    return p[..., :-1]

def window_attention_prompt(q, k, v, sinks):
    Bn, T = q.shape[:2]
    nb = T // BLOCK
    qb = q.reshape(Bn, nb, BLOCK, N_KV_HEADS, Q_PER_KV, HEAD_DIM)

    def band(z):
        zb = z.reshape(Bn, nb, BLOCK, N_KV_HEADS, HEAD_DIM)
        prev = jnp.pad(zb, ((0, 0), (1, 0), (0, 0), (0, 0), (0, 0)))[:, :-1]
        return jnp.concatenate([prev, zb], axis=2)

    kb, vb = band(k), band(v)
    s = jnp.einsum('bnqkgd,bnskd->bnkgqs', qb, kb).astype(jnp.float32) * (HEAD_DIM ** -0.5)
    qi = jnp.arange(BLOCK)[:, None]
    sj = jnp.arange(2 * BLOCK)[None, :]
    rel = BLOCK + qi - sj
    local = (rel >= 0) & (rel <= WINDOW)
    no_prev = (jnp.arange(nb)[:, None, None] == 0) & (sj[None] < BLOCK)
    mask = (local[None] & ~no_prev)[None, :, None, None]
    p = sink_softmax(s, mask, sinks)
    o = jnp.einsum('bnkgqs,bnskd->bnqkgd', p.astype(vb.dtype), vb)
    return o.reshape(Bn, T, ATTN_WIDTH)

def window_attention_sample(q, k, v, k_buf, v_buf, sinks):
    Bn, S = q.shape[:2]
    kk = jnp.concatenate([k_buf.astype(k.dtype), k], axis=1)
    vv = jnp.concatenate([v_buf.astype(v.dtype), v], axis=1)
    qg = q.reshape(Bn, S, N_KV_HEADS, Q_PER_KV, HEAD_DIM)
    s = jnp.einsum('bqkgd,bskd->bkgqs', qg, kk).astype(jnp.float32) * (HEAD_DIM ** -0.5)
    j = jnp.arange(S)[:, None]
    m = jnp.arange(WINDOW + S)[None, :]
    mask = (m >= j) & (m <= WINDOW + j)
    p = sink_softmax(s, mask, sinks)
    o = jnp.einsum('bkgqs,bskd->bqkgd', p.astype(vv.dtype), vv)
    return o.reshape(Bn, S, ATTN_WIDTH), kk[:, -WINDOW:], vv[:, -WINDOW:]

def hier_moe(h, w_group, b_group, w_router, b_router, w_gate, w_up, w_down):
    hf = h.astype(jnp.float32)
    pg = jax.nn.softmax(hf @ w_group + b_group, axis=-1)
    g_val, g_idx = lax.top_k(pg, 1)
    logits_all = jnp.einsum('btd,gde->btge', hf, w_router) + b_router
    onehot_g = jax.nn.one_hot(g_idx[..., 0], N_GROUPS, dtype=jnp.float32)
    pe = jax.nn.softmax(jnp.einsum('btge,btg->bte', logits_all, onehot_g), axis=-1)
    e_val, e_idx = lax.top_k(pe, TOP_K)
    weight = g_val * e_val / jnp.sum(e_val, -1, keepdims=True)
    expert = g_idx * EXPERTS_PER_GROUP + e_idx
    combine = jnp.sum(jax.nn.one_hot(expert, N_EXPERTS, dtype=jnp.float32) * weight[..., None], axis=-2)
    a = jnp.einsum('btd,edf->btef', h, w_gate)
    u = jnp.einsum('btd,edf->btef', h, w_up)
    z = jax.nn.silu(a) * u * combine[..., None].astype(a.dtype)
    return jnp.einsum('btef,efd->btd', z, w_down).astype(h.dtype)

def decoder_layer(x, c, conv_ctx, h0, k_buf, v_buf, lw):
    (w_ada, b_ada, w_in, conv_w, conv_b, w_rg_a, b_rg_a, w_rg_x, b_rg_x, lru_lambda, sinks,
     g_lru, g_attn, w_out, ln1_g, ln1_b, w_group, b_group, w_router, b_router,
     w_gate, w_up, w_down, ln2_g, ln2_b) = lw
    Bn, T = x.shape[:2]
    sh1, sc1, gt1, sh2, sc2, gt2 = ada_modulation(c, w_ada, b_ada)
    h = x * (1.0 + sc1) + sh1
    zin = h @ w_in
    xb, gate, q, k, v = jnp.split(zin, SPLITS, axis=-1)
    xc, conv_state = causal_conv(xb, conv_ctx, conv_w, conv_b)
    hs, h_last = rg_lru(xc, h0, w_rg_a, b_rg_a, w_rg_x, b_rg_x, lru_lambda)
    y_lru = (hs * jax.nn.gelu(gate.astype(jnp.float32))).astype(x.dtype)
    q = q.reshape(Bn, T, N_HEADS, HEAD_DIM)
    k = k.reshape(Bn, T, N_KV_HEADS, HEAD_DIM)
    v = v.reshape(Bn, T, N_KV_HEADS, HEAD_DIM)
    if k_buf is None:
        y_att = window_attention_prompt(q, k, v, sinks)
        k_new, v_new = k[:, -WINDOW:], v[:, -WINDOW:]
    else:
        y_att, k_new, v_new = window_attention_sample(q, k, v, k_buf, v_buf, sinks)
    mix = jnp.concatenate([rms_norm(y_lru, g_lru), rms_norm(y_att, g_attn)], axis=-1) @ w_out
    x = layer_norm(DEEPNORM_ALPHA * x + (1.0 + gt1) * mix, ln1_g, ln1_b)
    h = x * (1.0 + sc2) + sh2
    f = hier_moe(h, w_group, b_group, w_router, b_router, w_gate, w_up, w_down)
    x = layer_norm(DEEPNORM_ALPHA * x + (1.0 + gt2) * f, ln2_g, ln2_b)
    return x, conv_state, h_last, k_new, v_new

def setup_inputs(seed: int = 0) -> dict:
    key = jax.random.key(seed)
    ks = jax.random.split(key, 40)
    f32 = jnp.float32
    L = DEPTH

    def nrm(k, shape, scale):
        return jax.random.normal(k, shape, f32) * scale

    w_in = nrm(ks[8], (L, D_MODEL, IN_WIDTH), D_MODEL ** -0.5)
    w_in = w_in.at[..., IN_WIDTH - KV_WIDTH:].multiply(DEEPNORM_BETA)
    a_c = jax.random.uniform(ks[15], (L, LRU_WIDTH), f32, 0.9, 0.999)
    s = a_c ** (1.0 / LRU_C)
    lru_lambda = jnp.log(s) - jnp.log1p(-s)
    return {
        'x_prompt': nrm(ks[0], (BATCH, SEQ, D_MODEL), 1.0),
        'x_sample': nrm(ks[1], (DEC_BATCH, DEC_SEQ, D_MODEL), 1.0),
        'c_prompt': nrm(ks[2], (BATCH, D_MODEL), 1.0),
        'c_sample': nrm(ks[3], (DEC_BATCH, D_MODEL), 1.0),
        'state_conv': nrm(ks[4], (L, DEC_BATCH, CONV_WIDTH - 1, LRU_WIDTH), 1.0),
        'state_h': nrm(ks[5], (L, DEC_BATCH, LRU_WIDTH), 0.5),
        'cache_k': nrm(ks[6], (L, DEC_BATCH, WINDOW, N_KV_HEADS, HEAD_DIM), 1.0),
        'cache_v': nrm(ks[7], (L, DEC_BATCH, WINDOW, N_KV_HEADS, HEAD_DIM), DEEPNORM_BETA),
        'w_ada': nrm(ks[9], (L, D_MODEL, 6 * D_MODEL), 0.1 * D_MODEL ** -0.5),
        'b_ada': nrm(ks[10], (L, 6 * D_MODEL), 0.01),
        'w_in': w_in,
        'conv_w': nrm(ks[11], (L, CONV_WIDTH, LRU_WIDTH), CONV_WIDTH ** -0.5),
        'conv_b': nrm(ks[12], (L, LRU_WIDTH), 0.01),
        'w_rg_a': nrm(ks[13], (L, LRU_BLOCKS, LRU_BLOCK, LRU_BLOCK), LRU_BLOCK ** -0.5),
        'b_rg_a': nrm(ks[14], (L, LRU_BLOCKS, LRU_BLOCK), 0.01),
        'w_rg_x': nrm(ks[16], (L, LRU_BLOCKS, LRU_BLOCK, LRU_BLOCK), LRU_BLOCK ** -0.5),
        'b_rg_x': nrm(ks[17], (L, LRU_BLOCKS, LRU_BLOCK), 0.01),
        'lru_lambda': lru_lambda,
        'sinks': nrm(ks[18], (L, N_HEADS), 1.0),
        'g_lru': 1.0 + nrm(ks[19], (L, LRU_WIDTH), 0.01),
        'g_attn': 1.0 + nrm(ks[20], (L, ATTN_WIDTH), 0.01),
        'w_out': nrm(ks[21], (L, MIX_WIDTH, D_MODEL), DEEPNORM_BETA * MIX_WIDTH ** -0.5),
        'ln1_g': 1.0 + nrm(ks[22], (L, D_MODEL), 0.01),
        'ln1_b': nrm(ks[23], (L, D_MODEL), 0.01),
        'w_group': nrm(ks[24], (L, D_MODEL, N_GROUPS), D_MODEL ** -0.5),
        'b_group': nrm(ks[25], (L, N_GROUPS), 0.01),
        'w_router': nrm(ks[26], (L, N_GROUPS, D_MODEL, EXPERTS_PER_GROUP), D_MODEL ** -0.5),
        'b_router': nrm(ks[27], (L, N_GROUPS, EXPERTS_PER_GROUP), 0.01),
        'w_gate': nrm(ks[28], (L, N_EXPERTS, D_MODEL, D_EXPERT), D_MODEL ** -0.5),
        'w_up': nrm(ks[29], (L, N_EXPERTS, D_MODEL, D_EXPERT), D_MODEL ** -0.5),
        'w_down': nrm(ks[30], (L, N_EXPERTS, D_EXPERT, D_MODEL), DEEPNORM_BETA * D_EXPERT ** -0.5),
        'ln2_g': 1.0 + nrm(ks[31], (L, D_MODEL), 0.01),
        'ln2_b': nrm(ks[32], (L, D_MODEL), 0.01),
    }

def reference(x_prompt, x_sample, c_prompt, c_sample, state_conv, state_h, cache_k, cache_v,
              w_ada, b_ada, w_in, conv_w, conv_b, w_rg_a, b_rg_a, w_rg_x, b_rg_x, lru_lambda, sinks,
              g_lru, g_attn, w_out, ln1_g, ln1_b, w_group, b_group, w_router, b_router,
              w_gate, w_up, w_down, ln2_g, ln2_b):
    xp, xs = x_prompt, x_sample
    conv_p, h_p, k_p, v_p = [], [], [], []
    conv_s, h_s, k_s, v_s = [], [], [], []
    for l in range(DEPTH):
        lw = (w_ada[l], b_ada[l], w_in[l], conv_w[l], conv_b[l], w_rg_a[l], b_rg_a[l], w_rg_x[l],
              b_rg_x[l], lru_lambda[l], sinks[l], g_lru[l], g_attn[l], w_out[l], ln1_g[l], ln1_b[l],
              w_group[l], b_group[l], w_router[l], b_router[l], w_gate[l], w_up[l], w_down[l],
              ln2_g[l], ln2_b[l])
        zero_ctx = jnp.zeros((xp.shape[0], CONV_WIDTH - 1, LRU_WIDTH), xp.dtype)
        zero_h = jnp.zeros((xp.shape[0], LRU_WIDTH), jnp.float32)
        xp, cp, hp, kp, vp = decoder_layer(xp, c_prompt, zero_ctx, zero_h, None, None, lw)
        xs, cs, hs, kss, vss = decoder_layer(xs, c_sample, state_conv[l], state_h[l], cache_k[l], cache_v[l], lw)
        conv_p.append(cp); h_p.append(hp); k_p.append(kp); v_p.append(vp)
        conv_s.append(cs); h_s.append(hs); k_s.append(kss); v_s.append(vss)
    return (xp, xs,
            jnp.stack(conv_p), jnp.stack(h_p), jnp.stack(k_p), jnp.stack(v_p),
            jnp.stack(conv_s), jnp.stack(h_s), jnp.stack(k_s), jnp.stack(v_s))


_drawn_inputs = setup_inputs


def setup_inputs(seed=0):
    import zlib

    import numpy as np

    out = dict(_drawn_inputs(seed))
    spreads = {}
    factors = {'b_rg_a': 8.0,
     'b_rg_x': 8.0,
     'sinks': 6.683,
     'g_lru': 8.0,
     'g_attn': 7.782,
     'ln1_g': 3.756,
     'ln1_b': 4.549,
     'b_group': 7.217,
     'ln2_g': 33.158,
     'ln2_b': 31.742,
     'b_router': 8.0}
    for name, (base, spread) in spreads.items():
        noise = np.random.default_rng([zlib.crc32(name.encode()), seed]).standard_normal(out[name].shape)
        drawn = base * np.exp(spread * noise) if base else spread * noise
        out[name] = __import__('jax').numpy.asarray(drawn.astype(out[name].dtype))
    for name, factor in factors.items():
        out[name] = (out[name] * factor).astype(out[name].dtype)
    return out
```

```python
import concourse.bass as bass
from concourse import mybir
from contextlib import ExitStack

F32 = mybir.dt.float32
BF16 = mybir.dt.bfloat16
I32 = mybir.dt.int32
U32 = mybir.dt.uint32
ALU = mybir.AluOpType
ACT = mybir.ActivationFunctionType
AX = mybir.AxisListType

P = 128
D = 1024
KD = D // P
T = 512
NS = 8
NT = T + NS
TT = T // P
HALF = 256
NC = NS + 1
W = 512
FW = W // P
INW = 1792
CW = 4
LB = 64
NH, NKV, HD = 8, 2, 64
G = NH // NKV
WIN = 128
NG, EPG, NE = 4, 8, 32
DE = 256
CAP = 64
NPAIR = NE // 2
ROUNDS = (NT + CAP - 1) // CAP
SLOTS = NE * CAP
ALPHA = 2.0 ** 0.25
LN_EPS = 1e-5
RMS_EPS = 1e-6
SCALE = HD ** -0.5
NEG = -1e30
NOWHERE = 1 << 20
CONV = T + CW - 1 + NS * CW
XC = CONV - (CW - 1)
S0 = T + CW - 1
XH = XC // 2


def build(nc, A, O):
    ctx = ExitStack()
    with ctx:
        base = (nc.sbuf_base + 63) // 64 * 64
        size = {"x": 20480, "h": 16640, "y": 16640, "w": 32768, "m": 20480, "r": 98304}
        at, here = {}, base
        for k, v in size.items():
            at[k] = here
            here += v
        small_at = [here]

        def place(name, shape, off, dt=F32):
            return nc.alloc_sbuf_tensor_at(name, shape, dt, offset=off)

        def row(name, shape, region, off, dt=F32):
            return place(name, shape, at[region] + off, dt)

        def small(name, shape, dt=F32):
            n = 1
            for s in shape[1:]:
                n *= s
            n *= 2 if dt == BF16 else 4
            t = place(name, shape, small_at[0], dt)
            small_at[0] += (n + 31) // 32 * 32
            assert small_at[0] <= nc.sbuf_usable_end, small_at
            return t

        x_tok = row("x_tok", [P, TT + 1, D], "x", 0)
        hT = row("hT", [P, KD, NT], "h", 0)
        yT = row("yT", [P, 2 * FW, NT], "y", 0)
        xb = row("xb", [P, 2, CONV], "w", 0)
        xc = row("xc", [P, 3, XC], "w", 4384)
        tr = row("tr", [P, XC], "w", 10912)
        ti = row("ti", [P, XC], "w", 13088)
        aa = row("aa", [P, XC], "w", 15264)
        th = row("th", [P, XC], "w", 17440)
        a2 = row("a2", [P, XC], "w", 19616)
        wrg = row("wrg", [P, 2, FW, P], "w", 21792)
        m_sb = row("m_sb", [P, 3, 512], "w", 25888)
        gel = row("gel", [P, FW, NT], "w", 0)
        wout = row("wout", [P, KD, D], "w", 0)
        X = row("X", [P, 2, D], "w", 0)
        XT = row("XT", [P, 2, KD, P], "w", 8192)
        silu_g = row("silu_g", [P, DE], "w", 16384)
        z = row("z", [P, DE], "w", 17408)
        zT = row("zT", [P, 2, P], "w", 18432)
        yo = row("yo", [P, 2, D], "w", 19456)
        kc = row("kc", [P, NS, P], "m", 0)
        kbT = row("kbT", [P, NS, WIN + 1], "m", 4096)
        vc = row("vc", [P, NS, P], "m", 8224)
        ps = row("ps", [P, 2, WIN + 1], "m", 12320)
        psT = row("psT", [P, 2, P], "m", 13376)
        qz = row("qz", [P, NS, 32], "m", 14400)
        pnd = row("pnd", [NS, 2, P], "m", 15424)
        pnm = row("pnm", [P, 2, NS], "m", 16448)
        knv = row("knv", [NS, 2, P], "m", 16512)
        klast = row("klast", [P, P], "m", 17536)
        tails = row("tails", [20, FW, P], "m", 18048)
        mod = row("mod", [P, 5, D], "m", 0)
        sq = row("sq", [P, 2 * FW, NT], "h", 0)
        smod = row("smod", [NS, 4, D], "h", 0)
        ada = row("ada", [P, 4, 2048], "r", 0)
        win = row("win", [P, 3, KD, 256], "r", 32768)
        crow = row("crow", [NC, D], "r", 57344)
        csil = row("csil", [NC, D], "r", 61440)
        fill = row("fill", [P, ROUNDS * SLOTS // P * 2], "r", 65536, I32)
        prm = row("prm", [40, P], "r", 66688)
        stt_in = row("stt_in", [32, W], "r", 67200)
        b_row = row("b_row", [P, 3, 512], "y", 4 * NT * 4)
        cT = row("cT", [P, KD, 32], "r", 96448)
        mT = row("mT", [P, 2, KD, NC], "r", 97472)
        qT = row("qT", [P, FW, NT], "r", 71744)
        kTz = row("kTz", [P, NKV, 2, T], "r", 57344)
        vtok = row("vtok", [P, TT, P], "r", 65536)
        kvT = row("kvT", [P, 2, NT], "r", 67584)
        PT = row("PT", [P, 2, NKV, G * P], "r", 80064)
        Pm = [row("P0", [P, NH, 2 * P], "r", 88256), row("P1", [P, NH, 2 * P], "h", 4 * NT * 4)]
        u = row("u", [P, 2, D], "r", 73728)
        h2 = row("h2", [P, 2, D], "r", 81920)
        h2T = row("h2T", [P, KD, P], "r", 90112)
        wr = row("wr", [P, KD, NG + NE], "r", 94208)
        LGT = row("LGT", [NG + NE, P], "r", 95360)
        lg = row("lg", [P, NG + NE], "r", 95872)
        le = row("le", [P, NE], "r", 96032)
        oh = row("oh", [P, 2, NE], "r", 96160)
        rs = row("rs", [P, 264], "r", 96448)
        EXB = 24576
        wgu = [row(f"wgu{s}", [P, 2, KD, DE], "r", s * EXB) for s in range(4)]
        wdn = [row(f"wdn{s}", [P, 2, D], "r", s * EXB + 16384) for s in range(4)]
        yy = row("yy", [P, TT + 1, 2, D], "r", 0)
        ff = row("ff", [P, 2, D], "r", 81920)
        yout = row("yout", [P, 2, D], "w", 0)

        ident = small("ident", [P, P])
        mask = small("mask", [P, 2, P])
        tri = small("tri", [P, P], BF16)
        ones_bf = small("ones_bf", [P, P], BF16)
        ones = small("ones", [P, 32])
        iota_e = small("iota_e", [P, NE])
        iota_g = small("iota_g", [P, NE])
        iota_i = small("iota_i", [P, 2, NE], I32)
        pair_id = small("pair_id", [P, TT + 1, 2, 2], I32)
        bsel = small("bsel", [P, 2, NS])
        par = small("par", [P, 40])
        stT = small("stT", [P, FW, 32])
        sp4 = small("sp4", [P, 2, FW])
        spt = small("spt", [P, 6, FW])
        tail_in = small("tail_in", [P, FW, 20])
        sinks8 = small("sinks8", [P, 2, NH])
        sink_s = small("sink_s", [P, 2])
        mx = small("mx", [P, 2, NH])
        nb = small("nb", [P, 2, NH])
        es = small("es", [P, 2, NH])
        sums = small("sums", [P, 2, NH])
        rden = small("rden", [P, 2, NH])
        sv = small("sv", [P, 8, 2])
        rT = small("rT", [P, TT + 1, 2])
        brt = small("brt", [NG + NE, 1])
        bn = small("bn", [P, 2, 6])
        mv = small("mv", [P, 2])
        st1 = small("st1", [P, 4])
        lg8 = small("lg8", [P, 8])
        g8 = small("g8", [P, 8])
        gi = small("gi", [P, 8], U32)
        e8 = small("e8", [P, 8])
        ei = small("ei", [P, 8], U32)
        rt = small("rt", [P, 16])
        gexp = small("gexp", [P, NG])
        hot = small("hot", [P, TT + 1, NE], BF16)
        junk = small("junk", [P, NE])
        wt = small("wt", [P, TT + 1, 2])
        rki = small("rki", [P, 2, 2], I32)
        slot = small("slot", [P, TT + 1, 2], U32)
        over = small("over", [P, 1], I32)
        idx_all = small("idx_all", [P, NPAIR + 1, 2], I32)
        idx = small("idx", [P, 2, 2], I32)
        mark = small("mark", [P, 1])

        B = [ctx.enter_context(nc.psum_tensor(f"B{i}", [P, 512], F32)) for i in range(8)]

        m_dram = nc.dram_tensor("m_dram", (NC, 6, D), F32).ap()
        h_dram = nc.dram_tensor("h_dram", (NT, D), F32).ap()
        y_dram = nc.dram_tensor("y_dram", (2 * NT, D), F32).ap()
        table = nc.dram_tensor("table", (ROUNDS * SLOTS, 2), I32).ap()

        def sem(name):
            return ctx.enter_context(nc.semaphore(name))

        c_in, x_in, small_in, kv_in, brow_in, wrg_in = (sem(n) for n in ("c_in", "x_in", "small_in", "kv_in", "brow_in", "wrg_in"))
        ada_in = [sem(f"ada_in{i}") for i in range(4)]
        ada2_in = [sem(f"ada2_in{i}") for i in range(4)]
        win_in = [sem(f"win_in{i}") for i in range(3)]
        wout_in, mod_in, smod_in, lnp_in, wr_in = (sem(n) for n in ("wout_in", "mod_in", "smod_in", "lnp_in", "wr_in"))
        gu_in = [sem(f"gu_in{i}") for i in range(2)]
        dn_in = [sem(f"dn_in{i}") for i in range(2)]
        consts, sink_zero, wrg_zero, kz_zero, X_zero = (sem(n) for n in ("consts", "sink_zero", "wrg_zero", "kz_zero", "X_zero"))
        csil_ready, cT_ps, cT_ready = sem("csil_ready"), sem("cT_ps"), sem("cT_ready")
        xT_ps, xT_v, xT_a, xs_ps = sem("xT_ps"), sem("xT_v"), sem("xT_a"), sem("xs_ps")
        small_ps, small_ready = sem("small_ps"), sem("small_ready")
        ada_used, m_ready, m_stored = sem("ada_used"), sem("m_ready"), sem("m_stored")
        mT_ps, mT_ready = sem("mT_ps"), sem("mT_ready")
        h_v, h_a = sem("h_v"), sem("h_a")
        win_ps, zin_ready = sem("win_ps"), sem("zin_ready")
        xc_ready, gate_ps, gate_tanh, decay_ready = sem("xc_ready"), sem("gate_ps"), sem("gate_tanh"), sem("decay_ready")
        bnorm_ready, broot_ready, lru_done, gelu_ready = sem("bnorm_ready"), sem("broot_ready"), sem("lru_done"), sem("gelu_ready")
        sp_exp, sp_x, ylru = sem("sp_exp"), sem("sp_x"), sem("ylru")
        kv_ready, q_ready = sem("kv_ready"), sem("q_ready")
        vt_ps, vt_ready, tail_ps, tail_ready = sem("vt_ps"), sem("vt_ready"), sem("tail_ps"), sem("tail_ready")
        kcT_ps, kcT_ready, qz_ready, ss_ps = sem("kcT_ps"), sem("kcT_ready"), sem("qz_ready"), sem("ss_ps")
        snb_ready, sexp_done, sP_ready, sPT_ps, sPT_ready, sO_ps, sO_stored = (sem(n) for n in (
            "snb_ready", "sexp_done", "sP_ready", "sPT_ps", "sPT_ready", "sO_ps", "sO_stored"))
        S_ps, S_masked, nb_ready, exp_done, rden_ready, P_ready = (sem(n) for n in (
            "S_ps", "S_masked", "nb_ready", "exp_done", "rden_ready", "P_ready"))
        PT_ps, PT_ready, O_ps, O_stored = (sem(n) for n in ("PT_ps", "PT_ready", "O_ps", "O_stored"))
        sq_ready, ss_sum_ps, ms_ready, rs_ready, rsT_ps, rT_ready = (sem(n) for n in (
            "sq_ready", "ss_sum_ps", "ms_ready", "rs_ready", "rsT_ps", "rT_ready"))
        wout_scaled, L_ps, A_ps, L_ready, A_used = (sem(n) for n in (
            "wout_scaled", "L_ps", "A_ps", "L_ready", "A_used"))
        var_ready, std_ready, norm_ready, xhat_ready, x1_ready, h2_ready = (sem(n) for n in (
            "var_ready", "std_ready", "norm_ready", "xhat_ready", "x1_ready", "h2_ready"))
        h2_stored = [sem("h2_stored0"), sem("h2_stored1")]
        h2T_ps, h2T_v, h2T_a, lgT_ps, lgT_ready, lg_ps = (sem(n) for n in (
            "h2T_ps", "h2T_v", "h2T_a", "lgT_ps", "lgT_ready", "lg_ps"))
        top_ready, top_exp, hot_ready, rank_ps, slot_ready = (sem(n) for n in (
            "top_ready", "top_exp", "hot_ready", "rank_ps", "slot_ready"))
        tab_init, tab_done, count_ps, over_ready = (sem(n) for n in ("tab_init", "tab_done", "count_ps", "over_ready"))
        idx_in, idx_cur = sem("idx_in"), sem("idx_cur")
        X_in = [sem("X_in0"), sem("X_in1")]
        XT_ps, XT_v, XT_a, gu_ps, silu_done, z_ready, zT_ps, zT_ready, y_ps, y_v, y_a = (sem(n) for n in (
            "XT_ps", "XT_v", "XT_a", "gu_ps", "silu_done", "z_ready", "zT_ps", "zT_ready", "y_ps", "y_v", "y_a"))
        y_out = [sem("y_out0"), sem("y_out1")]
        experts_done, yy_in, out_ready, out_done = sem("experts_done"), [sem(f"yy_in{i}") for i in range(TT + 1)], sem("out_ready"), [sem("out_done0"), sem("out_done1")]
        f_used, xhat2_ready = sem("f_used"), sem("xhat2_ready")
        state_done, cache_done = sem("state_done"), sem("cache_done")
        dve_step, act_step, pool_step = sem("dve_step"), sem("act_step"), sem("pool_step")

        ORDER = [0, 1, 2, 3, 8, 9, 10, 11, 12, 13, 4, 5, 6, 7]
        WCH = [0, 1, 4, 5, 6, 2, 3]
        GELU_AT, Q_AT, K_AT = 10, 4, 8
        HALVES = [(0, HALF), (HALF, NT - HALF)]
        TILES = [(t, P) for t in range(TT)] + [(TT, NS)]

        def tok(t, n):
            return slice(t * P, t * P + n)

        block = ctx.enter_context(nc.Block())

        def pair_rows(ap):
            return ap.rearrange("(p k) n -> p k n", k=KD)

        wg_d = A["w_gate"][0].rearrange("e (p k) f -> e p k f", k=KD)
        wu_d = A["w_up"][0].rearrange("e (p k) f -> e p k f", k=KD)
        wd_d = A["w_down"][0].rearrange("e (p k) d -> e p k d", k=2)

        @block.sync
        def _(sp):
            sp.dma_start(crow[0:NS, :], A["c_sample"][:, :]).then_inc(c_in, 16)
            sp.dma_start(crow[NS:NC, :], A["c_prompt"][:, :]).then_inc(c_in, 16)
            sp.dma_start(x_tok[:, 0:TT, :], A["x_prompt"][0].rearrange("(t p) d -> p t d", p=P)).then_inc(x_in, 16)
            sp.dma_start(x_tok[0:NS, TT, :], A["x_sample"].rearrange("b s d -> (b s) d")).then_inc(x_in, 16)
            wa = A["w_ada"][0].rearrange("(p k) n -> p k n", k=KD)
            for j in range(KD):
                if j >= 4:
                    sp.wait_ge(ada_used, j - 3)
                sp.dma_start(ada[:, j % 4, :], wa[:, j, 0:2048]).then_inc(ada_in[j % 4], 16)
            wi = pair_rows(A["w_in"][0])
            for n, c in enumerate(WCH):
                if n >= 3:
                    sp.wait_ge(win_ps, 4 * (n - 2))
                sp.dma_start(win[:, n % 3, :, :], wi[:, :, c * 256:(c + 1) * 256]).then_inc(win_in[n % 3], 16)
            sp.wait_ge(ada_used, 24)
            sp.wait_ge(win_ps, 2 * len(ORDER))

            def load_expert(e, s, par_):
                sp.dma_start(wgu[s][:, 0, :, :], wg_d[e]).then_inc(gu_in[par_], 16)
                sp.dma_start(wgu[s][:, 1, :, :], wu_d[e]).then_inc(gu_in[par_], 16)

            def load_down(e, s, par_):
                sp.dma_start(wdn[s][:, :, :], wd_d[e]).then_inc(dn_in[par_], 16)

            md = m_dram.rearrange("i a n -> i (a n)")
            for r in (1, 2):
                sp.wait_ge(m_ready, 2 * r)
                for g in range(4):
                    c0 = r * 2048 + g * 512
                    sp.dma_start(md[:, c0:c0 + 512], m_sb[32 * g:32 * g + NC, r, :]).then_inc(m_stored, 16)
            sp.wait_ge(ylru, FW)
            sp.wait_ge(m_stored, 16 * 8)
            sp.dma_start(wout[:, :, :], A["w_out"][0].rearrange("(f p) n -> p f n", p=P)).then_inc(wout_in, 16)
            for s in range(2):
                load_expert(s, s, 0)
                load_down(s, s, 0)
            sp.wait_ge(sO_stored, 2)
            sp.wait_ge(state_done, 16 * 8)
            sp.wait_ge(cache_done, 16 * 3)
            for n, i in enumerate((2, 4, 3)):
                sp.dma_start(mod[:, n, :], m_dram[NS:NC, i, :].broadcast_to((P, D))).then_inc(mod_in, 16)
            sp.dma_start(mod[:, 3, :], A["ln1_g"].broadcast_to((P, D))).then_inc(mod_in, 16)
            sp.dma_start(mod[:, 4, :], A["ln1_b"].broadcast_to((P, D))).then_inc(mod_in, 16)
            sp.wait_ge(ss_sum_ps, 1)
            for n, i in enumerate((2, 4, 3, 5)):
                sp.dma_start(smod[:, n, :], m_dram[0:NS, i, :]).then_inc(smod_in, 16)
            sp.wait_ge(O_stored, 2 * TT)
            sp.dma_start(wr[:, :, 0:NG], pair_rows(A["w_group"][0])).then_inc(wr_in, 16)
            for g in range(NG):
                sp.dma_start(wr[:, :, NG + g * EPG:NG + (g + 1) * EPG], pair_rows(A["w_router"][0, g])).then_inc(wr_in, 16)
            load_expert(2, 2, 1)
            load_down(2, 2, 1)
            sp.wait_ge(slot_ready, TT + 1)
            sp.wait_ge(h2_stored[0], 16 * (TT // 2 + 1))
            sp.wait_ge(h2_stored[1], 16 * (TT // 2))
            load_expert(3, 3, 1)
            load_down(3, 3, 1)
            for n, a in ((3, "ln2_g"), (4, "ln2_b")):
                sp.dma_start(mod[:, n, :], A[a].broadcast_to((P, D))).then_inc(lnp_in, 16)
            sp.dma_start(mod[:, 0, :], m_dram[NS:NC, 5, :].broadcast_to((P, D))).then_inc(lnp_in, 16)

            def load_pair(i, n, par_):
                sp.wait_ge(y_ps, n - 1)
                for q in range(2):
                    e = 4 * i + (2 * par_ + q)
                    s = 2 * par_ + q
                    sp.dma_start(wgu[s][:, 0, :, :], wg_d[bass.ds(e, 1)].rearrange("a p k f -> p (a k) f")).then_inc(gu_in[par_], 16)
                    sp.dma_start(wgu[s][:, 1, :, :], wu_d[bass.ds(e, 1)].rearrange("a p k f -> p (a k) f")).then_inc(gu_in[par_], 16)
                    sp.dma_start(wdn[s][:, :, :], wd_d[bass.ds(e, 1)].rearrange("a p k d -> p (a k) d")).then_inc(dn_in[par_], 16)

            with sp.Fori(1, NPAIR // 2) as i:
                load_pair(i, 2 * i, 0)
                load_pair(i, 2 * i + 1, 1)
            sp.wait_ge(over_ready, 1)
            some_over = sp.value_load(over[0:1, 0:1], min_val=0, max_val=1)
            with sp.If(some_over > 0):
                with sp.Fori(1, ROUNDS) as r:
                    with sp.Fori(0, NPAIR // 2) as i:
                        load_pair(i, r * NPAIR + 2 * i, 0)
                        load_pair(i, r * NPAIR + 2 * i + 1, 1)
            sp.wait_ge(experts_done, 1)
            for t, n in TILES:
                for c in range(2):
                    sp.dma_start(yy[0:n, t, c, :], y_dram[c * NT + t * P:c * NT + t * P + n, :]).then_inc(yy_in[t], 16)
            yp = O[0][0].rearrange("(t p) d -> t p d", p=P)
            for t, n in TILES:
                sp.wait_ge(out_ready, t + 1)
                dst = yp[t] if t < TT else O[1].rearrange("b s d -> (b s) d")
                sp.dma_start(dst, yout[0:n, t % 2, :]).then_inc(out_done[t % 2], 16)
            sp.wait_ge(out_done[0], 16 * (TT // 2 + 1))
            sp.wait_ge(out_done[1], 16 * (TT // 2))

        @block.gpsimd
        def _(pool):
            steps = [0]

            def link(ins):
                steps[0] += 1
                ins.then_inc(pool_step, 1)
                pool.wait_ge(pool_step, steps[0])

            def step(ins):
                steps[0] += 1
                ins.then_inc(pool_step, 1)

            step(pool.memset(ident[:, :], 0.0))
            step(pool.memset(cT[:, :, :], 0.0))
            step(pool.memset(b_row[:, :, :], 0.0))
            step(pool.memset(mask[:, :, :], 0.0))
            step(pool.memset(ones[:, :], 1.0))
            step(pool.memset(ones_bf[:, :], 1.0))
            step(pool.memset(tri[:, :], 1.0))
            step(pool.memset(bsel[:, :, :], 1.0))
            step(pool.memset(fill[:, :], NOWHERE))
            step(pool.memset(idx_all[:, :, :], NOWHERE))
            step(pool.memset(lg8[:, :], NEG))
            pool.memset(sink_s[:, :], 0.0).then_inc(sink_zero, 1)
            pool.memset(wrg[:, :, :, :], 0.0).then_inc(wrg_zero, 1)
            step(pool.iota(iota_i[:, 0, :], pattern=[[1, NE]], base=0, channel_multiplier=0))
            step(pool.iota(iota_i[:, 1, :].rearrange("p (g e) -> p g e", e=EPG), pattern=[[1, NG], [0, EPG]],
                           base=0, channel_multiplier=0))
            for c in range(2):
                step(pool.iota(pair_id[:, :, c, 0], pattern=[[P, TT + 1]], base=0, channel_multiplier=1))
                link(pool.iota(pair_id[:, :, c, 1], pattern=[[P, TT + 1]], base=c * NT, channel_multiplier=1))
            pool.affine_select(out=ident[:, :], in_=ident[:, :], compare_op=ALU.not_equal, fill=1.0, base=0,
                               pattern=[[-1, P]], channel_multiplier=1).then_inc(consts, 1)
            step(pool.affine_select(out=mask[:, 0, :], in_=mask[:, 0, :], compare_op=ALU.is_ge, fill=NEG, base=0,
                                    pattern=[[1, P]], channel_multiplier=-1))
            step(pool.affine_select(out=mask[:, 1, :], in_=mask[:, 1, :], compare_op=ALU.is_ge, fill=NEG, base=0,
                                    pattern=[[-1, P]], channel_multiplier=1))
            step(pool.affine_select(out=tri[:, :], in_=tri[:, :], compare_op=ALU.is_gt, fill=0.0, base=0,
                                    pattern=[[1, P]], channel_multiplier=-1))
            link(pool.affine_select(out=bsel[:, :, :], in_=bsel[:, :, :], compare_op=ALU.is_ge, fill=0.0, base=0,
                                    pattern=[[P, 2], [-32, NS]], channel_multiplier=1))
            step(pool.affine_select(out=bsel[:, :, :], in_=bsel[:, :, :], compare_op=ALU.is_ge, fill=0.0, base=31,
                                    pattern=[[-P, 2], [32, NS]], channel_multiplier=-1))
            step(pool.tensor_copy(iota_e[:, :], iota_i[:, 0, :]))
            pool.wait_ge(pool_step, steps[0])
            pool.tensor_copy(iota_g[:, :], iota_i[:, 1, :]).then_inc(consts, 1)
            pool.dma_start(table.rearrange("(p n) w -> p (n w)", p=P), fill[:, :]).then_inc(tab_init, 16)
            for j in range(4):
                pool.dma_start(b_row[32 * j:32 * j + NC, :, :],
                               A["b_ada"].rearrange("a (r j n) -> a r j n", r=3, j=4)[:, :, j, :].broadcast_to((NC, 3, 512))).then_inc(brow_in, 16)
            pool.wait_ge(wrg_zero, 1)
            for g, a in enumerate(("w_rg_a", "w_rg_x")):
                wv = A[a][0].rearrange("(f n) d e -> n d f e", n=2)
                for n in range(2):
                    pool.dma_start(wrg[64 * n:64 * n + 64, g, :, 64 * n:64 * n + 64], wv[n]).then_inc(wrg_in, 16)
            wa = A["w_ada"][0].rearrange("(p k) n -> p k n", k=KD)
            for j in range(KD, 3 * KD):
                pool.wait_ge(ada_used, j - 3)
                pool.dma_start(ada[:, j % 4, :], wa[:, j % KD, (j // KD) * 2048:(j // KD + 1) * 2048]).then_inc(ada2_in[j % 4], 16)
                if j == 2 * KD:
                    pool.wait_ge(tab_init, 16)
                    pool.wait_ge(cT_ps, 1)
                    pool.memset(kTz[:, :, :, :], 0.0).then_inc(kz_zero, 1)
                    pool.memset(qz[:, :, :], 0.0).then_inc(kz_zero, 1)
            pool.wait_ge(tail_ready, 1)
            rows_ = tails[:, :, :].rearrange("r f p -> r (f p)")
            pool.dma_start(O[2][0, 0], rows_[0:3, :]).then_inc(state_done, 16)
            pool.dma_start(O[6][0, :, CW - 2, :], rows_[3:11, :]).then_inc(state_done, 16)
            pool.dma_start(O[3][0], rows_[11:12, :]).then_inc(state_done, 16)
            pool.dma_start(O[7][0], rows_[12:20, :]).then_inc(state_done, 16)
            pool.wait_ge(vt_ready, 3)
            pool.dma_start(O[4][0, 0].rearrange("w k d -> w (k d)"), klast[:, :]).then_inc(state_done, 16)
            pool.dma_start(O[5][0, 0].rearrange("w k d -> w (k d)"), vtok[:, TT - 1, :]).then_inc(state_done, 16)
            for n in range(2):
                pool.dma_start(O[8 + n][0, :, WIN - 1].rearrange("b k d -> b (k d)"), knv[:, n, :]).then_inc(state_done, 16)
            for b in range(TT):
                keys = slice(0, 2 * P) if b else slice(P, 2 * P)
                pool.wait_ge(rden_ready, b + 1)
                for h in range(NH):
                    pool.tensor_scalar(Pm[b % 2][:, h, keys], Pm[b % 2][:, h, keys], rden[:, b % 2, h:h + 1], None,
                                       ALU.mult).then_inc(P_ready, 1)
            pool.wait_ge(wout_in, 16)
            for f in range(2 * FW):
                pool.tensor_scalar(wout[:, f, :], wout[:, f, :], par[:, 32 + f:33 + f], None, ALU.mult).then_inc(wout_scaled, 1)
            pool.wait_ge(mod_in, 16 * 5)
            pool.wait_ge(tab_init, 16)

            def scatter(t, n):
                pool.wait_ge(slot_ready, t + 1)
                for c in range(2):
                    pool.indirect_dma_start(table[:, :], bass.IndirectOffsetOnAxis(ap=slot[0:n, t, c:c + 1], axis=0),
                                            pair_id[0:n, t, c, :], None, bounds_check=ROUNDS * SLOTS - 1,
                                            oob_is_err=False).then_inc(tab_done, 16)

            for t, n in TILES:
                pool.wait_ge(xhat_ready, t + 1)
                link(pool.tensor_tensor(u[0:n, t % 2, :], u[0:n, t % 2, :], mod[0:n, 3, :], ALU.mult))
                pool.tensor_tensor(x_tok[0:n, t, :], u[0:n, t % 2, :], mod[0:n, 4, :], ALU.add).then_inc(x1_ready, 1)
                if t >= 1:
                    scatter(*TILES[t - 1])
            scatter(*TILES[TT])
            pool.wait_ge(L_ps, TT + 1)
            pool.wait_ge(A_ps, TT)
            pool.memset(X[:, :, :], 0.0).then_inc(X_zero, 1)
            pool.wait_ge(X_zero, 1)
            pool.wait_ge(tab_done, 16 * 2 * (TT + 1))
            pool.wait_ge(h2_stored[0], 16 * (TT // 2 + 1))
            pool.wait_ge(h2_stored[1], 16 * (TT // 2))
            slots = table.rearrange("(r j s) w -> r s j w", r=ROUNDS, s=P)

            pool.dma_start(idx_all[:, 0:NPAIR, :], slots[0]).then_inc(idx_in, 16)
            pool.wait_ge(idx_in, 16)

            def counted(value):
                value = value if isinstance(value, int) else pool.to_reg(value)
                pool.wait_ge(tab_init, 16)
                return value

            def start_gather(par_, col, g):
                pool.tensor_copy(idx[:, par_, :], idx_all[:, bass.ds(col, 1), :].rearrange("p a w -> p (a w)")).then_inc(idx_cur, 1)
                pool.wait_ge(idx_cur, counted(g + 1))
                pool.indirect_dma_start(X[:, par_, :], None, h_dram[:, :],
                                        bass.IndirectOffsetOnAxis(ap=idx[:, par_, 0:1], axis=0),
                                        bounds_check=NT - 1, oob_is_err=False).then_inc(X_in[par_], 16)

            def scatter_y(par_, n):
                outputs = counted(n + 1)
                pool.wait_ge(y_v, outputs)
                pool.wait_ge(y_a, outputs)
                pool.indirect_dma_start(y_dram[:, :], bass.IndirectOffsetOnAxis(ap=idx[:, par_, 1:2], axis=0),
                                        yo[:, par_, :], None, bounds_check=2 * NT - 1,
                                        oob_is_err=False).then_inc(y_out[par_], 16)

            def pairs(r, first_loop):
                n0 = r * NPAIR
                g0 = r * (NPAIR + 1)
                start_gather(0, 0, g0)

                def turn(i, peeled):
                    n = n0 + 2 * i
                    g = g0 + 2 * i
                    if not peeled:
                        pool.wait_ge(XT_ps, 2 * n)
                        pool.wait_ge(y_out[1], 8 * n)
                    start_gather(1, 2 * i + 1, g + 1)
                    scatter_y(0, n)
                    pool.wait_ge(XT_ps, 2 * (n + 1))
                    pool.wait_ge(y_out[0], 8 * n + 16)
                    start_gather(0, 2 * i + 2, g + 2)
                    scatter_y(1, n + 1)

                if first_loop:
                    turn(0, True)
                    with pool.Fori(1, NPAIR // 2) as i:
                        turn(i, False)
                else:
                    with pool.Fori(0, NPAIR // 2) as i:
                        turn(i, False)
                pool.wait_ge(y_out[0], 8 * n0 + 8 * NPAIR)
                pool.wait_ge(y_out[1], 8 * n0 + 8 * NPAIR)
                pool.wait_ge(X_in[0], 16 * (NPAIR // 2 + 1) * (r + 1))

            pairs(0, True)
            pool.wait_ge(over_ready, 1)
            some_over = pool.value_load(over[0:1, 0:1], min_val=0, max_val=1)
            with pool.If(some_over > 0):
                with pool.Fori(1, ROUNDS) as r:
                    pool.dma_start(idx_all[:, 0:NPAIR, :], slots[bass.ds(r, 1)].rearrange("a s j w -> s (a j) w")).then_inc(idx_in, 16)
                    pool.wait_ge(idx_in, counted(16 * r + 16))
                    pairs(r, False)
            pool.memset(mark[:, :], 0.0).then_inc(experts_done, 1)
            for t, n in TILES:
                pool.wait_ge(xhat2_ready, t + 1)
                if t >= 2:
                    pool.wait_ge(out_done[t % 2], 16 * (t // 2))
                pool.tensor_tensor(yout[0:n, t % 2, :], ff[0:n, t % 2, :], mod[0:n, 4, :], ALU.add).then_inc(out_ready, 1)

        @block.scalar
        def _(act):
            steps = [0]

            def link(ins):
                steps[0] += 1
                ins.then_inc(act_step, 1)
                act.wait_ge(act_step, steps[0])

            act.dma_start(prm[0:16, :], A["conv_w"][0].rearrange("k (f p) -> (k f) p", p=P)).then_inc(small_in, 16)
            for n, a in enumerate(("conv_b", "b_rg_a", "b_rg_x", "lru_lambda", "g_lru", "g_attn")):
                v = A[a][0]
                v = v.rearrange("(f n) e -> f (n e)", n=2) if a in ("b_rg_a", "b_rg_x") else v.rearrange("(f p) -> f p", p=P)
                act.dma_start(prm[16 + 4 * n:20 + 4 * n, :], v).then_inc(small_in, 16)
            act.dma_start(stt_in[0:24, :], A["state_conv"][0].rearrange("b k n -> (b k) n")).then_inc(small_in, 16)
            act.dma_start(stt_in[24:32, :], A["state_h"][0]).then_inc(small_in, 16)
            act.dma_start(sinks8[:, 0, :], A["sinks"].broadcast_to((P, NH))).then_inc(small_in, 16)
            act.wait_ge(sink_zero, 1)
            for j in range(4):
                act.dma_start(sink_s[32 * j:32 * j + NH, 0:1], A["sinks"].rearrange("a h -> h a")).then_inc(small_in, 16)
            act.dma_start(kc[:, :, :], A["cache_k"][0].rearrange("b w k d -> w b (k d)")).then_inc(kv_in, 16)
            act.dma_start(vc[:, :, :], A["cache_v"][0].rearrange("b w k d -> w b (k d)")).then_inc(kv_in, 16)
            act.dma_start(brt[0:NG, :], A["b_group"].rearrange("a g -> g a")).then_inc(kv_in, 16)
            act.dma_start(brt[NG:NG + NE, :], A["b_router"][0].rearrange("g (e a) -> (g e) a", a=1)).then_inc(kv_in, 16)
            act.wait_ge(c_in, 32)
            act.activation(csil[:, :], crow[:, :], ACT.Silu).then_inc(csil_ready, 1)
            for n, a in ((8, "cache_k"), (9, "cache_v")):
                act.dma_start(O[n][0, :, 0:WIN - 1].rearrange("b w k d -> b w (k d)"),
                              A[a][0, :, 1:WIN].rearrange("b w k d -> b w (k d)")).then_inc(cache_done, 16)
            act.dma_start(O[6][0, :, 0:CW - 2, :], A["state_conv"][0, :, 1:CW - 1, :]).then_inc(cache_done, 16)
            for k in range(1, KD, 2):
                act.wait_ge(xT_ps, k + 1)
                act.activation(hT[:, k, 0:T], B[k % 4][:, :], ACT.Copy).then_inc(xT_a, 1)
            act.wait_ge(sp_x, 1)
            act.activation(spt[:, 1, :], spt[:, 0, :], ACT.Exp, scale=-1.0).then_inc(sp_exp, 1)
            act.wait_ge(mT_ready, 4)
            act.wait_ge(xT_a, 4)
            for k in range(1, KD, 2):
                act.activation(hT[:, k, 0:T], hT[:, k, 0:T], ACT.Identity, scale=mT[:, 1, k, NS:NC],
                               bias=mT[:, 0, k, NS:NC]).then_inc(h_a, 1)

            def lru_act(f):
                for g, dst in enumerate((tr, ti)):
                    for h in range(2):
                        act.wait_ge(gate_ps, 4 * f + 2 * g + h + 1)
                        if f and g == 0 and h == 0:
                            act.wait_ge(lru_done, f)
                        act.activation(dst[:, h * XH:(h + 1) * XH], B[6 + h][:, 0:XH], ACT.Tanh, scale=0.5,
                                       bias=spt[:, 4 + g, f:f + 1]).then_inc(gate_tanh, 1)
                act.wait_ge(gate_tanh, 4 * (f + 1))
                act.activation(aa[:, :], tr[:, :], ACT.Exp, scale=sp4[:, 1, f:f + 1], bias=sp4[:, 1, f:f + 1]).then_inc(decay_ready, 1)
                act.activation(th[:, :], tr[:, :], ACT.Tanh, scale=sp4[:, 0, f:f + 1], bias=sp4[:, 0, f:f + 1]).then_inc(decay_ready, 1)
                act.wait_ge(bnorm_ready, f + 1)
                act.activation(a2[:, :], a2[:, :], ACT.Sqrt, scale=0.25).then_inc(broot_ready, 1)

            for q, f in enumerate(ORDER):
                b0 = (q % 2) * 2
                if q < FW:
                    act.wait_ge(win_ps, 2 * q + 1)
                    if q >= 2:
                        act.wait_ge(xc_ready, q - 1)
                    act.activation(xb[:, q % 2, CW - 1:CW - 1 + HALF], B[b0][:, 0:HALF], ACT.Copy).then_inc(zin_ready, 1)
                    act.wait_ge(win_ps, 2 * q + 2)
                    act.activation(xb[:, q % 2, CW - 1 + HALF:CW - 1 + T], B[b0 + 1][:, 0:T - HALF], ACT.Copy).then_inc(zin_ready, 1)
                    act.activation(xb[:, q % 2, S0 + CW - 1:CONV:CW], B[b0 + 1][:, T - HALF:NT - HALF], ACT.Copy).then_inc(zin_ready, 1)
                elif q < K_AT:
                    for h, (c0, cn) in enumerate(HALVES):
                        act.wait_ge(win_ps, 2 * q + h + 1)
                        act.activation(qT[:, f - 8, c0:c0 + cn], B[b0 + h][:, 0:cn], ACT.Copy).then_inc(q_ready, 1)
                elif q < GELU_AT:
                    if q == K_AT:
                        act.wait_ge(kz_zero, 2)
                        act.wait_ge(tab_init, 16)
                    for h, (c0, cn) in enumerate(HALVES):
                        act.wait_ge(win_ps, 2 * q + h + 1)
                        if q == K_AT:
                            cp = min(cn, T - c0)
                            for kv in range(NKV):
                                for half in range(2):
                                    act.activation(kTz[64 * half:64 * half + 64, kv, half, c0:c0 + cp],
                                                   B[b0 + h][64 * kv:64 * kv + 64, 0:cp], ACT.Copy)
                        act.activation(kvT[:, q - K_AT, c0:c0 + cn], B[b0 + h][:, 0:cn], ACT.Copy).then_inc(kv_ready, 1)
                else:
                    if q == GELU_AT:
                        act.wait_ge(lru_done, FW)
                    for h, (c0, cn) in enumerate(HALVES):
                        act.wait_ge(win_ps, 2 * q + h + 1)
                        act.activation(gel[:, q - GELU_AT, c0:c0 + cn], B[b0 + h][:, 0:cn], ACT.Gelu_apprx_tanh).then_inc(gelu_ready, 1)
                if 2 <= q < 2 + FW:
                    lru_act(q - 2)

            for n in range(2):
                act.wait_ge(kcT_ps, n + 1)
                act.activation(kbT[:, 4 * n:4 * n + 4, 0:WIN], B[6 + n][:, :].rearrange("p (b w) -> p b w", w=WIN),
                               ACT.Copy).then_inc(kcT_ready, 1)
            act.wait_ge(snb_ready, 1)
            act.activation(sv[:, 3, 0:1], sink_s[:, 0:1], ACT.Exp, bias=sv[:, 2, 0:1]).then_inc(sexp_done, 1)
            act.activation(sv[:, 3, 1:2], sink_s[:, 0:1], ACT.Exp, bias=sv[:, 2, 1:2]).then_inc(sexp_done, 1)
            for n in range(2):
                act.activation(ps[:, n, :], ps[:, n, :], ACT.Exp, scale=SCALE, bias=sv[:, 2, n:n + 1],
                               accum_out=sv[:, 4, n:n + 1]).then_inc(sexp_done, 1)

            def exps(b):
                keys = slice(0, 2 * P) if b else slice(P, 2 * P)
                act.wait_ge(nb_ready, 2 * (b + 1))
                act.activation(es[:, b % 2, :], es[:, b % 2, :], ACT.Exp).then_inc(exp_done, 1)
                for h in range(NH):
                    act.activation(Pm[b % 2][:, h, keys], Pm[b % 2][:, h, keys], ACT.Exp, scale=SCALE,
                                   bias=nb[:, b % 2, h:h + 1], accum_out=sums[:, b % 2, h:h + 1]).then_inc(exp_done, 1)

            def pt_count(b):
                return 0 if b == 0 else 2 + 4 * (b - 1)

            def evacuate_PT(b):
                first = pt_count(b)
                kbs = (0, 1) if b else (1,)
                for n, (kb, kv) in enumerate((kb, kv) for kb in kbs for kv in range(NKV)):
                    act.wait_ge(PT_ps, first + n + 1)
                    if b and n == 0:
                        act.wait_ge(O_ps, b)
                    act.activation(PT[:, kb, kv, :], B[4 + n % 2][:, :], ACT.Copy).then_inc(PT_ready, 1)

            for b in range(TT + 1):
                if b < TT:
                    exps(b)
                if b >= 1:
                    evacuate_PT(b - 1)
            act.wait_ge(ylru, FW)
            for f in range(FW):
                act.activation(sq[:, f, :], yT[:, f, :], ACT.Square).then_inc(sq_ready, 1)
            act.wait_ge(sO_stored, 2)
            act.wait_ge(O_stored, 2 * TT)
            for f in range(FW, 2 * FW):
                act.activation(sq[:, f, :], yT[:, f, :], ACT.Square).then_inc(sq_ready, 1)
            act.wait_ge(ms_ready, 1)
            act.activation(rs[:, :], rs[:, :], ACT.Sqrt).then_inc(rs_ready, 1)

            def mixer_out(t, n):
                act.wait_ge(L_ps, t + 1)
                if t >= 2:
                    act.wait_ge(x1_ready, t - 1)
                for c in range(2):
                    src = B[c][:, :] if t < TT else B[0][32 * c:32 * c + n, :]
                    act.activation(u[0:n, t % 2, c * 512:(c + 1) * 512], src, ACT.Copy, scale=rT[0:n, t, 0:1]).then_inc(L_ready, 1)

            def xhat(t, n):
                act.wait_ge(var_ready, t + 1)
                act.activation(st1[0:n, 1:2], st1[0:n, 0:1], ACT.Sqrt).then_inc(std_ready, 1)
                act.wait_ge(norm_ready, t + 1)
                act.activation(u[0:n, t % 2, :], u[0:n, t % 2, :], ACT.Identity, scale=st1[0:n, 2:3],
                               bias=st1[0:n, 3:4]).then_inc(xhat_ready, 1)

            def after(t, n):
                act.wait_ge(h2_ready, t + 1)
                act.dma_start(h_dram[t * P:t * P + n, :], h2[0:n, t % 2, :]).then_inc(h2_stored[t % 2], 16)
                act.wait_ge(h2T_ps, 2 * t + 2)
                act.activation(h2T[:, 4:8, 0:n], B[5][:, :].rearrange("p (k m) -> p k m", m=P)[:, :, 0:n], ACT.Copy).then_inc(h2T_a, 1)
                act.wait_ge(top_ready, t + 1)
                act.activation(gexp[0:n, :], lg8[0:n, 0:NG], ACT.Exp, bias=rt[0:n, 0:1], accum_out=rt[0:n, 2:3]).then_inc(top_exp, 1)
                act.activation(rt[0:n, 3:4], rt[0:n, 1:2], ACT.Exp).then_inc(top_exp, 1)

            act.wait_ge(rT_ready, 3)
            for i in range(TT + 2):
                if i <= TT:
                    mixer_out(*TILES[i])
                    xhat(*TILES[i])
                if i >= 1:
                    after(*TILES[i - 1])

            def pair(n, par_):
                act.wait_ge(XT_ps, 2 * n + 2)
                act.activation(XT[:, par_, 4:8, :], B[1][:, :].rearrange("p (k m) -> p k m", m=P), ACT.Copy).then_inc(XT_a, 1)
                act.wait_ge(gu_ps, n + 1)
                act.activation(silu_g[:, :], B[2 + par_][:, 0:DE], ACT.Silu).then_inc(silu_done, 1)
                act.wait_ge(zT_ps, n + 1)
                act.activation(zT[:, :, :], B[4][:, 0:2 * P].rearrange("p (k m) -> p k m", m=P), ACT.Copy).then_inc(zT_ready, 1)
                act.wait_ge(y_ps, n + 1)

            def pair_tail(n, par_):
                act.activation(yo[:, par_, 512:D], B[6][:, :], ACT.Copy).then_inc(y_a, 1)

            def round_(r, first):
                n0 = r * NPAIR

                def turn(i, peeled):
                    n = n0 + 2 * i
                    pair(n, 0)
                    if not peeled:
                        act.wait_ge(y_out[0], 8 * n)
                    pair_tail(n, 0)
                    pair(n + 1, 1)
                    if not peeled:
                        act.wait_ge(y_out[1], 8 * n)
                    pair_tail(n + 1, 1)

                if first:
                    turn(0, True)
                    with act.Fori(1, NPAIR // 2) as i:
                        turn(i, False)
                else:
                    with act.Fori(0, NPAIR // 2) as i:
                        turn(i, False)

            round_(0, True)
            act.wait_ge(over_ready, 1)
            some_over = act.value_load(over[0:1, 0:1], min_val=0, max_val=1)
            with act.If(some_over > 0):
                with act.Fori(1, ROUNDS) as r:
                    round_(r, False)

            def std2(t, n):
                act.wait_ge(var_ready, TT + 2 + t)
                act.activation(st1[0:n, 1:2], st1[0:n, 0:1], ACT.Sqrt).then_inc(std_ready, 1)

            for t, n in TILES:
                act.wait_ge(yy_in[t], 32)
                act.activation(yy[0:n, t, 0, :], yy[0:n, t, 0, :], ACT.Copy, scale=wt[0:n, t, 0:1]).then_inc(f_used, 1)
                if t >= 1:
                    std2(*TILES[t - 1])
            std2(*TILES[TT])

        @block.vector
        def _(dve):
            steps = [0]

            def link(ins):
                steps[0] += 1
                ins.then_inc(dve_step, 1)
                dve.wait_ge(dve_step, steps[0])

            def step(ins):
                steps[0] += 1
                ins.then_inc(dve_step, 1)

            def settle():
                dve.wait_ge(dve_step, steps[0])

            dve.wait_ge(cT_ps, 1)
            dve.wait_ge(consts, 2)
            dve.tensor_copy(cT[:, :, 0:NC], B[7][:, 0:KD * 16].rearrange("p (k c) -> p k c", c=16)[:, :, 0:NC]).then_inc(cT_ready, 1)
            for k in range(0, KD, 2):
                dve.wait_ge(xT_ps, k + 1)
                dve.tensor_copy(hT[:, k, 0:T], B[k % 4][:, :]).then_inc(xT_v, 1)
            dve.wait_ge(xs_ps, 1)
            dve.tensor_copy(hT[:, :, T:NT], B[6][:, 0:KD * NS].rearrange("p (k b) -> p k b", b=NS)).then_inc(xT_v, 1)
            dve.wait_ge(small_ps, 1)
            dve.tensor_copy(par[:, :], B[5][:, 0:40]).then_inc(small_ready, 1)
            dve.tensor_copy(stT[:, :, :], B[5][:, 64:64 + FW * 32].rearrange("p (f c) -> p f c", c=32)).then_inc(small_ready, 1)
            dve.wait_ge(small_ready, 2)
            lam = par[:, 28:32]
            link(dve.tensor_scalar(spt[:, 1, :], lam, -1.0, None, ALU.mult))
            dve.tensor_tensor(spt[:, 0, :], spt[:, 1, :], lam, ALU.max).then_inc(sp_x, 1)
            link(dve.tensor_scalar(spt[:, 2, :], lam, -1.0, 0.0, ALU.mult, ALU.max))
            dve.wait_ge(sp_exp, 1)
            link(dve.tensor_scalar(spt[:, 3, :], spt[:, 1, :], 2.0, None, ALU.add))
            link(dve.reciprocal(spt[:, 3, :], spt[:, 3, :]))
            link(dve.tensor_tensor(spt[:, 3, :], spt[:, 3, :], spt[:, 1, :], ALU.mult))
            link(dve.tensor_tensor(spt[:, 1, :], spt[:, 3, :], spt[:, 3, :], ALU.mult))
            link(dve.tensor_scalar(spt[:, 4, :], spt[:, 1, :], 1.0 / 17, 1.0 / 15, ALU.mult, ALU.add))
            for c in (13, 11, 9, 7, 5, 3, 1):
                link(dve.tensor_tensor(spt[:, 4, :], spt[:, 4, :], spt[:, 1, :], ALU.mult))
                link(dve.tensor_scalar(spt[:, 4, :], spt[:, 4, :], 1.0 / c, None, ALU.add))
            link(dve.tensor_tensor(spt[:, 4, :], spt[:, 4, :], spt[:, 3, :], ALU.mult))
            link(dve.scalar_tensor_tensor(out=spt[:, 4, :], in0=spt[:, 4, :], scalar=2.0, in1=spt[:, 2, :], op0=ALU.mult, op1=ALU.add))
            link(dve.tensor_scalar(sp4[:, 0, :], spt[:, 4, :], 4.0, None, ALU.mult))
            link(dve.tensor_scalar(sp4[:, 1, :], spt[:, 4, :], -4.0, None, ALU.mult))
            step(dve.tensor_scalar(spt[:, 4, :], par[:, 20:24], 0.5, None, ALU.mult))
            step(dve.tensor_scalar(spt[:, 5, :], par[:, 24:28], 0.5, None, ALU.mult))
            dve.wait_ge(small_in, 16 * 14)
            step(dve.tensor_scalar(sinks8[:, 1, :], sinks8[:, 0, :], 1.0 / SCALE, None, ALU.mult))
            step(dve.tensor_scalar(sink_s[:, 1:2], sink_s[:, 0:1], 1.0 / SCALE, None, ALU.mult))

            def modulation(r):
                dve.wait_ge(ada_used, KD * (r + 1))
                if r == 0:
                    dve.wait_ge(brow_in, 16 * 4)
                link(dve.tensor_tensor(m_sb[:, r, :], B[4][:, :], b_row[:, r, :], ALU.add))
                plus = {0: (64, 128), 1: (0, 64), 2: (0, 128)}[r]
                for p0 in range(plus[0], plus[1], 64):
                    dve.tensor_scalar(m_sb[p0:p0 + 64, r, :], m_sb[p0:p0 + 64, r, :], 1.0, None, ALU.add).then_inc(m_ready, 1)

            modulation(0)
            for g in range(4):
                if g == 0:
                    dve.wait_ge(mT_ps, 1)
                for kk in range(2):
                    i = dve.tensor_copy(mT[64 * (g % 2):64 * (g % 2) + 64, g // 2, 4 * kk:4 * kk + 4, :],
                                        B[5 + 2 * kk][0:64, :].rearrange("p (k c) -> p k c", c=P)[:, :, 32 * g:32 * g + NC])
                    if kk:
                        i.then_inc(mT_ready, 1)
                    else:
                        step(i)
            dve.wait_ge(mT_ready, 4)
            dve.wait_ge(xT_v, 5)
            for k in range(0, KD, 2):
                dve.tensor_scalar(hT[:, k, 0:T], hT[:, k, 0:T], mT[:, 1, k, NS:NC], mT[:, 0, k, NS:NC], ALU.mult, ALU.add).then_inc(h_v, 1)
            link(dve.tensor_tensor(hT[:, :, T:NT], hT[:, :, T:NT], mT[:, 1, :, 0:NS], ALU.mult))
            dve.tensor_tensor(hT[:, :, T:NT], hT[:, :, T:NT], mT[:, 0, :, 0:NS], ALU.add).then_inc(h_v, 1)
            step(dve.memset(xb[:, :, 0:CW - 1], 0.0))

            def conv(f):
                v = xb[:, f % 2, :]
                o = xc[:, f % 3, :]
                step(dve.tensor_copy(xb[:, f % 2, S0:CONV].rearrange("p (b k) -> p b k", k=CW)[:, :, 0:CW - 1],
                                     stT[:, f, 0:24].rearrange("p (b k) -> p b k", k=CW - 1)))
                dve.wait_ge(zin_ready, 3 * (f + 1))
                settle()
                if f >= 3:
                    dve.wait_ge(gate_ps, 4 * (f - 2))
                step(dve.tensor_copy(tail_in[:, f, 0:3], v[:, T:T + 3]))
                step(dve.tensor_copy(tail_in[:, f, 3:11], v[:, S0 + CW - 1:CONV:CW]))
                link(dve.tensor_scalar(o, v[:, 0:XC], par[:, f:f + 1], par[:, 16 + f:17 + f], ALU.mult, ALU.add))
                for k in range(1, CW):
                    i = dve.scalar_tensor_tensor(out=o, in0=v[:, k:k + XC], scalar=par[:, 4 * k + f:4 * k + f + 1], in1=o,
                                                 op0=ALU.mult, op1=ALU.add)
                    if k < CW - 1:
                        link(i)
                    else:
                        i.then_inc(xc_ready, 1)

            def lru(f):
                o = xc[:, f % 3, :]
                dve.wait_ge(decay_ready, 2 * f + 1)
                link(dve.tensor_tensor(a2[:, :], aa[:, :], aa[:, :], ALU.mult))
                dve.wait_ge(decay_ready, 2 * f + 2)
                link(dve.scalar_tensor_tensor(out=a2[:, :], in0=a2[:, :], scalar=1.0, in1=th[:, :], op0=ALU.add, op1=ALU.mult))
                dve.tensor_scalar(a2[:, :], a2[:, :], 1e-30, None, ALU.max).then_inc(bnorm_ready, 1)
                link(dve.scalar_tensor_tensor(out=ti[:, :], in0=ti[:, :], scalar=1.0, in1=o, op0=ALU.add, op1=ALU.mult))
                dve.wait_ge(broot_ready, f + 1)
                link(dve.tensor_tensor(ti[:, :], ti[:, :], a2[:, :], ALU.mult))
                link(dve.tensor_tensor_scan(yT[:, f, 0:T], aa[:, 0:T], ti[:, 0:T], 0.0, ALU.mult, ALU.add))
                link(dve.tensor_tensor(yT[:, f, T:NT], aa[:, S0:XC:CW], stT[:, f, 24:32], ALU.mult))
                link(dve.tensor_tensor(yT[:, f, T:NT], yT[:, f, T:NT], ti[:, S0:XC:CW], ALU.add))
                dve.tensor_copy(tail_in[:, f, 11:20], yT[:, f, T - 1:NT]).then_inc(lru_done, 1)

            for f in range(FW):
                conv(f)
                if f >= 2:
                    lru(f - 2)
            for f in (2, 3):
                lru(f)
            modulation(1)
            modulation(2)
            for f in range(FW):
                dve.wait_ge(gelu_ready, 2 * (f + 1))
                dve.tensor_tensor(yT[:, f, :], yT[:, f, :], gel[:, f, :], ALU.mult).then_inc(ylru, 1)
            dve.wait_ge(vt_ps, 1)
            dve.tensor_copy(vtok[:, :, :], B[4][:, :].rearrange("p (t d) -> p t d", d=P)).then_inc(vt_ready, 1)
            dve.tensor_copy(klast[:, :], B[5][:, 0:P]).then_inc(vt_ready, 1)
            dve.tensor_copy(knv[:, :, :], B[5][0:NS, P:3 * P].rearrange("p (c d) -> p c d", d=P)).then_inc(vt_ready, 1)
            dve.wait_ge(tail_ps, 1)
            dve.tensor_copy(tails[:, :, :], B[6][0:20, :].rearrange("p (f d) -> p f d", d=P)).then_inc(tail_ready, 1)
            dve.wait_ge(kz_zero, 2)
            dve.wait_ge(q_ready, 2 * FW)
            for kv in range(NKV):
                for half in range(2):
                    dve.tensor_copy(qz[64 * kv:64 * kv + 64, :, kv * G + half:(kv + 1) * G:2].rearrange("p b i -> p i b"),
                                    qT[64 * half:64 * half + 64, 2 * kv:2 * kv + 2, T:NT]).then_inc(qz_ready, 1)
            dve.wait_ge(kv_ready, 2)
            dve.tensor_copy(kbT[:, :, WIN:WIN + 1], kvT[:, 0, T:NT].rearrange("p (b a) -> p b a", a=1)).then_inc(qz_ready, 1)
            dve.wait_ge(ss_ps, 1)
            step(dve.tensor_copy(ps[:, :, :], B[7][:, 0:2 * (WIN + 1)].rearrange("p (n w) -> p n w", w=WIN + 1)))
            link(dve.tensor_reduce(sv[:, 0, :], B[7][:, 0:2 * (WIN + 1)].rearrange("p (n w) -> p n w", w=WIN + 1), AX.X, ALU.max))
            link(dve.tensor_scalar(sv[:, 1, :], sv[:, 0, :], sink_s[:, 1:2], None, ALU.max))
            dve.tensor_scalar(sv[:, 2, :], sv[:, 1, :], -SCALE, None, ALU.mult).then_inc(snb_ready, 1)
            dve.wait_ge(sexp_done, 4)
            link(dve.tensor_tensor(sv[:, 5, :], sv[:, 4, :], sv[:, 3, :], ALU.add))
            link(dve.reciprocal(sv[:, 6, :], sv[:, 5, :]))
            for n in range(2):
                link(dve.tensor_scalar(ps[:, n, :], ps[:, n, :], sv[:, 6, n:n + 1], None, ALU.mult))
                dve.tensor_scalar(pnm[:, n, :], bsel[:, n, :], ps[:, n, WIN:WIN + 1], None, ALU.mult).then_inc(sP_ready, 1)
            dve.wait_ge(sPT_ps, 1)
            dve.tensor_copy(psT[:, :, :], B[6][:, 0:2 * P].rearrange("p (n m) -> p n m", m=P)).then_inc(sPT_ready, 1)
            dve.tensor_copy(pnd[:, :, :], B[5][0:NS, 0:2 * P].rearrange("p (n m) -> p n m", m=P)).then_inc(sPT_ready, 1)

            def mask_rows(b):
                keys = slice(0, 2 * P) if b else slice(P, 2 * P)
                kn = 2 * P if b else P
                if b >= 2:
                    dve.wait_ge(PT_ps, 2 + 4 * (b - 2))
                for h in range(NH):
                    if h % 2 == 0:
                        dve.wait_ge(S_ps, 4 * b + h // 2 + 1)
                    dve.tensor_tensor_reduce(out=Pm[b % 2][:, h, keys], in0=B[h // 2][:, (h % 2) * kn:(h % 2 + 1) * kn],
                                             in1=mask[:, :, :].rearrange("p a k -> p (a k)")[:, keys], scale=1.0, scalar=NEG,
                                             op0=ALU.add, op1=ALU.max, accum_out=mx[:, b % 2, h:h + 1]).then_inc(S_masked, 1)
                dve.wait_ge(S_masked, NH * (b + 1))
                link(dve.tensor_tensor(mx[:, b % 2, :], mx[:, b % 2, :], sinks8[:, 1, :], ALU.max))
                dve.tensor_scalar(nb[:, b % 2, :], mx[:, b % 2, :], -SCALE, None, ALU.mult).then_inc(nb_ready, 1)
                dve.wait_ge(nb_ready, 2 * b + 1)
                dve.tensor_tensor(es[:, b % 2, :], sinks8[:, 0, :], nb[:, b % 2, :], ALU.add).then_inc(nb_ready, 1)

            def denominators(b):
                dve.wait_ge(exp_done, (NH + 1) * (b + 1))
                link(dve.tensor_tensor(sums[:, b % 2, :], sums[:, b % 2, :], es[:, b % 2, :], ALU.add))
                dve.reciprocal(rden[:, b % 2, :], sums[:, b % 2, :]).then_inc(rden_ready, 1)

            def store_O(b):
                dve.wait_ge(O_ps, b + 1)
                for kv in range(NKV):
                    for half in range(2):
                        i = dve.tensor_copy(yT[64 * half:64 * half + 64, FW + 2 * kv:FW + 2 * kv + 2, b * P:(b + 1) * P],
                                            B[6][64 * kv:64 * kv + 64, :].rearrange("p (g q) -> p g q", q=P)[:, half::2, :])
                        if half:
                            i.then_inc(O_stored, 1)
                        else:
                            step(i)

            for b in range(TT + 2):
                if b < TT:
                    mask_rows(b)
                if 1 <= b <= TT:
                    denominators(b - 1)
                if b == 1:
                    dve.wait_ge(sO_ps, 1)
                    for kv in range(NKV):
                        for half in range(2):
                            i = dve.tensor_copy(yT[64 * half:64 * half + 64, FW + 2 * kv:FW + 2 * kv + 2, T:NT].rearrange("p i b -> p b i"),
                                                B[7][64 * kv:64 * kv + 64, 0:NS * 32].rearrange("p (b h) -> p b h", h=32)[:, :, kv * G + half:(kv + 1) * G:2])
                            if half:
                                i.then_inc(sO_stored, 1)
                            else:
                                step(i)
                if b >= 2:
                    store_O(b - 2)
            dve.wait_ge(ss_sum_ps, 1)
            dve.tensor_scalar(rs[:, :], B[4][:, 0:264], 1.0 / W, RMS_EPS, ALU.mult, ALU.add).then_inc(ms_ready, 1)
            dve.wait_ge(rs_ready, 1)
            dve.reciprocal(rs[:, :], rs[:, :]).then_inc(rs_ready, 1)
            dve.wait_ge(rsT_ps, 1)
            for c in range(2):
                dve.tensor_copy(rT[:, 0:TT, :].rearrange("p (h c) g -> p h c g", c=2)[:, :, c, :],
                                B[5][:, c * P:(c + 1) * P].rearrange("p (g h x) -> p h g x", g=2, h=2)[:, :, :, 0]).then_inc(rT_ready, 1)
            dve.tensor_copy(rT[0:NS, TT, :], B[5][0:NS, 2 * P:3 * P].rearrange("p (g h x) -> p g h x", g=2, h=2)[:, :, 1, 0]).then_inc(rT_ready, 1)
            dve.wait_ge(rT_ready, 3)
            dve.wait_ge(mod_in, 16 * 5)

            def layer_norm_stats(src, n, i):
                for c in range(2):
                    step(dve.bn_stats(bn[0:n, c, :], src[:, c * 512:(c + 1) * 512]))
                settle()
                link(dve.bn_aggr(mv[0:n, :], bn[0:n, :, :].rearrange("p a b -> p (a b)")))
                dve.tensor_scalar(st1[0:n, 0:1], mv[0:n, 1:2], LN_EPS, None, ALU.add).then_inc(var_ready, 1)
                dve.wait_ge(std_ready, i + 1)
                link(dve.reciprocal(st1[0:n, 2:3], st1[0:n, 1:2]))
                dve.scalar_tensor_tensor(out=st1[0:n, 3:4], in0=mv[0:n, 0:1], scalar=-1.0, in1=st1[0:n, 2:3],
                                         op0=ALU.mult, op1=ALU.mult).then_inc(norm_ready, 1)

            def residual(t, n):
                gate = mod[:, 0, :] if t < TT else smod[0:NS, 0, :]
                dve.wait_ge(A_ps, min(t + 1, TT))
                dve.wait_ge(L_ready, 2 * (t + 1))
                for c in range(2):
                    src = B[2 + c][:, :] if t < TT else B[0][64 + 32 * c:64 + 32 * c + n, :]
                    dve.scalar_tensor_tensor(out=u[0:n, t % 2, c * 512:(c + 1) * 512], in0=src, scalar=rT[0:n, t, 1:2],
                                             in1=u[0:n, t % 2, c * 512:(c + 1) * 512], op0=ALU.mult, op1=ALU.add).then_inc(A_used, 1)
                dve.wait_ge(A_used, 2 * (t + 1))
                link(dve.tensor_tensor(u[0:n, t % 2, :], u[0:n, t % 2, :], gate, ALU.mult))
                link(dve.scalar_tensor_tensor(out=u[0:n, t % 2, :], in0=x_tok[0:n, t, :], scalar=ALPHA, in1=u[0:n, t % 2, :],
                                              op0=ALU.mult, op1=ALU.add))
                layer_norm_stats(u[0:n, t % 2, :], n, t)

            def modulate2(t, n):
                scale = mod[:, 1, :] if t < TT else smod[0:NS, 1, :]
                shift = mod[:, 2, :] if t < TT else smod[0:NS, 2, :]
                dve.wait_ge(x1_ready, t + 1)
                if t >= 2:
                    dve.wait_ge(h2_stored[t % 2], 16 * (t // 2))
                    dve.wait_ge(h2T_ps, 2 * (t - 1))
                link(dve.tensor_tensor(h2[0:n, t % 2, :], x_tok[0:n, t, :], scale, ALU.mult))
                dve.tensor_tensor(h2[0:n, t % 2, :], h2[0:n, t % 2, :], shift, ALU.add).then_inc(h2_ready, 1)

            def routing(t, n):
                dve.wait_ge(h2T_ps, 2 * t + 1)
                dve.tensor_copy(h2T[:, 0:4, 0:n], B[4][:, :].rearrange("p (k m) -> p k m", m=P)[:, :, 0:n]).then_inc(h2T_v, 1)
                dve.wait_ge(lgT_ps, t + 1)
                dve.tensor_scalar(LGT[:, 0:n], B[6][0:NG + NE, 0:n], brt[:, 0:1], None, ALU.add).then_inc(lgT_ready, 1)
                dve.wait_ge(lg_ps, t + 1)
                step(dve.tensor_copy(lg8[0:n, 0:NG], B[6][0:n, 256:256 + NG]))
                link(dve.tensor_copy(lg[0:n, :], B[6][0:n, 256:256 + NG + NE]))
                link(dve.max(g8[0:n, :], lg8[0:n, :]))
                step(dve.tensor_scalar(rt[0:n, 0:1], g8[0:n, 0:1], -1.0, None, ALU.mult))
                link(dve.max_index(gi[0:n, :], g8[0:n, :], lg8[0:n, :]))
                link(dve.tensor_copy(rt[0:n, 4:5], gi[0:n, 0:1]))
                link(dve.tensor_scalar(le[0:n, :], iota_g[0:n, :], rt[0:n, 4:5], NEG, ALU.not_equal, ALU.mult))
                link(dve.tensor_tensor(le[0:n, :], le[0:n, :], lg[0:n, NG:NG + NE], ALU.add))
                link(dve.max(e8[0:n, :], le[0:n, :]))
                link(dve.max_index(ei[0:n, :], e8[0:n, :], le[0:n, :]))
                dve.tensor_tensor(rt[0:n, 1:2], e8[0:n, 1:2], e8[0:n, 0:1], ALU.subtract).then_inc(top_ready, 1)
                link(dve.tensor_copy(rt[0:n, 6:8], ei[0:n, 0:2]))
                for c in range(2):
                    step(dve.tensor_scalar(oh[0:n, c, :], iota_e[0:n, :], rt[0:n, 6 + c:7 + c], None, ALU.is_equal))
                settle()
                dve.tensor_tensor(hot[0:n, t, :], oh[0:n, 0, :], oh[0:n, 1, :], ALU.add).then_inc(hot_ready, 1)
                dve.wait_ge(top_exp, 2 * (t + 1))
                link(dve.tensor_scalar(rt[0:n, 8:9], rt[0:n, 3:4], 1.0, rt[0:n, 2:3], ALU.add, ALU.mult))
                link(dve.reciprocal(wt[0:n, t, 0:1], rt[0:n, 8:9]))
                step(dve.tensor_tensor(wt[0:n, t, 1:2], wt[0:n, t, 0:1], rt[0:n, 3:4], ALU.mult))
                dve.wait_ge(rank_ps, t + 1)
                for c in range(2):
                    link(dve.tensor_tensor_reduce(out=junk[0:n, :], in0=B[7][0:n, 0:NE], in1=oh[0:n, c, :], scale=1.0, scalar=0.0,
                                                  op0=ALU.mult, op1=ALU.add, accum_out=rt[0:n, 10 + c:11 + c]))
                link(dve.tensor_copy(rki[0:n, 0, :], rt[0:n, 10:12]))
                step(dve.tensor_scalar(rki[0:n, 1, :], rki[0:n, 0, :], 6, None, ALU.arith_shift_right))
                link(dve.scalar_tensor_tensor(out=rt[0:n, 12:14], in0=rt[0:n, 6:8], scalar=float(CAP), in1=rt[0:n, 10:12],
                                              op0=ALU.mult, op1=ALU.add))
                dve.scalar_tensor_tensor(out=slot[0:n, t, :], in0=rki[0:n, 1, :], scalar=float(SLOTS - CAP), in1=rt[0:n, 12:14],
                                         op0=ALU.mult, op1=ALU.add).then_inc(slot_ready, 1)

            for i in range(TT + 2):
                if i == TT:
                    dve.wait_ge(smod_in, 64)
                if i <= TT:
                    residual(*TILES[i])
                if i >= 1:
                    routing(*TILES[i - 1])
                if i <= TT:
                    modulate2(*TILES[i])
            dve.wait_ge(count_ps, 1)
            link(dve.tensor_reduce(rt[:, 14:15], B[5][:, 0:NE], AX.X, ALU.max))
            dve.tensor_scalar(over[:, :], rt[:, 14:15], float(CAP), None, ALU.is_gt).then_inc(over_ready, 1)

            def pair(n, par_, peeled):
                dve.wait_ge(XT_ps, 2 * n + 1)
                dve.tensor_copy(XT[:, par_, 0:4, :], B[0][:, :].rearrange("p (k m) -> p k m", m=P)).then_inc(XT_v, 1)
                dve.wait_ge(silu_done, n + 1)
                if not peeled:
                    dve.wait_ge(zT_ps, n)
                dve.tensor_tensor(z[:, :], silu_g[:, :], B[2 + par_][:, DE:2 * DE], ALU.mult).then_inc(z_ready, 1)
                dve.wait_ge(y_ps, n + 1)

            def round_(r, first):
                n0 = r * NPAIR

                def turn(i, peeled):
                    n = n0 + 2 * i
                    for par_ in range(2):
                        pair(n + par_, par_, peeled and par_ == 0)
                        if not peeled:
                            dve.wait_ge(y_out[par_], 8 * n)
                        dve.tensor_copy(yo[:, par_, 0:512], B[5][:, :]).then_inc(y_v, 1)

                if first:
                    turn(0, True)
                    with dve.Fori(1, NPAIR // 2) as i:
                        turn(i, False)
                else:
                    with dve.Fori(0, NPAIR // 2) as i:
                        turn(i, False)

            round_(0, True)
            dve.wait_ge(over_ready, 1)
            some_over = dve.value_load(over[0:1, 0:1], min_val=0, max_val=1)
            with dve.If(some_over > 0):
                with dve.Fori(1, ROUNDS) as r:
                    round_(r, False)
            dve.wait_ge(lnp_in, 48)
            for t, n in TILES:
                gate = mod[:, 0, :] if t < TT else smod[0:NS, 3, :]
                dve.wait_ge(f_used, t + 1)
                f = yy[0:n, t, 0, :]
                link(dve.scalar_tensor_tensor(out=f, in0=yy[0:n, t, 1, :], scalar=wt[0:n, t, 1:2], in1=f, op0=ALU.mult, op1=ALU.add))
                link(dve.tensor_tensor(f, f, gate, ALU.mult))
                link(dve.scalar_tensor_tensor(out=f, in0=x_tok[0:n, t, :], scalar=ALPHA, in1=f, op0=ALU.mult, op1=ALU.add))
                layer_norm_stats(f, n, TT + 1 + t)
                dve.wait_ge(norm_ready, TT + 2 + t)
                link(dve.tensor_scalar(f, f, st1[0:n, 2:3], st1[0:n, 3:4], ALU.mult, ALU.add))
                if t >= 2:
                    dve.wait_ge(out_ready, t - 1)
                dve.tensor_tensor(ff[0:n, t % 2, :], f, mod[0:n, 3, :], ALU.mult).then_inc(xhat2_ready, 1)

        @block.tensor
        def _(pe):
            pe.wait_ge(consts, 1)
            pe.wait_ge(csil_ready, 1)
            for k in range(KD):
                last = pe.transpose(B[7][:, 16 * k:16 * k + NC], csil[:, k::KD], ident[0:NC, 0:NC])
            last.then_inc(cT_ps, 1)
            pe.wait_ge(x_in, 32)
            for k in range(KD):
                if k >= 4:
                    if k % 2:
                        pe.wait_ge(xT_a, (k - 4) // 2 + 1)
                    else:
                        pe.wait_ge(xT_v, (k - 4) // 2 + 1)
                for t in range(TT):
                    last = pe.transpose(B[k % 4][:, t * P:(t + 1) * P], x_tok[:, t, k::KD], ident[:, :])
                last.then_inc(xT_ps, 1)
            for k in range(KD):
                last = pe.transpose(B[6][:, NS * k:NS * k + NS], x_tok[0:NS, TT, k::KD], ident[0:NS, 0:NS])
            last.then_inc(xs_ps, 1)
            pe.wait_ge(small_in, 16 * 14)
            pe.transpose(B[5][:, 0:40], prm[:, :], ident[0:40, 0:40])
            for f in range(FW):
                last = pe.transpose(B[5][:, 64 + 32 * f:96 + 32 * f], stt_in[:, f * P:(f + 1) * P], ident[0:32, 0:32])
            last.then_inc(small_ps, 1)

            def modulation(r):
                if r:
                    pe.wait_ge(m_ready, r)
                for k in range(KD):
                    j = r * KD + k
                    if r:
                        pe.wait_ge(ada2_in[j % 4], 16 * ((j - KD) // 4 + 1))
                    else:
                        pe.wait_ge(ada_in[j % 4], 16 * (j // 4 + 1))
                    for g in range(4):
                        last = pe.matmul(B[4][32 * g:32 * g + 32, :], cT[:, k, :], ada[:, j % 4, g * 512:(g + 1) * 512],
                                         start=(k == 0), stop=(k == KD - 1))
                    last.then_inc(ada_used, 1)

            pe.wait_ge(cT_ready, 1)
            modulation(0)
            pe.wait_ge(m_ready, 1)
            pe.wait_ge(small_ready, 2)
            for k in range(KD):
                last = pe.transpose(B[5 + 2 * (k // 4)][0:64, (k % 4) * P:(k % 4 + 1) * P], m_sb[:, 0, k::KD], ident[:, :])
            last.then_inc(mT_ps, 1)

            def evacuated(q):
                if q < FW:
                    pe.wait_ge(zin_ready, 3 * (q + 1))
                elif q < K_AT:
                    pe.wait_ge(q_ready, 2 * (q - FW + 1))
                elif q < GELU_AT:
                    pe.wait_ge(kv_ready, 2 * (q - K_AT + 1))
                else:
                    pe.wait_ge(gelu_ready, 2 * (q - GELU_AT + 1))

            def project_in(q):
                n = WCH.index(ORDER[q] // 2)
                pe.wait_ge(win_in[n % 3], 16 * (n // 3 + 1))
                if q >= 2:
                    evacuated(q - 2)
                col = (ORDER[q] % 2) * P
                for h, (c0, cn) in enumerate(HALVES):
                    for k in range(KD):
                        if q == 0 and h == 0:
                            if k % 2:
                                pe.wait_ge(h_a, k // 2 + 1)
                            else:
                                pe.wait_ge(h_v, k // 2 + 1)
                        if q == 0 and h == 1 and k == 0:
                            pe.wait_ge(h_v, 5)
                        last = pe.matmul(B[(q % 2) * 2 + h][:, 0:cn], win[:, n % 3, k, col:col + P], hT[:, k, c0:c0 + cn],
                                         start=(k == 0), stop=(k == KD - 1))
                    last.then_inc(win_ps, 1)

            def lru_gates(f):
                pe.wait_ge(xc_ready, f + 1)
                if f == 0:
                    pe.wait_ge(kv_in, 16 * 4)
                    pe.wait_ge(wrg_in, 16 * 4)
                    pe.wait_ge(mT_ready, 4)
                for g in range(2):
                    for h in range(2):
                        if 2 * f + g:
                            pe.wait_ge(gate_tanh, 4 * f + 2 * (g - 1) + h + 1)
                        pe.matmul(B[6 + h][:, 0:XH], wrg[:, g, f, :], xc[:, f % 3, h * XH:(h + 1) * XH],
                                  start=True, stop=True).then_inc(gate_ps, 1)

            for q in range(len(ORDER)):
                project_in(q)
                if 2 <= q < 2 + FW:
                    lru_gates(q - 2)
                if q == 5:
                    modulation(1)
                if q == 9:
                    modulation(2)

            pe.wait_ge(kv_ready, 4)
            pe.wait_ge(m_ready, 4)
            for t in range(TT):
                pe.transpose(B[4][:, t * P:(t + 1) * P], kvT[:, 1, t * P:(t + 1) * P], ident[:, :])
            pe.transpose(B[5][:, 0:P], kvT[:, 0, T - P:T], ident[:, :])
            for n in range(2):
                last = pe.transpose(B[5][0:NS, (1 + n) * P:(2 + n) * P], kvT[:, n, T:NT], ident[:, :])
            last.then_inc(vt_ps, 1)
            pe.wait_ge(lru_done, FW)
            pe.wait_ge(gate_tanh, 4 * FW)
            for f in range(FW):
                last = pe.transpose(B[6][0:20, f * P:(f + 1) * P], tail_in[:, f, :], ident[:, :])
            last.then_inc(tail_ps, 1)
            for b in range(NS):
                if b == 4:
                    pe.wait_ge(gate_tanh, 4 * FW)
                if b == 0:
                    pe.wait_ge(tail_ready, 1)
                last = pe.transpose(B[6 + b // 4][:, (b % 4) * P:(b % 4 + 1) * P], kc[:, b, :], ident[:, :])
                if b % 4 == 3:
                    last.then_inc(kcT_ps, 1)
            pe.wait_ge(kcT_ready, 2)
            pe.wait_ge(qz_ready, 5)
            for b in range(NS):
                j = b % 4
                c0 = (b // 4) * (WIN + 1)
                last = pe.matmul(B[7][32 * j:32 * j + 32, c0:c0 + WIN + 1], qz[:, b, :], kbT[:, b, :], start=True, stop=True)
            last.then_inc(ss_ps, 1)

            def scores(b):
                k0 = max(0, b - 1) * P
                kn = (b + 1) * P - k0
                for p in range(NH // 2):
                    if b:
                        pe.wait_ge(S_masked, NH * (b - 1) + 2 * p + 2)
                    pe.matmul(B[p][:, 0:2 * kn], qT[:, p, b * P:(b + 1) * P], kTz[:, p // 2, :, k0:k0 + kn],
                              start=True, stop=True).then_inc(S_ps, 1)

            def pt_count(b):
                return 0 if b == 0 else 2 + 4 * (b - 1)

            def weigh(b):
                first = pt_count(b)
                kbs = (0, 1) if b else (1,)
                n = 0
                for kb in kbs:
                    for kv in range(NKV):
                        pe.wait_ge(P_ready, NH * b + G * (kv + 1))
                        if first + n >= 2:
                            pe.wait_ge(PT_ready, first + n - 1)
                        for g in range(G):
                            last = pe.transpose(B[4 + n % 2][:, g * P:(g + 1) * P],
                                                Pm[b % 2][:, kv * G + g, kb * P:(kb + 1) * P], ident[:, :])
                        last.then_inc(PT_ps, 1)
                        n += 1
                if b:
                    pe.wait_ge(O_stored, 2 * b)
                pe.wait_ge(PT_ready, first + n)
                for kb in kbs:
                    for kv in range(NKV):
                        last = pe.matmul(B[6][64 * kv:64 * kv + 64, :], vtok[:, b - 1 + kb, 64 * kv:64 * kv + 64],
                                         PT[:, kb, kv, :], start=(kb == kbs[0]), stop=(kb == 1))
                last.then_inc(O_ps, 1)

            evacuated(GELU_AT + 2)
            evacuated(GELU_AT + 3)
            scores(0)
            pe.wait_ge(sP_ready, 2)
            for n in range(2):
                pe.transpose(B[6][:, n * P:(n + 1) * P], ps[:, n, 0:WIN], ident[:, :])
            for n in range(2):
                last = pe.transpose(B[5][0:NS, n * P:(n + 1) * P], pnm[:, n, :], ident[:, :])
            last.then_inc(sPT_ps, 1)
            pe.wait_ge(sPT_ready, 2)
            for b in range(NS):
                pe.matmul(B[7][:, 32 * b:32 * b + 32], knv[:, 1, :], pnd[:, b // 4, 32 * (b % 4):32 * (b % 4) + 32], start=True, stop=False)
                last = pe.matmul(B[7][:, 32 * b:32 * b + 32], vc[:, b, :], psT[:, b // 4, 32 * (b % 4):32 * (b % 4) + 32],
                                 start=False, stop=True)
            last.then_inc(sO_ps, 1)
            for b in range(1, TT + 1):
                if b < TT:
                    scores(b)
                weigh(b - 1)

            pe.wait_ge(PT_ready, pt_count(TT))
            for f in range(FW):
                for g in range(2):
                    pe.wait_ge(sq_ready, 4 * g + f + 1 if g == 0 else 2 * FW)
                    for h in range(2):
                        j = 2 * g + h
                        last = pe.matmul(B[4][32 * j:32 * j + 32, 0:264], ones[:, :], sq[:, 4 * g + f, h * HALF:h * HALF + 264],
                                         start=(f == 0), stop=(f == FW - 1))
            last.then_inc(ss_sum_ps, 1)
            pe.wait_ge(rs_ready, 2)
            for c in range(2):
                pe.transpose(B[5][:, c * P:(c + 1) * P], rs[:, c * P:(c + 1) * P], ident[:, :])
            pe.transpose(B[5][0:NS, 2 * P:3 * P], rs[:, 2 * P:2 * P + NS], ident[:, :]).then_inc(rsT_ps, 1)

            def project_out(t, n):
                if t == 0:
                    pe.wait_ge(wout_scaled, 2 * FW)
                if t < TT:
                    for g in range(2):
                        if t:
                            pe.wait_ge(A_used if g else L_ready, 2 * t)
                        for f in range(FW):
                            for c in range(2):
                                last = pe.matmul(B[2 * g + c][:, :], yT[:, FW * g + f, t * P:(t + 1) * P],
                                                 wout[:, FW * g + f, c * 512:(c + 1) * 512], start=(f == 0), stop=(f == FW - 1))
                        last.then_inc(A_ps if g else L_ps, 1)
                else:
                    pe.wait_ge(L_ready, 2 * t)
                    for f in range(FW):
                        for g in range(2):
                            for c in range(2):
                                j = 2 * g + c
                                last = pe.matmul(B[0][32 * j:32 * j + n, :], yT[:, FW * g + f, T:NT],
                                                 wout[:, FW * g + f, c * 512:(c + 1) * 512], start=(f == 0), stop=(f == FW - 1))
                    last.then_inc(L_ps, 1)

            def route(t, n):
                pe.wait_ge(h2_ready, t + 1)
                if t == 0:
                    pe.wait_ge(rT_ready, 3)
                else:
                    pe.wait_ge(h2T_v, t)
                    pe.wait_ge(h2T_a, t)
                for k in range(KD):
                    last = pe.transpose(B[4 + k // 4][:, (k % 4) * P:(k % 4) * P + n], h2[0:n, t % 2, k::KD], ident[0:n, 0:n])
                    if k % 4 == 3:
                        last.then_inc(h2T_ps, 1)
                if t == 0:
                    pe.wait_ge(wr_in, 16 * 5)
                    pe.wait_ge(O_stored, 2 * TT)
                else:
                    pe.wait_ge(top_ready, t)
                pe.wait_ge(h2T_v, t + 1)
                pe.wait_ge(h2T_a, t + 1)
                for k in range(KD):
                    last = pe.matmul(B[6][0:NG + NE, 0:n], wr[:, k, :], h2T[:, k, 0:n], start=(k == 0), stop=(k == KD - 1))
                last.then_inc(lgT_ps, 1)
                pe.wait_ge(lgT_ready, t + 1)
                pe.transpose(B[6][0:n, 256:256 + NG + NE], LGT[:, 0:n], ident[0:NG + NE, 0:NG + NE]).then_inc(lg_ps, 1)
                pe.wait_ge(hot_ready, t + 1)
                if t:
                    pe.wait_ge(slot_ready, t)
                else:
                    pe.wait_ge(sO_stored, 2)
                for t2 in range(t):
                    pe.matmul(B[7][0:n, 0:NE], ones_bf[:, 0:n], hot[:, t2, :], start=(t2 == 0), stop=False)
                pe.matmul(B[7][0:n, 0:NE], tri[0:n, 0:n], hot[0:n, t, :], start=(t == 0), stop=True).then_inc(rank_ps, 1)

            for i in range(TT + 2):
                if i <= TT:
                    project_out(*TILES[i])
                if i >= 1:
                    route(*TILES[i - 1])
            for t, n in TILES:
                last = pe.matmul(B[5][:, 0:NE], ones_bf[0:n, :], hot[0:n, t, :], start=(t == 0), stop=(t == TT))
            last.then_inc(count_ps, 1)

            def pair(n, turn, r, par_, peeled):
                pe.wait_ge(X_in[par_], 16 * turn + 16 + (16 * r if par_ == 0 else 0))
                if not (peeled and par_ == 0):
                    pe.wait_ge(XT_v, n)
                    pe.wait_ge(XT_a, n)
                for k in range(KD):
                    last = pe.transpose(B[k // 4][:, (k % 4) * P:(k % 4 + 1) * P], X[:, par_, k::KD], ident[:, :])
                    if k % 4 == 3:
                        last.then_inc(XT_ps, 1)
                pe.wait_ge(gu_in[par_], 64 * turn + 64)
                pe.wait_ge(XT_v, n + 1)
                pe.wait_ge(XT_a, n + 1)
                for k in range(KD):
                    for q in range(2):
                        last = pe.matmul(B[2 + par_][64 * q:64 * q + 64, :], XT[:, par_, k, 64 * q:64 * q + 64],
                                         wgu[2 * par_ + q][:, :, k, :], start=(k == 0), stop=(k == KD - 1))
                last.then_inc(gu_ps, 1)
                pe.wait_ge(z_ready, n + 1)
                for k in range(2):
                    last = pe.transpose(B[4][:, k * P:(k + 1) * P], z[:, k::2], ident[:, :])
                last.then_inc(zT_ps, 1)
                pe.wait_ge(dn_in[par_], 32 * turn + 32)
                pe.wait_ge(zT_ready, n + 1)
                if not (peeled and par_ == 0):
                    pe.wait_ge(y_v, n)
                    pe.wait_ge(y_a, n)
                for k in range(2):
                    for c in range(2):
                        for q in range(2):
                            last = pe.matmul(B[5 + c][64 * q:64 * q + 64, :], zT[:, k, 64 * q:64 * q + 64],
                                             wdn[2 * par_ + q][:, k, c * 512:(c + 1) * 512], start=(k == 0), stop=(k == 1))
                last.then_inc(y_ps, 1)

            def turn(i, r, peeled):
                for par_ in range(2):
                    pair(r * NPAIR + 2 * i + par_, r * (NPAIR // 2) + i, r, par_, peeled)

            pe.wait_ge(over_ready, 1)
            turn(0, 0, True)
            with pe.Fori(1, NPAIR // 2) as i:
                turn(i, 0, False)
            some_over = pe.value_load(over[0:1, 0:1], min_val=0, max_val=1)
            with pe.If(some_over > 0):
                with pe.Fori(1, ROUNDS) as r:
                    with pe.Fori(0, NPAIR // 2) as i:
                        turn(i, r, False)


_INS = ["x_prompt", "x_sample", "c_prompt", "c_sample", "state_conv", "state_h", "cache_k", "cache_v", "w_ada", "b_ada",
        "w_in", "conv_w", "conv_b", "w_rg_a", "b_rg_a", "w_rg_x", "b_rg_x", "lru_lambda", "sinks", "g_lru", "g_attn",
        "w_out", "ln1_g", "ln1_b", "w_group", "b_group", "w_router", "b_router", "w_gate", "w_up", "w_down",
        "ln2_g", "ln2_b"]
_OUTS = [(1, T, D), (NS, 1, D), (1, 1, CW - 1, W), (1, 1, W), (1, 1, WIN, NKV, HD), (1, 1, WIN, NKV, HD),
         (1, NS, CW - 1, W), (1, NS, W), (1, NS, WIN, NKV, HD), (1, NS, WIN, NKV, HD)]


def kernel(**inputs):
    import numpy as np
    import concourse.bacc as bacc
    from concourse.bass_utils import run_bass_kernel_spmd

    nc = bacc.Bacc("TRN2", target_bir_lowering=False, num_devices=1)
    arrays, A, O = {}, {}, []
    for name in _INS:
        a = np.ascontiguousarray(inputs[name])
        arrays[f"in_{name}"] = a
        A[name] = nc.dram_tensor(f"in_{name}", a.shape, mybir.dt.from_np(a.dtype), kind="ExternalInput").ap()
    for i, shape in enumerate(_OUTS):
        O.append(nc.dram_tensor(f"out_{i}", shape, F32, kind="ExternalOutput").ap())
    build(nc, A, O)
    r = run_bass_kernel_spmd(nc, [arrays], core_ids=[0])
    return tuple(r.results[0][f"out_{i}"] for i in range(len(_OUTS)))
```

```python
import concourse.bass as bass
from concourse import mybir
from contextlib import ExitStack

F32 = mybir.dt.float32
BF16 = mybir.dt.bfloat16
I32 = mybir.dt.int32
U32 = mybir.dt.uint32
ALU = mybir.AluOpType
ACT = mybir.ActivationFunctionType
AX = mybir.AxisListType

P = 128
D = 1024
KD = D // P
T = 512
NS = 8
NT = T + NS
TT = T // P
HALF = 256
NC = NS + 1
W = 512
FW = W // P
INW = 1792
CW = 4
LB = 64
NH, NKV, HD = 8, 2, 64
G = NH // NKV
WIN = 128
NG, EPG, NE = 4, 8, 32
DE = 256
CAP = 64
NPAIR = NE // 2
ROWS = (NT + CAP - 1) // CAP * CAP
MAXSTEP = (2 * NT + (CAP - 1) * NPAIR) // CAP
TURNS = (MAXSTEP + 1) // 2
MINTURNS = NPAIR // 2
NSTEP = 2 * TURNS + 2
TABROWS = (NE + 2) * ROWS
ALPHA = 2.0 ** 0.25
LN_EPS = 1e-5
RMS_EPS = 1e-6
SCALE = HD ** -0.5
NEG = -1e30
NOWHERE = 1 << 20
CONV = T + CW - 1 + NS * CW
XC = CONV - (CW - 1)
S0 = T + CW - 1
XH = XC // 2


def build(nc, A, O):
    ctx = ExitStack()
    with ctx:
        base = (nc.sbuf_base + 63) // 64 * 64
        size = {"x": 20480, "h": 16640, "y": 16640, "w": 32768, "m": 20480, "r": 98304}
        at, here = {}, base
        for k, v in size.items():
            at[k] = here
            here += v
        small_at = [here]

        def place(name, shape, off, dt=F32):
            return nc.alloc_sbuf_tensor_at(name, shape, dt, offset=off)

        def row(name, shape, region, off, dt=F32):
            return place(name, shape, at[region] + off, dt)

        def small(name, shape, dt=F32):
            n = 1
            for s in shape[1:]:
                n *= s
            n *= 2 if dt == BF16 else 4
            t = place(name, shape, small_at[0], dt)
            small_at[0] += (n + 31) // 32 * 32
            assert small_at[0] <= nc.sbuf_usable_end, small_at
            return t

        x_tok = row("x_tok", [P, TT + 1, D], "x", 0)
        hT = row("hT", [P, KD, NT], "h", 0)
        yT = row("yT", [P, 2 * FW, NT], "y", 0)
        xb = row("xb", [P, 2, CONV], "w", 0)
        xc = row("xc", [P, 3, XC], "w", 4384)
        tr = row("tr", [P, XC], "w", 10912)
        ti = row("ti", [P, XC], "w", 13088)
        aa = row("aa", [P, XC], "w", 15264)
        th = row("th", [P, XC], "w", 17440)
        a2 = row("a2", [P, XC], "w", 19616)
        wrg = row("wrg", [P, 2, FW, P], "w", 21792)
        m_sb = row("m_sb", [P, 3, 512], "w", 25888)
        gel = row("gel", [P, FW, NT], "w", 0)
        wout = row("wout", [P, KD, D], "w", 0)
        X = row("X", [P, 2, D], "w", 0)
        XT = row("XT", [P, 2, KD, P], "w", 8192)
        silu_g = row("silu_g", [P, DE], "w", 16384)
        z = row("z", [P, DE], "w", 17408)
        zT = row("zT", [P, 2, P], "w", 18432)
        yo = row("yo", [P, 2, D], "w", 19456)
        kc = row("kc", [P, NS, P], "m", 0)
        kbT = row("kbT", [P, NS, WIN + 1], "m", 4096)
        vc = row("vc", [P, NS, P], "m", 8224)
        ps = row("ps", [P, 2, WIN + 1], "m", 12320)
        psT = row("psT", [P, 2, P], "m", 13376)
        qz = row("qz", [P, NS, 32], "m", 14400)
        pnd = row("pnd", [NS, 2, P], "m", 15424)
        pnm = row("pnm", [P, 2, NS], "m", 16448)
        knv = row("knv", [NS, 2, P], "m", 16512)
        klast = row("klast", [P, P], "m", 17536)
        tails = row("tails", [20, FW, P], "m", 18048)
        mod = row("mod", [P, 5, D], "m", 0)
        sq = row("sq", [P, 2 * FW, NT], "h", 0)
        smod = row("smod", [NS, 4, D], "h", 0)
        ada = row("ada", [P, 4, 2048], "r", 0)
        win = row("win", [P, 3, KD, 256], "r", 32768)
        crow = row("crow", [NC, D], "r", 57344)
        csil = row("csil", [NC, D], "r", 61440)
        fill = row("fill", [P, TABROWS * 2 // P], "r", 65536, I32)
        prm = row("prm", [40, P], "r", 66784)
        stt_in = row("stt_in", [32, W], "r", 67296)
        b_row = row("b_row", [P, 3, 512], "y", 4 * NT * 4)
        cT = row("cT", [P, KD, 32], "r", 96448)
        mT = row("mT", [P, 2, KD, NC], "r", 97472)
        qT = row("qT", [P, FW, NT], "r", 71744)
        kTz = row("kTz", [P, NKV, 2, T], "r", 57344)
        vtok = row("vtok", [P, TT, P], "r", 65536)
        kvT = row("kvT", [P, 2, NT], "r", 67584)
        PT = row("PT", [P, 2, NKV, G * P], "r", 80064)
        Pm = [row("P0", [P, NH, 2 * P], "r", 88256), row("P1", [P, NH, 2 * P], "h", 4 * NT * 4)]
        u = row("u", [P, 2, D], "r", 73728)
        h2 = row("h2", [P, 2, D], "r", 81920)
        h2T = row("h2T", [P, KD, P], "r", 90112)
        wr = row("wr", [P, KD, NG + NE], "r", 94208)
        LGT = row("LGT", [NG + NE, P], "r", 95360)
        lg = row("lg", [P, NG + NE], "r", 95872)
        le = row("le", [P, NE], "r", 96032)
        oh = row("oh", [P, 2, NE], "r", 96160)
        rs = row("rs", [P, 264], "r", 96448)
        EXW = 2 * KD * DE + 2 * D
        GU = 2 * KD * DE
        wex = row("wex", [P, 4, EXW], "r", 0)
        yy = row("yy", [P, TT + 1, 2, D], "r", 0)
        ff = row("ff", [P, 2, D], "r", 81920)
        yout = row("yout", [P, 2, D], "w", 0)

        ident = small("ident", [P, P])
        mask = small("mask", [P, 2, P])
        tri = small("tri", [P, P], BF16)
        ones_bf = small("ones_bf", [P, P], BF16)
        ones = small("ones", [P, 32])
        iota_e = small("iota_e", [P, NE])
        iota_g = small("iota_g", [P, NE])
        iota_i = small("iota_i", [P, 2, NE], I32)
        pair_id = small("pair_id", [P, TT + 1, 2, 2], I32)
        bsel = small("bsel", [P, 2, NS])
        par = small("par", [P, 40])
        stT = small("stT", [P, FW, 32])
        sp4 = small("sp4", [P, 2, FW])
        spt = small("spt", [P, 6, FW])
        tail_in = small("tail_in", [P, FW, 20])
        sinks8 = small("sinks8", [P, 2, NH])
        sink_s = small("sink_s", [P, 2])
        mx = small("mx", [P, 2, NH])
        nb = small("nb", [P, 2, NH])
        es = small("es", [P, 2, NH])
        sums = small("sums", [P, 2, NH])
        rden = small("rden", [P, 2, NH])
        sv = small("sv", [P, 8, 2])
        rT = small("rT", [P, TT + 1, 2])
        brt = small("brt", [NG + NE, 1])
        bn = small("bn", [P, 2, 6])
        mv = small("mv", [P, 2])
        st1 = small("st1", [P, 4])
        lg8 = small("lg8", [P, 8])
        g8 = small("g8", [P, 8])
        gi = small("gi", [P, 8], U32)
        e8 = small("e8", [P, 8])
        ei = small("ei", [P, 8], U32)
        rt = small("rt", [P, 16])
        gexp = small("gexp", [P, NG])
        hot = small("hot", [P, TT + 1, NE], BF16)
        junk = small("junk", [P, NE])
        wt = small("wt", [P, TT + 1, 2])
        slot = small("slot", [P, TT + 1, 2], U32)
        pmax = small("pmax", [P, NPAIR])
        pnum_i = small("pnum_i", [P, 2, NPAIR], I32)
        pnum = small("pnum", [P, NPAIR])
        pend = small("pend", [P, NPAIR])
        pend_i = small("pend_i", [P, NPAIR], I32)
        sgrid_i = row("sgrid_i", [P, NSTEP, NPAIR], "y", 0, I32)
        sgrid = row("sgrid", [P, NSTEP, NPAIR], "y", 4096)
        past = row("past", [P, NSTEP, NPAIR], "y", 8192)
        spair = small("spair", [P, 2, NSTEP])
        srow = small("srow", [P, NSTEP])
        row_i = small("row_i", [P, NSTEP], I32)
        row0 = small("row0", [P, NSTEP])
        tabrow = small("tabrow", [P, NSTEP], I32)
        place_i = small("place_i", [P, NSTEP], I32)
        spair_i = small("spair_i", [P, NSTEP], I32)
        wneed = small("wneed", [P, NSTEP], I32)
        turns = small("turns", [P, 2], I32)
        cur = small("cur", [P, 2], I32)
        idx = small("idx", [P, 2, 2], I32)
        mark = small("mark", [P, 1])

        B = [ctx.enter_context(nc.psum_tensor(f"B{i}", [P, 512], F32)) for i in range(8)]

        m_dram = nc.dram_tensor("m_dram", (NC, 6, D), F32).ap()
        h_dram = nc.dram_tensor("h_dram", (NT, D), F32).ap()
        y_dram = nc.dram_tensor("y_dram", (2 * NT, D), F32).ap()
        table = nc.dram_tensor("table", (TABROWS, 2), I32).ap()

        def sem(name):
            return ctx.enter_context(nc.semaphore(name))

        c_in, x_in, small_in, kv_in, brow_in, wrg_in = (sem(n) for n in ("c_in", "x_in", "small_in", "kv_in", "brow_in", "wrg_in"))
        ada_in = [sem(f"ada_in{i}") for i in range(4)]
        ada2_in = [sem(f"ada2_in{i}") for i in range(4)]
        win_in = [sem(f"win_in{i}") for i in range(3)]
        wout_in, mod_in, smod_in, lnp_in, wr_in = (sem(n) for n in ("wout_in", "mod_in", "smod_in", "lnp_in", "wr_in"))
        w_in, w_ready = [sem(f"w_in{i}") for i in range(2)], sem("w_ready")
        consts, sink_zero, wrg_zero, kz_zero, X_zero = (sem(n) for n in ("consts", "sink_zero", "wrg_zero", "kz_zero", "X_zero"))
        csil_ready, cT_ps, cT_ready = sem("csil_ready"), sem("cT_ps"), sem("cT_ready")
        xT_ps, xT_v, xT_a, xs_ps = sem("xT_ps"), sem("xT_v"), sem("xT_a"), sem("xs_ps")
        small_ps, small_ready = sem("small_ps"), sem("small_ready")
        ada_used, m_ready, m_stored = sem("ada_used"), sem("m_ready"), sem("m_stored")
        mT_ps, mT_ready = sem("mT_ps"), sem("mT_ready")
        h_v, h_a = sem("h_v"), sem("h_a")
        win_ps, zin_ready = sem("win_ps"), sem("zin_ready")
        xc_ready, gate_ps, gate_tanh, decay_ready = sem("xc_ready"), sem("gate_ps"), sem("gate_tanh"), sem("decay_ready")
        bnorm_ready, broot_ready, lru_done, gelu_ready = sem("bnorm_ready"), sem("broot_ready"), sem("lru_done"), sem("gelu_ready")
        sp_exp, sp_x, ylru = sem("sp_exp"), sem("sp_x"), sem("ylru")
        kv_ready, q_ready = sem("kv_ready"), sem("q_ready")
        vt_ps, vt_ready, tail_ps, tail_ready = sem("vt_ps"), sem("vt_ready"), sem("tail_ps"), sem("tail_ready")
        kcT_ps, kcT_ready, qz_ready, ss_ps = sem("kcT_ps"), sem("kcT_ready"), sem("qz_ready"), sem("ss_ps")
        snb_ready, sexp_done, sP_ready, sPT_ps, sPT_ready, sO_ps, sO_stored = (sem(n) for n in (
            "snb_ready", "sexp_done", "sP_ready", "sPT_ps", "sPT_ready", "sO_ps", "sO_stored"))
        S_ps, S_masked, nb_ready, exp_done, rden_ready, P_ready = (sem(n) for n in (
            "S_ps", "S_masked", "nb_ready", "exp_done", "rden_ready", "P_ready"))
        PT_ps, PT_ready, O_ps, O_stored = (sem(n) for n in ("PT_ps", "PT_ready", "O_ps", "O_stored"))
        sq_ready, ss_sum_ps, ms_ready, rs_ready, rsT_ps, rT_ready = (sem(n) for n in (
            "sq_ready", "ss_sum_ps", "ms_ready", "rs_ready", "rsT_ps", "rT_ready"))
        wout_scaled, L_ps, A_ps, L_ready, A_used = (sem(n) for n in (
            "wout_scaled", "L_ps", "A_ps", "L_ready", "A_used"))
        var_ready, std_ready, norm_ready, xhat_ready, x1_ready, h2_ready = (sem(n) for n in (
            "var_ready", "std_ready", "norm_ready", "xhat_ready", "x1_ready", "h2_ready"))
        h2_stored = [sem("h2_stored0"), sem("h2_stored1")]
        h2T_ps, h2T_v, h2T_a, lgT_ps, lgT_ready, lg_ps = (sem(n) for n in (
            "h2T_ps", "h2T_v", "h2T_a", "lgT_ps", "lgT_ready", "lg_ps"))
        top_ready, top_exp, hot_ready, rank_ps, slot_ready = (sem(n) for n in (
            "top_ready", "top_exp", "hot_ready", "rank_ps", "slot_ready"))
        tab_init, tab_done, count_ps, steps_ready, grid_ready = (sem(n) for n in (
            "tab_init", "tab_done", "count_ps", "steps_ready", "grid_ready"))
        idx_in, idx_cur = [sem("idx_in0"), sem("idx_in1")], sem("idx_cur")
        X_in = [sem("X_in0"), sem("X_in1")]
        XT_ps, XT_v, XT_a, gu_ps, silu_done, z_ready, zT_ps, zT_ready, y_ps, y_v, y_a = (sem(n) for n in (
            "XT_ps", "XT_v", "XT_a", "gu_ps", "silu_done", "z_ready", "zT_ps", "zT_ready", "y_ps", "y_v", "y_a"))
        y_out = [sem("y_out0"), sem("y_out1")]
        experts_done, yy_in, out_ready, out_done = sem("experts_done"), [sem(f"yy_in{i}") for i in range(TT + 1)], sem("out_ready"), [sem("out_done0"), sem("out_done1")]
        f_used, xhat2_ready = sem("f_used"), sem("xhat2_ready")
        state_done, cache_done = sem("state_done"), sem("cache_done")
        dve_step, act_step, pool_step = sem("dve_step"), sem("act_step"), sem("pool_step")

        ORDER = [0, 1, 2, 3, 8, 9, 10, 11, 12, 13, 4, 5, 6, 7]
        WCH = [0, 1, 4, 5, 6, 2, 3]
        GELU_AT, Q_AT, K_AT = 10, 4, 8
        HALVES = [(0, HALF), (HALF, NT - HALF)]
        TILES = [(t, P) for t in range(TT)] + [(TT, NS)]

        def over_steps(v):
            return v[:, :].rearrange("p (a n) -> p a n", a=1).broadcast_to((P, NSTEP, NPAIR))

        block = ctx.enter_context(nc.Block())

        def pair_rows(ap):
            return ap.rearrange("(p k) n -> p k n", k=KD)

        wg_d = A["w_gate"][0].rearrange("e (p k) f -> e p k f", k=KD)
        wu_d = A["w_up"][0].rearrange("e (p k) f -> e p k f", k=KD)
        wd_d = A["w_down"][0].rearrange("e (p k) d -> e p k d", k=2)

        @block.sync
        def _(sp):
            sp.dma_start(crow[0:NS, :], A["c_sample"][:, :]).then_inc(c_in, 16)
            sp.dma_start(crow[NS:NC, :], A["c_prompt"][:, :]).then_inc(c_in, 16)
            sp.dma_start(x_tok[:, 0:TT, :], A["x_prompt"][0].rearrange("(t p) d -> p t d", p=P)).then_inc(x_in, 16)
            sp.dma_start(x_tok[0:NS, TT, :], A["x_sample"].rearrange("b s d -> (b s) d")).then_inc(x_in, 16)
            wa = A["w_ada"][0].rearrange("(p k) n -> p k n", k=KD)
            for j in range(KD):
                if j >= 4:
                    sp.wait_ge(ada_used, j - 3)
                sp.dma_start(ada[:, j % 4, :], wa[:, j, 0:2048]).then_inc(ada_in[j % 4], 16)
            wi = pair_rows(A["w_in"][0])
            for n, c in enumerate(WCH):
                if n >= 3:
                    sp.wait_ge(win_ps, 4 * (n - 2))
                sp.dma_start(win[:, n % 3, :, :], wi[:, :, c * 256:(c + 1) * 256]).then_inc(win_in[n % 3], 16)
            sp.wait_ge(ada_used, 24)
            sp.wait_ge(win_ps, 2 * len(ORDER))

            def load_expert(e, s, par_):
                sp.dma_start(wex[:, s, 0:KD * DE], wg_d[e].rearrange("p k f -> p (k f)")).then_inc(w_in[par_], 16)
                sp.dma_start(wex[:, s, KD * DE:GU], wu_d[e].rearrange("p k f -> p (k f)")).then_inc(w_in[par_], 16)
                sp.dma_start(wex[:, s, GU:EXW], wd_d[e].rearrange("p k d -> p (k d)")).then_inc(w_in[par_], 16)

            md = m_dram.rearrange("i a n -> i (a n)")
            for r in (1, 2):
                sp.wait_ge(m_ready, 2 * r)
                for g in range(4):
                    c0 = r * 2048 + g * 512
                    sp.dma_start(md[:, c0:c0 + 512], m_sb[32 * g:32 * g + NC, r, :]).then_inc(m_stored, 16)
            sp.wait_ge(ylru, FW)
            sp.wait_ge(m_stored, 16 * 8)
            sp.dma_start(wout[:, :, :], A["w_out"][0].rearrange("(f p) n -> p f n", p=P)).then_inc(wout_in, 16)
            for s in range(2):
                load_expert(s, s, 0)
            sp.wait_ge(sO_stored, 2)
            sp.wait_ge(state_done, 16 * 8)
            sp.wait_ge(cache_done, 16 * 3)
            for n, i in enumerate((2, 4, 3)):
                sp.dma_start(mod[:, n, :], m_dram[NS:NC, i, :].broadcast_to((P, D))).then_inc(mod_in, 16)
            sp.dma_start(mod[:, 3, :], A["ln1_g"].broadcast_to((P, D))).then_inc(mod_in, 16)
            sp.dma_start(mod[:, 4, :], A["ln1_b"].broadcast_to((P, D))).then_inc(mod_in, 16)
            sp.wait_ge(ss_sum_ps, 1)
            for n, i in enumerate((2, 4, 3, 5)):
                sp.dma_start(smod[:, n, :], m_dram[0:NS, i, :]).then_inc(smod_in, 16)
            sp.wait_ge(O_stored, 2 * TT)
            sp.dma_start(wr[:, :, 0:NG], pair_rows(A["w_group"][0])).then_inc(wr_in, 16)
            for g in range(NG):
                sp.dma_start(wr[:, :, NG + g * EPG:NG + (g + 1) * EPG], pair_rows(A["w_router"][0, g])).then_inc(wr_in, 16)
            load_expert(2, 2, 1)
            sp.wait_ge(slot_ready, TT + 1)
            sp.wait_ge(h2_stored[0], 16 * (TT // 2 + 1))
            sp.wait_ge(h2_stored[1], 16 * (TT // 2))
            load_expert(3, 3, 1)
            for n, a in ((3, "ln2_g"), (4, "ln2_b")):
                sp.dma_start(mod[:, n, :], A[a].broadcast_to((P, D))).then_inc(lnp_in, 16)
            sp.dma_start(mod[:, 0, :], m_dram[NS:NC, 5, :].broadcast_to((P, D))).then_inc(lnp_in, 16)

            sp.wait_ge(w_in[0], 96)
            sp.sem_inc(w_ready, 1)
            sp.wait_ge(steps_ready, 1)

            def load_pair(i, par_):
                last_step = sp.value_load(pend_i[0:1, bass.ds(2 * i + (par_ - 2), 1)], min_val=1, max_val=MAXSTEP)
                sp.wait_ge(y_ps, last_step)
                for q in range(2):
                    e = 4 * i + (2 * par_ + q)
                    s = 2 * par_ + q
                    sp.dma_start(wex[:, s, 0:KD * DE], wg_d[bass.ds(e, 1)].rearrange("a p k f -> p (a k f)")).then_inc(w_in[par_], 16)
                    sp.dma_start(wex[:, s, KD * DE:GU], wu_d[bass.ds(e, 1)].rearrange("a p k f -> p (a k f)")).then_inc(w_in[par_], 16)
                    sp.dma_start(wex[:, s, GU:EXW], wd_d[bass.ds(e, 1)].rearrange("a p k d -> p (a k d)")).then_inc(w_in[par_], 16)
                sp.wait_ge(w_in[1 - par_], 96 * i + 96 * par_)
                sp.sem_inc(w_ready, 1)

            with sp.Fori(1, NPAIR // 2) as i:
                load_pair(i, 0)
                load_pair(i, 1)
            sp.wait_ge(w_in[1], 96 * (NPAIR // 2))
            sp.sem_inc(w_ready, 1)
            sp.wait_ge(experts_done, 1)
            for t, n in TILES:
                for c in range(2):
                    sp.dma_start(yy[0:n, t, c, :], y_dram[c * NT + t * P:c * NT + t * P + n, :]).then_inc(yy_in[t], 16)
            yp = O[0][0].rearrange("(t p) d -> t p d", p=P)
            for t, n in TILES:
                sp.wait_ge(out_ready, t + 1)
                dst = yp[t] if t < TT else O[1].rearrange("b s d -> (b s) d")
                sp.dma_start(dst, yout[0:n, t % 2, :]).then_inc(out_done[t % 2], 16)
            sp.wait_ge(out_done[0], 16 * (TT // 2 + 1))
            sp.wait_ge(out_done[1], 16 * (TT // 2))

        @block.gpsimd
        def _(pool):
            steps = [0]

            def link(ins):
                steps[0] += 1
                ins.then_inc(pool_step, 1)
                pool.wait_ge(pool_step, steps[0])

            def step(ins):
                steps[0] += 1
                ins.then_inc(pool_step, 1)

            step(pool.memset(ident[:, :], 0.0))
            step(pool.memset(cT[:, :, :], 0.0))
            step(pool.memset(b_row[:, :, :], 0.0))
            step(pool.memset(mask[:, :, :], 0.0))
            step(pool.memset(ones[:, :], 1.0))
            step(pool.memset(ones_bf[:, :], 1.0))
            step(pool.memset(tri[:, :], 1.0))
            step(pool.memset(bsel[:, :, :], 1.0))
            step(pool.memset(fill[:, :], NOWHERE))
            step(pool.memset(lg8[:, :], NEG))
            pool.memset(sink_s[:, :], 0.0).then_inc(sink_zero, 1)
            pool.memset(wrg[:, :, :, :], 0.0).then_inc(wrg_zero, 1)
            step(pool.iota(iota_i[:, 0, :], pattern=[[1, NE]], base=0, channel_multiplier=0))
            step(pool.iota(iota_i[:, 1, :].rearrange("p (g e) -> p g e", e=EPG), pattern=[[1, NG], [0, EPG]],
                           base=0, channel_multiplier=0))
            pool.wait_ge(pool_step, steps[0])
            for q in range(2):
                link(pool.iota(row_i[64 * q:64 * q + 64, :], pattern=[[CAP, NSTEP]], base=q * ROWS, channel_multiplier=1))
            for c in range(2):
                step(pool.iota(pair_id[:, :, c, 0], pattern=[[P, TT + 1]], base=0, channel_multiplier=1))
                link(pool.iota(pair_id[:, :, c, 1], pattern=[[P, TT + 1]], base=c * NT, channel_multiplier=1))
            pool.affine_select(out=ident[:, :], in_=ident[:, :], compare_op=ALU.not_equal, fill=1.0, base=0,
                               pattern=[[-1, P]], channel_multiplier=1).then_inc(consts, 1)
            step(pool.affine_select(out=mask[:, 0, :], in_=mask[:, 0, :], compare_op=ALU.is_ge, fill=NEG, base=0,
                                    pattern=[[1, P]], channel_multiplier=-1))
            step(pool.affine_select(out=mask[:, 1, :], in_=mask[:, 1, :], compare_op=ALU.is_ge, fill=NEG, base=0,
                                    pattern=[[-1, P]], channel_multiplier=1))
            step(pool.affine_select(out=tri[:, :], in_=tri[:, :], compare_op=ALU.is_gt, fill=0.0, base=0,
                                    pattern=[[1, P]], channel_multiplier=-1))
            link(pool.affine_select(out=bsel[:, :, :], in_=bsel[:, :, :], compare_op=ALU.is_ge, fill=0.0, base=0,
                                    pattern=[[P, 2], [-32, NS]], channel_multiplier=1))
            step(pool.affine_select(out=bsel[:, :, :], in_=bsel[:, :, :], compare_op=ALU.is_ge, fill=0.0, base=31,
                                    pattern=[[-P, 2], [32, NS]], channel_multiplier=-1))
            step(pool.tensor_copy(iota_e[:, :], iota_i[:, 0, :]))
            step(pool.tensor_copy(row0[:, :], row_i[:, :]))
            pool.wait_ge(pool_step, steps[0])
            pool.tensor_copy(iota_g[:, :], iota_i[:, 1, :]).then_inc(consts, 1)
            pool.dma_start(table.rearrange("(p n) w -> p (n w)", p=P), fill[:, :]).then_inc(tab_init, 16)
            for j in range(4):
                pool.dma_start(b_row[32 * j:32 * j + NC, :, :],
                               A["b_ada"].rearrange("a (r j n) -> a r j n", r=3, j=4)[:, :, j, :].broadcast_to((NC, 3, 512))).then_inc(brow_in, 16)
            pool.wait_ge(wrg_zero, 1)
            for g, a in enumerate(("w_rg_a", "w_rg_x")):
                wv = A[a][0].rearrange("(f n) d e -> n d f e", n=2)
                for n in range(2):
                    pool.dma_start(wrg[64 * n:64 * n + 64, g, :, 64 * n:64 * n + 64], wv[n]).then_inc(wrg_in, 16)
            wa = A["w_ada"][0].rearrange("(p k) n -> p k n", k=KD)
            for j in range(KD, 3 * KD):
                pool.wait_ge(ada_used, j - 3)
                pool.dma_start(ada[:, j % 4, :], wa[:, j % KD, (j // KD) * 2048:(j // KD + 1) * 2048]).then_inc(ada2_in[j % 4], 16)
                if j == 2 * KD:
                    pool.wait_ge(tab_init, 16)
                    pool.wait_ge(cT_ps, 1)
                    pool.memset(kTz[:, :, :, :], 0.0).then_inc(kz_zero, 1)
                    pool.memset(qz[:, :, :], 0.0).then_inc(kz_zero, 1)
            pool.wait_ge(tail_ready, 1)
            rows_ = tails[:, :, :].rearrange("r f p -> r (f p)")
            pool.dma_start(O[2][0, 0], rows_[0:3, :]).then_inc(state_done, 16)
            pool.dma_start(O[6][0, :, CW - 2, :], rows_[3:11, :]).then_inc(state_done, 16)
            pool.dma_start(O[3][0], rows_[11:12, :]).then_inc(state_done, 16)
            pool.dma_start(O[7][0], rows_[12:20, :]).then_inc(state_done, 16)
            pool.wait_ge(vt_ready, 3)
            pool.dma_start(O[4][0, 0].rearrange("w k d -> w (k d)"), klast[:, :]).then_inc(state_done, 16)
            pool.dma_start(O[5][0, 0].rearrange("w k d -> w (k d)"), vtok[:, TT - 1, :]).then_inc(state_done, 16)
            for n in range(2):
                pool.dma_start(O[8 + n][0, :, WIN - 1].rearrange("b k d -> b (k d)"), knv[:, n, :]).then_inc(state_done, 16)
            for b in range(TT):
                keys = slice(0, 2 * P) if b else slice(P, 2 * P)
                pool.wait_ge(rden_ready, b + 1)
                for h in range(NH):
                    pool.tensor_scalar(Pm[b % 2][:, h, keys], Pm[b % 2][:, h, keys], rden[:, b % 2, h:h + 1], None,
                                       ALU.mult).then_inc(P_ready, 1)
            pool.wait_ge(wout_in, 16)
            for f in range(2 * FW):
                pool.tensor_scalar(wout[:, f, :], wout[:, f, :], par[:, 32 + f:33 + f], None, ALU.mult).then_inc(wout_scaled, 1)
            pool.wait_ge(mod_in, 16 * 5)
            pool.wait_ge(tab_init, 16)

            def scatter(t, n):
                pool.wait_ge(slot_ready, t + 1)
                for c in range(2):
                    pool.indirect_dma_start(table[:, :], bass.IndirectOffsetOnAxis(ap=slot[0:n, t, c:c + 1], axis=0),
                                            pair_id[0:n, t, c, :], None, bounds_check=TABROWS - 1,
                                            oob_is_err=False).then_inc(tab_done, 16)

            for t, n in TILES:
                pool.wait_ge(xhat_ready, t + 1)
                link(pool.tensor_tensor(u[0:n, t % 2, :], u[0:n, t % 2, :], mod[0:n, 3, :], ALU.mult))
                pool.tensor_tensor(x_tok[0:n, t, :], u[0:n, t % 2, :], mod[0:n, 4, :], ALU.add).then_inc(x1_ready, 1)
                if t >= 1:
                    scatter(*TILES[t - 1])
            pool.wait_ge(L_ps, TT + 1)
            pool.wait_ge(A_ps, TT)
            pool.memset(X[:, :, :], 0.0).then_inc(X_zero, 1)
            link(pool.iota(sgrid_i[:, :, :], pattern=[[1, NSTEP], [0, NPAIR]], base=0, channel_multiplier=0))
            pool.tensor_copy(sgrid[:, :, :], sgrid_i[:, :, :]).then_inc(grid_ready, 1)
            scatter(*TILES[TT])
            pool.wait_ge(X_zero, 1)
            pool.wait_ge(tab_done, 16 * 2 * (TT + 1))
            pool.wait_ge(h2_stored[0], 16 * (TT // 2 + 1))
            pool.wait_ge(h2_stored[1], 16 * (TT // 2))
            pool.wait_ge(steps_ready, 1)

            def counted(*values):
                values = [v if isinstance(v, int) else pool.to_reg(v) for v in values]
                pool.wait_ge(tab_init, 16)
                return values if len(values) > 1 else values[0]

            def start_gather(par_, i, s, x_free):
                pool.tensor_copy(cur[:, par_:par_ + 1], tabrow[:, bass.ds(s, 1)]).then_inc(idx_cur, 1)
                pool.wait_ge(idx_cur, counted(s + 1))
                pool.indirect_dma_start(idx[:, par_, :], None, table[:, :],
                                        bass.IndirectOffsetOnAxis(ap=cur[:, par_:par_ + 1], axis=0),
                                        bounds_check=TABROWS - 1, oob_is_err=False).then_inc(idx_in[par_], 16)
                if x_free is None:
                    pool.wait_ge(idx_in[par_], 16 * i + 16)
                else:
                    entries, transposed = counted(16 * i + 16, x_free)
                    pool.wait_ge(idx_in[par_], entries)
                    pool.wait_ge(XT_ps, transposed)
                pool.indirect_dma_start(X[:, par_, :], None, h_dram[:, :],
                                        bass.IndirectOffsetOnAxis(ap=idx[:, par_, 0:1], axis=0),
                                        bounds_check=NT - 1, oob_is_err=False).then_inc(X_in[par_], 16)

            def scatter_y(par_, n):
                outputs = counted(n + 1)
                pool.wait_ge(y_v, outputs)
                pool.wait_ge(y_a, outputs)
                pool.indirect_dma_start(y_dram[:, :], bass.IndirectOffsetOnAxis(ap=idx[:, par_, 1:2], axis=0),
                                        yo[:, par_, :], None, bounds_check=2 * NT - 1,
                                        oob_is_err=False).then_inc(y_out[par_], 16)

            def turn(i, peeled):
                if not peeled:
                    pool.wait_ge(y_out[1], 16 * i)
                start_gather(1, i, 2 * i + 1, None if peeled else 4 * i)
                scatter_y(0, 2 * i)
                pool.wait_ge(y_out[0], 16 * i + 16)
                start_gather(0, i + 1, 2 * i + 2, 4 * i + 2)
                scatter_y(1, 2 * i + 1)

            start_gather(0, 0, 0, None)
            turn(0, True)
            with pool.Fori(1, MINTURNS) as i:
                turn(i, False)
            nturns = pool.value_load(turns[0:1, 0:1], min_val=MINTURNS, max_val=TURNS)
            with pool.Fori(MINTURNS, TURNS) as i:
                with pool.If(nturns > i):
                    turn(i, False)
            scattered, gathered = counted(16 * nturns, 16 * nturns + 16)
            pool.wait_ge(y_out[0], scattered)
            pool.wait_ge(y_out[1], scattered)
            pool.wait_ge(X_in[0], gathered)
            pool.memset(mark[:, :], 0.0).then_inc(experts_done, 1)
            for t, n in TILES:
                pool.wait_ge(xhat2_ready, t + 1)
                if t >= 2:
                    pool.wait_ge(out_done[t % 2], 16 * (t // 2))
                pool.tensor_tensor(yout[0:n, t % 2, :], ff[0:n, t % 2, :], mod[0:n, 4, :], ALU.add).then_inc(out_ready, 1)

        @block.scalar
        def _(act):
            steps = [0]

            def link(ins):
                steps[0] += 1
                ins.then_inc(act_step, 1)
                act.wait_ge(act_step, steps[0])

            act.dma_start(prm[0:16, :], A["conv_w"][0].rearrange("k (f p) -> (k f) p", p=P)).then_inc(small_in, 16)
            for n, a in enumerate(("conv_b", "b_rg_a", "b_rg_x", "lru_lambda", "g_lru", "g_attn")):
                v = A[a][0]
                v = v.rearrange("(f n) e -> f (n e)", n=2) if a in ("b_rg_a", "b_rg_x") else v.rearrange("(f p) -> f p", p=P)
                act.dma_start(prm[16 + 4 * n:20 + 4 * n, :], v).then_inc(small_in, 16)
            act.dma_start(stt_in[0:24, :], A["state_conv"][0].rearrange("b k n -> (b k) n")).then_inc(small_in, 16)
            act.dma_start(stt_in[24:32, :], A["state_h"][0]).then_inc(small_in, 16)
            act.dma_start(sinks8[:, 0, :], A["sinks"].broadcast_to((P, NH))).then_inc(small_in, 16)
            act.wait_ge(sink_zero, 1)
            for j in range(4):
                act.dma_start(sink_s[32 * j:32 * j + NH, 0:1], A["sinks"].rearrange("a h -> h a")).then_inc(small_in, 16)
            act.dma_start(kc[:, :, :], A["cache_k"][0].rearrange("b w k d -> w b (k d)")).then_inc(kv_in, 16)
            act.dma_start(vc[:, :, :], A["cache_v"][0].rearrange("b w k d -> w b (k d)")).then_inc(kv_in, 16)
            act.dma_start(brt[0:NG, :], A["b_group"].rearrange("a g -> g a")).then_inc(kv_in, 16)
            act.dma_start(brt[NG:NG + NE, :], A["b_router"][0].rearrange("g (e a) -> (g e) a", a=1)).then_inc(kv_in, 16)
            act.wait_ge(c_in, 32)
            act.activation(csil[:, :], crow[:, :], ACT.Silu).then_inc(csil_ready, 1)
            for n, a in ((8, "cache_k"), (9, "cache_v")):
                act.dma_start(O[n][0, :, 0:WIN - 1].rearrange("b w k d -> b w (k d)"),
                              A[a][0, :, 1:WIN].rearrange("b w k d -> b w (k d)")).then_inc(cache_done, 16)
            act.dma_start(O[6][0, :, 0:CW - 2, :], A["state_conv"][0, :, 1:CW - 1, :]).then_inc(cache_done, 16)
            for k in range(1, KD, 2):
                act.wait_ge(xT_ps, k + 1)
                act.activation(hT[:, k, 0:T], B[k % 4][:, :], ACT.Copy).then_inc(xT_a, 1)
            act.wait_ge(sp_x, 1)
            act.activation(spt[:, 1, :], spt[:, 0, :], ACT.Exp, scale=-1.0).then_inc(sp_exp, 1)
            act.wait_ge(mT_ready, 4)
            act.wait_ge(xT_a, 4)
            for k in range(1, KD, 2):
                act.activation(hT[:, k, 0:T], hT[:, k, 0:T], ACT.Identity, scale=mT[:, 1, k, NS:NC],
                               bias=mT[:, 0, k, NS:NC]).then_inc(h_a, 1)

            def lru_act(f):
                for g, dst in enumerate((tr, ti)):
                    for h in range(2):
                        act.wait_ge(gate_ps, 4 * f + 2 * g + h + 1)
                        if f and g == 0 and h == 0:
                            act.wait_ge(lru_done, f)
                        act.activation(dst[:, h * XH:(h + 1) * XH], B[6 + h][:, 0:XH], ACT.Tanh, scale=0.5,
                                       bias=spt[:, 4 + g, f:f + 1]).then_inc(gate_tanh, 1)
                act.wait_ge(gate_tanh, 4 * (f + 1))
                act.activation(aa[:, :], tr[:, :], ACT.Exp, scale=sp4[:, 1, f:f + 1], bias=sp4[:, 1, f:f + 1]).then_inc(decay_ready, 1)
                act.activation(th[:, :], tr[:, :], ACT.Tanh, scale=sp4[:, 0, f:f + 1], bias=sp4[:, 0, f:f + 1]).then_inc(decay_ready, 1)
                act.wait_ge(bnorm_ready, f + 1)
                act.activation(a2[:, :], a2[:, :], ACT.Sqrt, scale=0.25).then_inc(broot_ready, 1)

            for q, f in enumerate(ORDER):
                b0 = (q % 2) * 2
                if q < FW:
                    act.wait_ge(win_ps, 2 * q + 1)
                    if q >= 2:
                        act.wait_ge(xc_ready, q - 1)
                    act.activation(xb[:, q % 2, CW - 1:CW - 1 + HALF], B[b0][:, 0:HALF], ACT.Copy).then_inc(zin_ready, 1)
                    act.wait_ge(win_ps, 2 * q + 2)
                    act.activation(xb[:, q % 2, CW - 1 + HALF:CW - 1 + T], B[b0 + 1][:, 0:T - HALF], ACT.Copy).then_inc(zin_ready, 1)
                    act.activation(xb[:, q % 2, S0 + CW - 1:CONV:CW], B[b0 + 1][:, T - HALF:NT - HALF], ACT.Copy).then_inc(zin_ready, 1)
                elif q < K_AT:
                    for h, (c0, cn) in enumerate(HALVES):
                        act.wait_ge(win_ps, 2 * q + h + 1)
                        act.activation(qT[:, f - 8, c0:c0 + cn], B[b0 + h][:, 0:cn], ACT.Copy).then_inc(q_ready, 1)
                elif q < GELU_AT:
                    if q == K_AT:
                        act.wait_ge(kz_zero, 2)
                        act.wait_ge(tab_init, 16)
                    for h, (c0, cn) in enumerate(HALVES):
                        act.wait_ge(win_ps, 2 * q + h + 1)
                        if q == K_AT:
                            cp = min(cn, T - c0)
                            for kv in range(NKV):
                                for half in range(2):
                                    act.activation(kTz[64 * half:64 * half + 64, kv, half, c0:c0 + cp],
                                                   B[b0 + h][64 * kv:64 * kv + 64, 0:cp], ACT.Copy)
                        act.activation(kvT[:, q - K_AT, c0:c0 + cn], B[b0 + h][:, 0:cn], ACT.Copy).then_inc(kv_ready, 1)
                else:
                    if q == GELU_AT:
                        act.wait_ge(lru_done, FW)
                    for h, (c0, cn) in enumerate(HALVES):
                        act.wait_ge(win_ps, 2 * q + h + 1)
                        act.activation(gel[:, q - GELU_AT, c0:c0 + cn], B[b0 + h][:, 0:cn], ACT.Gelu_apprx_tanh).then_inc(gelu_ready, 1)
                if 2 <= q < 2 + FW:
                    lru_act(q - 2)

            for n in range(2):
                act.wait_ge(kcT_ps, n + 1)
                act.activation(kbT[:, 4 * n:4 * n + 4, 0:WIN], B[6 + n][:, :].rearrange("p (b w) -> p b w", w=WIN),
                               ACT.Copy).then_inc(kcT_ready, 1)
            act.wait_ge(snb_ready, 1)
            act.activation(sv[:, 3, 0:1], sink_s[:, 0:1], ACT.Exp, bias=sv[:, 2, 0:1]).then_inc(sexp_done, 1)
            act.activation(sv[:, 3, 1:2], sink_s[:, 0:1], ACT.Exp, bias=sv[:, 2, 1:2]).then_inc(sexp_done, 1)
            for n in range(2):
                act.activation(ps[:, n, :], ps[:, n, :], ACT.Exp, scale=SCALE, bias=sv[:, 2, n:n + 1],
                               accum_out=sv[:, 4, n:n + 1]).then_inc(sexp_done, 1)

            def exps(b):
                keys = slice(0, 2 * P) if b else slice(P, 2 * P)
                act.wait_ge(nb_ready, 2 * (b + 1))
                act.activation(es[:, b % 2, :], es[:, b % 2, :], ACT.Exp).then_inc(exp_done, 1)
                for h in range(NH):
                    act.activation(Pm[b % 2][:, h, keys], Pm[b % 2][:, h, keys], ACT.Exp, scale=SCALE,
                                   bias=nb[:, b % 2, h:h + 1], accum_out=sums[:, b % 2, h:h + 1]).then_inc(exp_done, 1)

            def pt_count(b):
                return 0 if b == 0 else 2 + 4 * (b - 1)

            def evacuate_PT(b):
                first = pt_count(b)
                kbs = (0, 1) if b else (1,)
                for n, (kb, kv) in enumerate((kb, kv) for kb in kbs for kv in range(NKV)):
                    act.wait_ge(PT_ps, first + n + 1)
                    if b and n == 0:
                        act.wait_ge(O_ps, b)
                    act.activation(PT[:, kb, kv, :], B[4 + n % 2][:, :], ACT.Copy).then_inc(PT_ready, 1)

            for b in range(TT + 1):
                if b < TT:
                    exps(b)
                if b >= 1:
                    evacuate_PT(b - 1)
            act.wait_ge(ylru, FW)
            for f in range(FW):
                act.activation(sq[:, f, :], yT[:, f, :], ACT.Square).then_inc(sq_ready, 1)
            act.wait_ge(sO_stored, 2)
            act.wait_ge(O_stored, 2 * TT)
            for f in range(FW, 2 * FW):
                act.activation(sq[:, f, :], yT[:, f, :], ACT.Square).then_inc(sq_ready, 1)
            act.wait_ge(ms_ready, 1)
            act.activation(rs[:, :], rs[:, :], ACT.Sqrt).then_inc(rs_ready, 1)

            def mixer_out(t, n):
                act.wait_ge(L_ps, t + 1)
                if t >= 2:
                    act.wait_ge(x1_ready, t - 1)
                for c in range(2):
                    src = B[c][:, :] if t < TT else B[0][32 * c:32 * c + n, :]
                    act.activation(u[0:n, t % 2, c * 512:(c + 1) * 512], src, ACT.Copy, scale=rT[0:n, t, 0:1]).then_inc(L_ready, 1)

            def xhat(t, n):
                act.wait_ge(var_ready, t + 1)
                act.activation(st1[0:n, 1:2], st1[0:n, 0:1], ACT.Sqrt).then_inc(std_ready, 1)
                act.wait_ge(norm_ready, t + 1)
                act.activation(u[0:n, t % 2, :], u[0:n, t % 2, :], ACT.Identity, scale=st1[0:n, 2:3],
                               bias=st1[0:n, 3:4]).then_inc(xhat_ready, 1)

            def after(t, n):
                act.wait_ge(h2_ready, t + 1)
                act.dma_start(h_dram[t * P:t * P + n, :], h2[0:n, t % 2, :]).then_inc(h2_stored[t % 2], 16)
                act.wait_ge(h2T_ps, 2 * t + 2)
                act.activation(h2T[:, 4:8, 0:n], B[5][:, :].rearrange("p (k m) -> p k m", m=P)[:, :, 0:n], ACT.Copy).then_inc(h2T_a, 1)
                act.wait_ge(top_ready, t + 1)
                act.activation(gexp[0:n, :], lg8[0:n, 0:NG], ACT.Exp, bias=rt[0:n, 0:1], accum_out=rt[0:n, 2:3]).then_inc(top_exp, 1)
                act.activation(rt[0:n, 3:4], rt[0:n, 1:2], ACT.Exp).then_inc(top_exp, 1)

            act.wait_ge(rT_ready, 3)
            for i in range(TT + 2):
                if i <= TT:
                    mixer_out(*TILES[i])
                    xhat(*TILES[i])
                if i >= 1:
                    after(*TILES[i - 1])

            def pair(n, par_):
                act.wait_ge(XT_ps, 2 * n + 2)
                act.activation(XT[:, par_, 4:8, :], B[1][:, :].rearrange("p (k m) -> p k m", m=P), ACT.Copy).then_inc(XT_a, 1)
                act.wait_ge(gu_ps, n + 1)
                act.activation(silu_g[:, :], B[2 + par_][:, 0:DE], ACT.Silu).then_inc(silu_done, 1)
                act.wait_ge(zT_ps, n + 1)
                act.activation(zT[:, :, :], B[4][:, 0:2 * P].rearrange("p (k m) -> p k m", m=P), ACT.Copy).then_inc(zT_ready, 1)
                act.wait_ge(y_ps, n + 1)

            def pair_tail(par_):
                act.activation(yo[:, par_, 512:D], B[6][:, :], ACT.Copy).then_inc(y_a, 1)

            def turn(i, peeled):
                for par_ in range(2):
                    pair(2 * i + par_, par_)
                    if not peeled:
                        act.wait_ge(y_out[par_], 16 * i)
                    pair_tail(par_)

            turn(0, True)
            with act.Fori(1, MINTURNS) as i:
                turn(i, False)
            nturns = act.value_load(turns[0:1, 0:1], min_val=MINTURNS, max_val=TURNS)
            with act.Fori(MINTURNS, TURNS) as i:
                with act.If(nturns > i):
                    turn(i, False)

            def std2(t, n):
                act.wait_ge(var_ready, TT + 2 + t)
                act.activation(st1[0:n, 1:2], st1[0:n, 0:1], ACT.Sqrt).then_inc(std_ready, 1)

            for t, n in TILES:
                act.wait_ge(yy_in[t], 32)
                act.activation(yy[0:n, t, 0, :], yy[0:n, t, 0, :], ACT.Copy, scale=wt[0:n, t, 0:1]).then_inc(f_used, 1)
                if t >= 1:
                    std2(*TILES[t - 1])
            std2(*TILES[TT])

        @block.vector
        def _(dve):
            steps = [0]

            def link(ins):
                steps[0] += 1
                ins.then_inc(dve_step, 1)
                dve.wait_ge(dve_step, steps[0])

            def step(ins):
                steps[0] += 1
                ins.then_inc(dve_step, 1)

            def settle():
                dve.wait_ge(dve_step, steps[0])

            dve.wait_ge(cT_ps, 1)
            dve.wait_ge(consts, 2)
            dve.tensor_copy(cT[:, :, 0:NC], B[7][:, 0:KD * 16].rearrange("p (k c) -> p k c", c=16)[:, :, 0:NC]).then_inc(cT_ready, 1)
            for k in range(0, KD, 2):
                dve.wait_ge(xT_ps, k + 1)
                dve.tensor_copy(hT[:, k, 0:T], B[k % 4][:, :]).then_inc(xT_v, 1)
            dve.wait_ge(xs_ps, 1)
            dve.tensor_copy(hT[:, :, T:NT], B[6][:, 0:KD * NS].rearrange("p (k b) -> p k b", b=NS)).then_inc(xT_v, 1)
            dve.wait_ge(small_ps, 1)
            dve.tensor_copy(par[:, :], B[5][:, 0:40]).then_inc(small_ready, 1)
            dve.tensor_copy(stT[:, :, :], B[5][:, 64:64 + FW * 32].rearrange("p (f c) -> p f c", c=32)).then_inc(small_ready, 1)
            dve.wait_ge(small_ready, 2)
            lam = par[:, 28:32]
            link(dve.tensor_scalar(spt[:, 1, :], lam, -1.0, None, ALU.mult))
            dve.tensor_tensor(spt[:, 0, :], spt[:, 1, :], lam, ALU.max).then_inc(sp_x, 1)
            link(dve.tensor_scalar(spt[:, 2, :], lam, -1.0, 0.0, ALU.mult, ALU.max))
            dve.wait_ge(sp_exp, 1)
            link(dve.tensor_scalar(spt[:, 3, :], spt[:, 1, :], 2.0, None, ALU.add))
            link(dve.reciprocal(spt[:, 3, :], spt[:, 3, :]))
            link(dve.tensor_tensor(spt[:, 3, :], spt[:, 3, :], spt[:, 1, :], ALU.mult))
            link(dve.tensor_tensor(spt[:, 1, :], spt[:, 3, :], spt[:, 3, :], ALU.mult))
            link(dve.tensor_scalar(spt[:, 4, :], spt[:, 1, :], 1.0 / 17, 1.0 / 15, ALU.mult, ALU.add))
            for c in (13, 11, 9, 7, 5, 3, 1):
                link(dve.tensor_tensor(spt[:, 4, :], spt[:, 4, :], spt[:, 1, :], ALU.mult))
                link(dve.tensor_scalar(spt[:, 4, :], spt[:, 4, :], 1.0 / c, None, ALU.add))
            link(dve.tensor_tensor(spt[:, 4, :], spt[:, 4, :], spt[:, 3, :], ALU.mult))
            link(dve.scalar_tensor_tensor(out=spt[:, 4, :], in0=spt[:, 4, :], scalar=2.0, in1=spt[:, 2, :], op0=ALU.mult, op1=ALU.add))
            link(dve.tensor_scalar(sp4[:, 0, :], spt[:, 4, :], 4.0, None, ALU.mult))
            link(dve.tensor_scalar(sp4[:, 1, :], spt[:, 4, :], -4.0, None, ALU.mult))
            step(dve.tensor_scalar(spt[:, 4, :], par[:, 20:24], 0.5, None, ALU.mult))
            step(dve.tensor_scalar(spt[:, 5, :], par[:, 24:28], 0.5, None, ALU.mult))
            dve.wait_ge(small_in, 16 * 14)
            step(dve.tensor_scalar(sinks8[:, 1, :], sinks8[:, 0, :], 1.0 / SCALE, None, ALU.mult))
            step(dve.tensor_scalar(sink_s[:, 1:2], sink_s[:, 0:1], 1.0 / SCALE, None, ALU.mult))

            def modulation(r):
                dve.wait_ge(ada_used, KD * (r + 1))
                if r == 0:
                    dve.wait_ge(brow_in, 16 * 4)
                link(dve.tensor_tensor(m_sb[:, r, :], B[4][:, :], b_row[:, r, :], ALU.add))
                plus = {0: (64, 128), 1: (0, 64), 2: (0, 128)}[r]
                for p0 in range(plus[0], plus[1], 64):
                    dve.tensor_scalar(m_sb[p0:p0 + 64, r, :], m_sb[p0:p0 + 64, r, :], 1.0, None, ALU.add).then_inc(m_ready, 1)

            modulation(0)
            for g in range(4):
                if g == 0:
                    dve.wait_ge(mT_ps, 1)
                for kk in range(2):
                    i = dve.tensor_copy(mT[64 * (g % 2):64 * (g % 2) + 64, g // 2, 4 * kk:4 * kk + 4, :],
                                        B[5 + 2 * kk][0:64, :].rearrange("p (k c) -> p k c", c=P)[:, :, 32 * g:32 * g + NC])
                    if kk:
                        i.then_inc(mT_ready, 1)
                    else:
                        step(i)
            dve.wait_ge(mT_ready, 4)
            dve.wait_ge(xT_v, 5)
            for k in range(0, KD, 2):
                dve.tensor_scalar(hT[:, k, 0:T], hT[:, k, 0:T], mT[:, 1, k, NS:NC], mT[:, 0, k, NS:NC], ALU.mult, ALU.add).then_inc(h_v, 1)
            link(dve.tensor_tensor(hT[:, :, T:NT], hT[:, :, T:NT], mT[:, 1, :, 0:NS], ALU.mult))
            dve.tensor_tensor(hT[:, :, T:NT], hT[:, :, T:NT], mT[:, 0, :, 0:NS], ALU.add).then_inc(h_v, 1)
            step(dve.memset(xb[:, :, 0:CW - 1], 0.0))

            def conv(f):
                v = xb[:, f % 2, :]
                o = xc[:, f % 3, :]
                step(dve.tensor_copy(xb[:, f % 2, S0:CONV].rearrange("p (b k) -> p b k", k=CW)[:, :, 0:CW - 1],
                                     stT[:, f, 0:24].rearrange("p (b k) -> p b k", k=CW - 1)))
                dve.wait_ge(zin_ready, 3 * (f + 1))
                settle()
                if f >= 3:
                    dve.wait_ge(gate_ps, 4 * (f - 2))
                step(dve.tensor_copy(tail_in[:, f, 0:3], v[:, T:T + 3]))
                step(dve.tensor_copy(tail_in[:, f, 3:11], v[:, S0 + CW - 1:CONV:CW]))
                link(dve.tensor_scalar(o, v[:, 0:XC], par[:, f:f + 1], par[:, 16 + f:17 + f], ALU.mult, ALU.add))
                for k in range(1, CW):
                    i = dve.scalar_tensor_tensor(out=o, in0=v[:, k:k + XC], scalar=par[:, 4 * k + f:4 * k + f + 1], in1=o,
                                                 op0=ALU.mult, op1=ALU.add)
                    if k < CW - 1:
                        link(i)
                    else:
                        i.then_inc(xc_ready, 1)

            def lru(f):
                o = xc[:, f % 3, :]
                dve.wait_ge(decay_ready, 2 * f + 1)
                link(dve.tensor_tensor(a2[:, :], aa[:, :], aa[:, :], ALU.mult))
                dve.wait_ge(decay_ready, 2 * f + 2)
                link(dve.scalar_tensor_tensor(out=a2[:, :], in0=a2[:, :], scalar=1.0, in1=th[:, :], op0=ALU.add, op1=ALU.mult))
                dve.tensor_scalar(a2[:, :], a2[:, :], 1e-30, None, ALU.max).then_inc(bnorm_ready, 1)
                link(dve.scalar_tensor_tensor(out=ti[:, :], in0=ti[:, :], scalar=1.0, in1=o, op0=ALU.add, op1=ALU.mult))
                dve.wait_ge(broot_ready, f + 1)
                link(dve.tensor_tensor(ti[:, :], ti[:, :], a2[:, :], ALU.mult))
                link(dve.tensor_tensor_scan(yT[:, f, 0:T], aa[:, 0:T], ti[:, 0:T], 0.0, ALU.mult, ALU.add))
                link(dve.tensor_tensor(yT[:, f, T:NT], aa[:, S0:XC:CW], stT[:, f, 24:32], ALU.mult))
                link(dve.tensor_tensor(yT[:, f, T:NT], yT[:, f, T:NT], ti[:, S0:XC:CW], ALU.add))
                dve.tensor_copy(tail_in[:, f, 11:20], yT[:, f, T - 1:NT]).then_inc(lru_done, 1)

            for f in range(FW):
                conv(f)
                if f >= 2:
                    lru(f - 2)
            for f in (2, 3):
                lru(f)
            modulation(1)
            modulation(2)
            for f in range(FW):
                dve.wait_ge(gelu_ready, 2 * (f + 1))
                dve.tensor_tensor(yT[:, f, :], yT[:, f, :], gel[:, f, :], ALU.mult).then_inc(ylru, 1)
            dve.wait_ge(vt_ps, 1)
            dve.tensor_copy(vtok[:, :, :], B[4][:, :].rearrange("p (t d) -> p t d", d=P)).then_inc(vt_ready, 1)
            dve.tensor_copy(klast[:, :], B[5][:, 0:P]).then_inc(vt_ready, 1)
            dve.tensor_copy(knv[:, :, :], B[5][0:NS, P:3 * P].rearrange("p (c d) -> p c d", d=P)).then_inc(vt_ready, 1)
            dve.wait_ge(tail_ps, 1)
            dve.tensor_copy(tails[:, :, :], B[6][0:20, :].rearrange("p (f d) -> p f d", d=P)).then_inc(tail_ready, 1)
            dve.wait_ge(kz_zero, 2)
            dve.wait_ge(q_ready, 2 * FW)
            for kv in range(NKV):
                for half in range(2):
                    dve.tensor_copy(qz[64 * kv:64 * kv + 64, :, kv * G + half:(kv + 1) * G:2].rearrange("p b i -> p i b"),
                                    qT[64 * half:64 * half + 64, 2 * kv:2 * kv + 2, T:NT]).then_inc(qz_ready, 1)
            dve.wait_ge(kv_ready, 2)
            dve.tensor_copy(kbT[:, :, WIN:WIN + 1], kvT[:, 0, T:NT].rearrange("p (b a) -> p b a", a=1)).then_inc(qz_ready, 1)
            dve.wait_ge(ss_ps, 1)
            step(dve.tensor_copy(ps[:, :, :], B[7][:, 0:2 * (WIN + 1)].rearrange("p (n w) -> p n w", w=WIN + 1)))
            link(dve.tensor_reduce(sv[:, 0, :], B[7][:, 0:2 * (WIN + 1)].rearrange("p (n w) -> p n w", w=WIN + 1), AX.X, ALU.max))
            link(dve.tensor_scalar(sv[:, 1, :], sv[:, 0, :], sink_s[:, 1:2], None, ALU.max))
            dve.tensor_scalar(sv[:, 2, :], sv[:, 1, :], -SCALE, None, ALU.mult).then_inc(snb_ready, 1)
            dve.wait_ge(sexp_done, 4)
            link(dve.tensor_tensor(sv[:, 5, :], sv[:, 4, :], sv[:, 3, :], ALU.add))
            link(dve.reciprocal(sv[:, 6, :], sv[:, 5, :]))
            for n in range(2):
                link(dve.tensor_scalar(ps[:, n, :], ps[:, n, :], sv[:, 6, n:n + 1], None, ALU.mult))
                dve.tensor_scalar(pnm[:, n, :], bsel[:, n, :], ps[:, n, WIN:WIN + 1], None, ALU.mult).then_inc(sP_ready, 1)
            dve.wait_ge(sPT_ps, 1)
            dve.tensor_copy(psT[:, :, :], B[6][:, 0:2 * P].rearrange("p (n m) -> p n m", m=P)).then_inc(sPT_ready, 1)
            dve.tensor_copy(pnd[:, :, :], B[5][0:NS, 0:2 * P].rearrange("p (n m) -> p n m", m=P)).then_inc(sPT_ready, 1)

            def mask_rows(b):
                keys = slice(0, 2 * P) if b else slice(P, 2 * P)
                kn = 2 * P if b else P
                if b >= 2:
                    dve.wait_ge(PT_ps, 2 + 4 * (b - 2))
                for h in range(NH):
                    if h % 2 == 0:
                        dve.wait_ge(S_ps, 4 * b + h // 2 + 1)
                    dve.tensor_tensor_reduce(out=Pm[b % 2][:, h, keys], in0=B[h // 2][:, (h % 2) * kn:(h % 2 + 1) * kn],
                                             in1=mask[:, :, :].rearrange("p a k -> p (a k)")[:, keys], scale=1.0, scalar=NEG,
                                             op0=ALU.add, op1=ALU.max, accum_out=mx[:, b % 2, h:h + 1]).then_inc(S_masked, 1)
                dve.wait_ge(S_masked, NH * (b + 1))
                link(dve.tensor_tensor(mx[:, b % 2, :], mx[:, b % 2, :], sinks8[:, 1, :], ALU.max))
                dve.tensor_scalar(nb[:, b % 2, :], mx[:, b % 2, :], -SCALE, None, ALU.mult).then_inc(nb_ready, 1)
                dve.wait_ge(nb_ready, 2 * b + 1)
                dve.tensor_tensor(es[:, b % 2, :], sinks8[:, 0, :], nb[:, b % 2, :], ALU.add).then_inc(nb_ready, 1)

            def denominators(b):
                dve.wait_ge(exp_done, (NH + 1) * (b + 1))
                link(dve.tensor_tensor(sums[:, b % 2, :], sums[:, b % 2, :], es[:, b % 2, :], ALU.add))
                dve.reciprocal(rden[:, b % 2, :], sums[:, b % 2, :]).then_inc(rden_ready, 1)

            def store_O(b):
                dve.wait_ge(O_ps, b + 1)
                for kv in range(NKV):
                    for half in range(2):
                        i = dve.tensor_copy(yT[64 * half:64 * half + 64, FW + 2 * kv:FW + 2 * kv + 2, b * P:(b + 1) * P],
                                            B[6][64 * kv:64 * kv + 64, :].rearrange("p (g q) -> p g q", q=P)[:, half::2, :])
                        if half:
                            i.then_inc(O_stored, 1)
                        else:
                            step(i)

            for b in range(TT + 2):
                if b < TT:
                    mask_rows(b)
                if 1 <= b <= TT:
                    denominators(b - 1)
                if b == 1:
                    dve.wait_ge(sO_ps, 1)
                    for kv in range(NKV):
                        for half in range(2):
                            i = dve.tensor_copy(yT[64 * half:64 * half + 64, FW + 2 * kv:FW + 2 * kv + 2, T:NT].rearrange("p i b -> p b i"),
                                                B[7][64 * kv:64 * kv + 64, 0:NS * 32].rearrange("p (b h) -> p b h", h=32)[:, :, kv * G + half:(kv + 1) * G:2])
                            if half:
                                i.then_inc(sO_stored, 1)
                            else:
                                step(i)
                if b >= 2:
                    store_O(b - 2)
            dve.wait_ge(ss_sum_ps, 1)
            dve.tensor_scalar(rs[:, :], B[4][:, 0:264], 1.0 / W, RMS_EPS, ALU.mult, ALU.add).then_inc(ms_ready, 1)
            dve.wait_ge(rs_ready, 1)
            dve.reciprocal(rs[:, :], rs[:, :]).then_inc(rs_ready, 1)
            dve.wait_ge(rsT_ps, 1)
            for c in range(2):
                dve.tensor_copy(rT[:, 0:TT, :].rearrange("p (h c) g -> p h c g", c=2)[:, :, c, :],
                                B[5][:, c * P:(c + 1) * P].rearrange("p (g h x) -> p h g x", g=2, h=2)[:, :, :, 0]).then_inc(rT_ready, 1)
            dve.tensor_copy(rT[0:NS, TT, :], B[5][0:NS, 2 * P:3 * P].rearrange("p (g h x) -> p g h x", g=2, h=2)[:, :, 1, 0]).then_inc(rT_ready, 1)
            dve.wait_ge(rT_ready, 3)
            dve.wait_ge(mod_in, 16 * 5)

            def layer_norm_stats(src, n, i):
                for c in range(2):
                    step(dve.bn_stats(bn[0:n, c, :], src[:, c * 512:(c + 1) * 512]))
                settle()
                link(dve.bn_aggr(mv[0:n, :], bn[0:n, :, :].rearrange("p a b -> p (a b)")))
                dve.tensor_scalar(st1[0:n, 0:1], mv[0:n, 1:2], LN_EPS, None, ALU.add).then_inc(var_ready, 1)
                dve.wait_ge(std_ready, i + 1)
                link(dve.reciprocal(st1[0:n, 2:3], st1[0:n, 1:2]))
                dve.scalar_tensor_tensor(out=st1[0:n, 3:4], in0=mv[0:n, 0:1], scalar=-1.0, in1=st1[0:n, 2:3],
                                         op0=ALU.mult, op1=ALU.mult).then_inc(norm_ready, 1)

            def residual(t, n):
                gate = mod[:, 0, :] if t < TT else smod[0:NS, 0, :]
                dve.wait_ge(A_ps, min(t + 1, TT))
                dve.wait_ge(L_ready, 2 * (t + 1))
                for c in range(2):
                    src = B[2 + c][:, :] if t < TT else B[0][64 + 32 * c:64 + 32 * c + n, :]
                    dve.scalar_tensor_tensor(out=u[0:n, t % 2, c * 512:(c + 1) * 512], in0=src, scalar=rT[0:n, t, 1:2],
                                             in1=u[0:n, t % 2, c * 512:(c + 1) * 512], op0=ALU.mult, op1=ALU.add).then_inc(A_used, 1)
                dve.wait_ge(A_used, 2 * (t + 1))
                link(dve.tensor_tensor(u[0:n, t % 2, :], u[0:n, t % 2, :], gate, ALU.mult))
                link(dve.scalar_tensor_tensor(out=u[0:n, t % 2, :], in0=x_tok[0:n, t, :], scalar=ALPHA, in1=u[0:n, t % 2, :],
                                              op0=ALU.mult, op1=ALU.add))
                layer_norm_stats(u[0:n, t % 2, :], n, t)

            def modulate2(t, n):
                scale = mod[:, 1, :] if t < TT else smod[0:NS, 1, :]
                shift = mod[:, 2, :] if t < TT else smod[0:NS, 2, :]
                dve.wait_ge(x1_ready, t + 1)
                if t >= 2:
                    dve.wait_ge(h2_stored[t % 2], 16 * (t // 2))
                    dve.wait_ge(h2T_ps, 2 * (t - 1))
                link(dve.tensor_tensor(h2[0:n, t % 2, :], x_tok[0:n, t, :], scale, ALU.mult))
                dve.tensor_tensor(h2[0:n, t % 2, :], h2[0:n, t % 2, :], shift, ALU.add).then_inc(h2_ready, 1)

            def routing(t, n):
                dve.wait_ge(h2T_ps, 2 * t + 1)
                dve.tensor_copy(h2T[:, 0:4, 0:n], B[4][:, :].rearrange("p (k m) -> p k m", m=P)[:, :, 0:n]).then_inc(h2T_v, 1)
                dve.wait_ge(lgT_ps, t + 1)
                dve.tensor_scalar(LGT[:, 0:n], B[6][0:NG + NE, 0:n], brt[:, 0:1], None, ALU.add).then_inc(lgT_ready, 1)
                dve.wait_ge(lg_ps, t + 1)
                step(dve.tensor_copy(lg8[0:n, 0:NG], B[6][0:n, 256:256 + NG]))
                link(dve.tensor_copy(lg[0:n, :], B[6][0:n, 256:256 + NG + NE]))
                link(dve.max(g8[0:n, :], lg8[0:n, :]))
                step(dve.tensor_scalar(rt[0:n, 0:1], g8[0:n, 0:1], -1.0, None, ALU.mult))
                link(dve.max_index(gi[0:n, :], g8[0:n, :], lg8[0:n, :]))
                link(dve.tensor_copy(rt[0:n, 4:5], gi[0:n, 0:1]))
                link(dve.tensor_scalar(le[0:n, :], iota_g[0:n, :], rt[0:n, 4:5], NEG, ALU.not_equal, ALU.mult))
                link(dve.tensor_tensor(le[0:n, :], le[0:n, :], lg[0:n, NG:NG + NE], ALU.add))
                link(dve.max(e8[0:n, :], le[0:n, :]))
                link(dve.max_index(ei[0:n, :], e8[0:n, :], le[0:n, :]))
                dve.tensor_tensor(rt[0:n, 1:2], e8[0:n, 1:2], e8[0:n, 0:1], ALU.subtract).then_inc(top_ready, 1)
                link(dve.tensor_copy(rt[0:n, 6:8], ei[0:n, 0:2]))
                for c in range(2):
                    step(dve.tensor_scalar(oh[0:n, c, :], iota_e[0:n, :], rt[0:n, 6 + c:7 + c], None, ALU.is_equal))
                settle()
                dve.tensor_tensor(hot[0:n, t, :], oh[0:n, 0, :], oh[0:n, 1, :], ALU.add).then_inc(hot_ready, 1)
                dve.wait_ge(top_exp, 2 * (t + 1))
                link(dve.tensor_scalar(rt[0:n, 8:9], rt[0:n, 3:4], 1.0, rt[0:n, 2:3], ALU.add, ALU.mult))
                link(dve.reciprocal(wt[0:n, t, 0:1], rt[0:n, 8:9]))
                step(dve.tensor_tensor(wt[0:n, t, 1:2], wt[0:n, t, 0:1], rt[0:n, 3:4], ALU.mult))
                dve.wait_ge(rank_ps, t + 1)
                for c in range(2):
                    link(dve.tensor_tensor_reduce(out=junk[0:n, :], in0=B[7][0:n, 0:NE], in1=oh[0:n, c, :], scale=1.0, scalar=0.0,
                                                  op0=ALU.mult, op1=ALU.add, accum_out=rt[0:n, 10 + c:11 + c]))
                dve.scalar_tensor_tensor(out=slot[0:n, t, :], in0=rt[0:n, 6:8], scalar=float(ROWS), in1=rt[0:n, 10:12],
                                         op0=ALU.mult, op1=ALU.add).then_inc(slot_ready, 1)

            for i in range(TT + 2):
                if i == TT:
                    dve.wait_ge(smod_in, 64)
                if i <= TT:
                    residual(*TILES[i])
                if i >= 1:
                    routing(*TILES[i - 1])
                if i <= TT:
                    modulate2(*TILES[i])
            dve.wait_ge(count_ps, 1)
            dve.wait_ge(grid_ready, 1)
            link(dve.tensor_reduce(pmax[:, :], B[5][:, 0:NE].rearrange("p (a b) -> p a b", b=2), AX.X, ALU.max))
            link(dve.tensor_scalar(pnum_i[:, 0, :], pmax[:, :], 1.0, float(CAP - 1), ALU.max, ALU.add))
            link(dve.tensor_scalar(pnum_i[:, 1, :], pnum_i[:, 0, :], 6, None, ALU.arith_shift_right))
            link(dve.tensor_copy(pnum[:, :], pnum_i[:, 1, :]))
            link(dve.tensor_tensor_scan(pend[:, :], ones[:, 0:NPAIR], pnum[:, :], 0.0, ALU.mult, ALU.add))
            step(dve.tensor_copy(pend_i[:, :], pend[:, :]))
            link(dve.tensor_tensor(past[:, :, :], sgrid[:, :, :], over_steps(pend), ALU.is_ge))
            link(dve.tensor_reduce(spair[:, 0, :], past[:, :, :], AX.X, ALU.add))
            link(dve.tensor_tensor(past[:, :, :], past[:, :, :], over_steps(pnum), ALU.mult))
            link(dve.tensor_reduce(spair[:, 1, :], past[:, :, :], AX.X, ALU.add))
            link(dve.scalar_tensor_tensor(out=srow[:, :], in0=spair[:, 0, :], scalar=float(2 * ROWS), in1=row0[:, :],
                                          op0=ALU.mult, op1=ALU.add))
            step(dve.scalar_tensor_tensor(out=tabrow[:, :], in0=spair[:, 1, :], scalar=float(-CAP), in1=srow[:, :],
                                          op0=ALU.mult, op1=ALU.add))
            link(dve.tensor_copy(spair_i[:, :], spair[:, 0, :]))
            step(dve.tensor_scalar(place_i[:, :], spair_i[:, :], 1, None, ALU.bitwise_and))
            step(dve.tensor_scalar(wneed[:, :], spair[:, 0, :], float(NPAIR - 1), 1.0, ALU.min, ALU.add))
            link(dve.tensor_scalar(turns[:, 1:2], pend[:, NPAIR - 1:NPAIR], 1.0, None, ALU.add))
            dve.tensor_scalar(turns[:, 0:1], turns[:, 1:2], 1, None, ALU.arith_shift_right).then_inc(steps_ready, 1)
            dve.wait_ge(steps_ready, 1)

            def pair(n, par_, peeled):
                dve.wait_ge(XT_ps, 2 * n + 1)
                dve.tensor_copy(XT[:, par_, 0:4, :], B[0][:, :].rearrange("p (k m) -> p k m", m=P)).then_inc(XT_v, 1)
                dve.wait_ge(silu_done, n + 1)
                if not peeled:
                    dve.wait_ge(zT_ps, n)
                dve.tensor_tensor(z[:, :], silu_g[:, :], B[2 + par_][:, DE:2 * DE], ALU.mult).then_inc(z_ready, 1)
                dve.wait_ge(y_ps, n + 1)

            def turn(i, peeled):
                for par_ in range(2):
                    pair(2 * i + par_, par_, peeled and par_ == 0)
                    if not peeled:
                        dve.wait_ge(y_out[par_], 16 * i)
                    dve.tensor_copy(yo[:, par_, 0:512], B[5][:, :]).then_inc(y_v, 1)

            turn(0, True)
            with dve.Fori(1, MINTURNS) as i:
                turn(i, False)
            nturns = dve.value_load(turns[0:1, 0:1], min_val=MINTURNS, max_val=TURNS)
            with dve.Fori(MINTURNS, TURNS) as i:
                with dve.If(nturns > i):
                    turn(i, False)
            dve.wait_ge(lnp_in, 48)
            for t, n in TILES:
                gate = mod[:, 0, :] if t < TT else smod[0:NS, 3, :]
                dve.wait_ge(f_used, t + 1)
                f = yy[0:n, t, 0, :]
                link(dve.scalar_tensor_tensor(out=f, in0=yy[0:n, t, 1, :], scalar=wt[0:n, t, 1:2], in1=f, op0=ALU.mult, op1=ALU.add))
                link(dve.tensor_tensor(f, f, gate, ALU.mult))
                link(dve.scalar_tensor_tensor(out=f, in0=x_tok[0:n, t, :], scalar=ALPHA, in1=f, op0=ALU.mult, op1=ALU.add))
                layer_norm_stats(f, n, TT + 1 + t)
                dve.wait_ge(norm_ready, TT + 2 + t)
                link(dve.tensor_scalar(f, f, st1[0:n, 2:3], st1[0:n, 3:4], ALU.mult, ALU.add))
                if t >= 2:
                    dve.wait_ge(out_ready, t - 1)
                dve.tensor_tensor(ff[0:n, t % 2, :], f, mod[0:n, 3, :], ALU.mult).then_inc(xhat2_ready, 1)

        @block.tensor
        def _(pe):
            pe.wait_ge(consts, 1)
            pe.wait_ge(csil_ready, 1)
            for k in range(KD):
                last = pe.transpose(B[7][:, 16 * k:16 * k + NC], csil[:, k::KD], ident[0:NC, 0:NC])
            last.then_inc(cT_ps, 1)
            pe.wait_ge(x_in, 32)
            for k in range(KD):
                if k >= 4:
                    if k % 2:
                        pe.wait_ge(xT_a, (k - 4) // 2 + 1)
                    else:
                        pe.wait_ge(xT_v, (k - 4) // 2 + 1)
                for t in range(TT):
                    last = pe.transpose(B[k % 4][:, t * P:(t + 1) * P], x_tok[:, t, k::KD], ident[:, :])
                last.then_inc(xT_ps, 1)
            for k in range(KD):
                last = pe.transpose(B[6][:, NS * k:NS * k + NS], x_tok[0:NS, TT, k::KD], ident[0:NS, 0:NS])
            last.then_inc(xs_ps, 1)
            pe.wait_ge(small_in, 16 * 14)
            pe.transpose(B[5][:, 0:40], prm[:, :], ident[0:40, 0:40])
            for f in range(FW):
                last = pe.transpose(B[5][:, 64 + 32 * f:96 + 32 * f], stt_in[:, f * P:(f + 1) * P], ident[0:32, 0:32])
            last.then_inc(small_ps, 1)

            def modulation(r):
                if r:
                    pe.wait_ge(m_ready, r)
                for k in range(KD):
                    j = r * KD + k
                    if r:
                        pe.wait_ge(ada2_in[j % 4], 16 * ((j - KD) // 4 + 1))
                    else:
                        pe.wait_ge(ada_in[j % 4], 16 * (j // 4 + 1))
                    for g in range(4):
                        last = pe.matmul(B[4][32 * g:32 * g + 32, :], cT[:, k, :], ada[:, j % 4, g * 512:(g + 1) * 512],
                                         start=(k == 0), stop=(k == KD - 1))
                    last.then_inc(ada_used, 1)

            pe.wait_ge(cT_ready, 1)
            modulation(0)
            pe.wait_ge(m_ready, 1)
            pe.wait_ge(small_ready, 2)
            for k in range(KD):
                last = pe.transpose(B[5 + 2 * (k // 4)][0:64, (k % 4) * P:(k % 4 + 1) * P], m_sb[:, 0, k::KD], ident[:, :])
            last.then_inc(mT_ps, 1)

            def evacuated(q):
                if q < FW:
                    pe.wait_ge(zin_ready, 3 * (q + 1))
                elif q < K_AT:
                    pe.wait_ge(q_ready, 2 * (q - FW + 1))
                elif q < GELU_AT:
                    pe.wait_ge(kv_ready, 2 * (q - K_AT + 1))
                else:
                    pe.wait_ge(gelu_ready, 2 * (q - GELU_AT + 1))

            def project_in(q):
                n = WCH.index(ORDER[q] // 2)
                pe.wait_ge(win_in[n % 3], 16 * (n // 3 + 1))
                if q >= 2:
                    evacuated(q - 2)
                col = (ORDER[q] % 2) * P
                for h, (c0, cn) in enumerate(HALVES):
                    for k in range(KD):
                        if q == 0 and h == 0:
                            if k % 2:
                                pe.wait_ge(h_a, k // 2 + 1)
                            else:
                                pe.wait_ge(h_v, k // 2 + 1)
                        if q == 0 and h == 1 and k == 0:
                            pe.wait_ge(h_v, 5)
                        last = pe.matmul(B[(q % 2) * 2 + h][:, 0:cn], win[:, n % 3, k, col:col + P], hT[:, k, c0:c0 + cn],
                                         start=(k == 0), stop=(k == KD - 1))
                    last.then_inc(win_ps, 1)

            def lru_gates(f):
                pe.wait_ge(xc_ready, f + 1)
                if f == 0:
                    pe.wait_ge(kv_in, 16 * 4)
                    pe.wait_ge(wrg_in, 16 * 4)
                    pe.wait_ge(mT_ready, 4)
                for g in range(2):
                    for h in range(2):
                        if 2 * f + g:
                            pe.wait_ge(gate_tanh, 4 * f + 2 * (g - 1) + h + 1)
                        pe.matmul(B[6 + h][:, 0:XH], wrg[:, g, f, :], xc[:, f % 3, h * XH:(h + 1) * XH],
                                  start=True, stop=True).then_inc(gate_ps, 1)

            for q in range(len(ORDER)):
                project_in(q)
                if 2 <= q < 2 + FW:
                    lru_gates(q - 2)
                if q == 5:
                    modulation(1)
                if q == 9:
                    modulation(2)

            pe.wait_ge(kv_ready, 4)
            pe.wait_ge(m_ready, 4)
            for t in range(TT):
                pe.transpose(B[4][:, t * P:(t + 1) * P], kvT[:, 1, t * P:(t + 1) * P], ident[:, :])
            pe.transpose(B[5][:, 0:P], kvT[:, 0, T - P:T], ident[:, :])
            for n in range(2):
                last = pe.transpose(B[5][0:NS, (1 + n) * P:(2 + n) * P], kvT[:, n, T:NT], ident[:, :])
            last.then_inc(vt_ps, 1)
            pe.wait_ge(lru_done, FW)
            pe.wait_ge(gate_tanh, 4 * FW)
            for f in range(FW):
                last = pe.transpose(B[6][0:20, f * P:(f + 1) * P], tail_in[:, f, :], ident[:, :])
            last.then_inc(tail_ps, 1)
            for b in range(NS):
                if b == 4:
                    pe.wait_ge(gate_tanh, 4 * FW)
                if b == 0:
                    pe.wait_ge(tail_ready, 1)
                last = pe.transpose(B[6 + b // 4][:, (b % 4) * P:(b % 4 + 1) * P], kc[:, b, :], ident[:, :])
                if b % 4 == 3:
                    last.then_inc(kcT_ps, 1)
            pe.wait_ge(kcT_ready, 2)
            pe.wait_ge(qz_ready, 5)
            for b in range(NS):
                j = b % 4
                c0 = (b // 4) * (WIN + 1)
                last = pe.matmul(B[7][32 * j:32 * j + 32, c0:c0 + WIN + 1], qz[:, b, :], kbT[:, b, :], start=True, stop=True)
            last.then_inc(ss_ps, 1)

            def scores(b):
                k0 = max(0, b - 1) * P
                kn = (b + 1) * P - k0
                for p in range(NH // 2):
                    if b:
                        pe.wait_ge(S_masked, NH * (b - 1) + 2 * p + 2)
                    pe.matmul(B[p][:, 0:2 * kn], qT[:, p, b * P:(b + 1) * P], kTz[:, p // 2, :, k0:k0 + kn],
                              start=True, stop=True).then_inc(S_ps, 1)

            def pt_count(b):
                return 0 if b == 0 else 2 + 4 * (b - 1)

            def weigh(b):
                first = pt_count(b)
                kbs = (0, 1) if b else (1,)
                n = 0
                for kb in kbs:
                    for kv in range(NKV):
                        pe.wait_ge(P_ready, NH * b + G * (kv + 1))
                        if first + n >= 2:
                            pe.wait_ge(PT_ready, first + n - 1)
                        for g in range(G):
                            last = pe.transpose(B[4 + n % 2][:, g * P:(g + 1) * P],
                                                Pm[b % 2][:, kv * G + g, kb * P:(kb + 1) * P], ident[:, :])
                        last.then_inc(PT_ps, 1)
                        n += 1
                if b:
                    pe.wait_ge(O_stored, 2 * b)
                pe.wait_ge(PT_ready, first + n)
                for kb in kbs:
                    for kv in range(NKV):
                        last = pe.matmul(B[6][64 * kv:64 * kv + 64, :], vtok[:, b - 1 + kb, 64 * kv:64 * kv + 64],
                                         PT[:, kb, kv, :], start=(kb == kbs[0]), stop=(kb == 1))
                last.then_inc(O_ps, 1)

            evacuated(GELU_AT + 2)
            evacuated(GELU_AT + 3)
            scores(0)
            pe.wait_ge(sP_ready, 2)
            for n in range(2):
                pe.transpose(B[6][:, n * P:(n + 1) * P], ps[:, n, 0:WIN], ident[:, :])
            for n in range(2):
                last = pe.transpose(B[5][0:NS, n * P:(n + 1) * P], pnm[:, n, :], ident[:, :])
            last.then_inc(sPT_ps, 1)
            pe.wait_ge(sPT_ready, 2)
            for b in range(NS):
                pe.matmul(B[7][:, 32 * b:32 * b + 32], knv[:, 1, :], pnd[:, b // 4, 32 * (b % 4):32 * (b % 4) + 32], start=True, stop=False)
                last = pe.matmul(B[7][:, 32 * b:32 * b + 32], vc[:, b, :], psT[:, b // 4, 32 * (b % 4):32 * (b % 4) + 32],
                                 start=False, stop=True)
            last.then_inc(sO_ps, 1)
            for b in range(1, TT + 1):
                if b < TT:
                    scores(b)
                weigh(b - 1)

            pe.wait_ge(PT_ready, pt_count(TT))
            for f in range(FW):
                for g in range(2):
                    pe.wait_ge(sq_ready, 4 * g + f + 1 if g == 0 else 2 * FW)
                    for h in range(2):
                        j = 2 * g + h
                        last = pe.matmul(B[4][32 * j:32 * j + 32, 0:264], ones[:, :], sq[:, 4 * g + f, h * HALF:h * HALF + 264],
                                         start=(f == 0), stop=(f == FW - 1))
            last.then_inc(ss_sum_ps, 1)
            pe.wait_ge(rs_ready, 2)
            for c in range(2):
                pe.transpose(B[5][:, c * P:(c + 1) * P], rs[:, c * P:(c + 1) * P], ident[:, :])
            pe.transpose(B[5][0:NS, 2 * P:3 * P], rs[:, 2 * P:2 * P + NS], ident[:, :]).then_inc(rsT_ps, 1)

            def project_out(t, n):
                if t == 0:
                    pe.wait_ge(wout_scaled, 2 * FW)
                if t < TT:
                    for g in range(2):
                        if t:
                            pe.wait_ge(A_used if g else L_ready, 2 * t)
                        for f in range(FW):
                            for c in range(2):
                                last = pe.matmul(B[2 * g + c][:, :], yT[:, FW * g + f, t * P:(t + 1) * P],
                                                 wout[:, FW * g + f, c * 512:(c + 1) * 512], start=(f == 0), stop=(f == FW - 1))
                        last.then_inc(A_ps if g else L_ps, 1)
                else:
                    pe.wait_ge(L_ready, 2 * t)
                    for f in range(FW):
                        for g in range(2):
                            for c in range(2):
                                j = 2 * g + c
                                last = pe.matmul(B[0][32 * j:32 * j + n, :], yT[:, FW * g + f, T:NT],
                                                 wout[:, FW * g + f, c * 512:(c + 1) * 512], start=(f == 0), stop=(f == FW - 1))
                    last.then_inc(L_ps, 1)

            def route(t, n):
                pe.wait_ge(h2_ready, t + 1)
                if t == 0:
                    pe.wait_ge(rT_ready, 3)
                else:
                    pe.wait_ge(h2T_v, t)
                    pe.wait_ge(h2T_a, t)
                for k in range(KD):
                    last = pe.transpose(B[4 + k // 4][:, (k % 4) * P:(k % 4) * P + n], h2[0:n, t % 2, k::KD], ident[0:n, 0:n])
                    if k % 4 == 3:
                        last.then_inc(h2T_ps, 1)
                if t == 0:
                    pe.wait_ge(wr_in, 16 * 5)
                    pe.wait_ge(O_stored, 2 * TT)
                else:
                    pe.wait_ge(top_ready, t)
                pe.wait_ge(h2T_v, t + 1)
                pe.wait_ge(h2T_a, t + 1)
                for k in range(KD):
                    last = pe.matmul(B[6][0:NG + NE, 0:n], wr[:, k, :], h2T[:, k, 0:n], start=(k == 0), stop=(k == KD - 1))
                last.then_inc(lgT_ps, 1)
                pe.wait_ge(lgT_ready, t + 1)
                pe.transpose(B[6][0:n, 256:256 + NG + NE], LGT[:, 0:n], ident[0:NG + NE, 0:NG + NE]).then_inc(lg_ps, 1)
                pe.wait_ge(hot_ready, t + 1)
                if t:
                    pe.wait_ge(slot_ready, t)
                else:
                    pe.wait_ge(sO_stored, 2)
                for t2 in range(t):
                    pe.matmul(B[7][0:n, 0:NE], ones_bf[:, 0:n], hot[:, t2, :], start=(t2 == 0), stop=False)
                pe.matmul(B[7][0:n, 0:NE], tri[0:n, 0:n], hot[0:n, t, :], start=(t == 0), stop=True).then_inc(rank_ps, 1)

            for i in range(TT + 2):
                if i <= TT:
                    project_out(*TILES[i])
                if i >= 1:
                    route(*TILES[i - 1])
            for t, n in TILES:
                last = pe.matmul(B[5][:, 0:NE], ones_bf[0:n, :], hot[0:n, t, :], start=(t == 0), stop=(t == TT))
            last.then_inc(count_ps, 1)

            def pair(i, par_, peeled):
                n = 2 * i + par_
                place = pe.value_load(place_i[0:1, bass.ds(n, 1)], min_val=0, max_val=1)
                need = pe.value_load(wneed[0:1, bass.ds(n, 1)], min_val=1, max_val=NPAIR)
                pe.wait_ge(X_in[par_], 16 * i + 16)
                if not (peeled and par_ == 0):
                    pe.wait_ge(XT_v, n)
                    pe.wait_ge(XT_a, n)
                for k in range(KD):
                    last = pe.transpose(B[k // 4][:, (k % 4) * P:(k % 4 + 1) * P], X[:, par_, k::KD], ident[:, :])
                    if k % 4 == 3:
                        last.then_inc(XT_ps, 1)
                pe.wait_ge(w_ready, need)
                pe.wait_ge(XT_v, n + 1)
                pe.wait_ge(XT_a, n + 1)
                for pl in range(2):
                    with pe.If(place > 0 if pl else place < 1):
                        for k in range(KD):
                            for q in range(2):
                                gu = wex[:, 2 * pl + q, 0:GU].rearrange("p (c k f) -> p c k f", c=2, k=KD)
                                last = pe.matmul(B[2 + par_][64 * q:64 * q + 64, :], XT[:, par_, k, 64 * q:64 * q + 64],
                                                 gu[:, :, k, :], start=(k == 0), stop=(k == KD - 1))
                        last.then_inc(gu_ps, 1)
                pe.wait_ge(z_ready, n + 1)
                for k in range(2):
                    last = pe.transpose(B[4][:, k * P:(k + 1) * P], z[:, k::2], ident[:, :])
                last.then_inc(zT_ps, 1)
                pe.wait_ge(zT_ready, n + 1)
                if not (peeled and par_ == 0):
                    pe.wait_ge(y_v, n)
                    pe.wait_ge(y_a, n)
                for pl in range(2):
                    with pe.If(place > 0 if pl else place < 1):
                        for k in range(2):
                            for c in range(2):
                                for q in range(2):
                                    dn = GU + k * D + c * 512
                                    last = pe.matmul(B[5 + c][64 * q:64 * q + 64, :], zT[:, k, 64 * q:64 * q + 64],
                                                     wex[:, 2 * pl + q, dn:dn + 512], start=(k == 0), stop=(k == 1))
                        last.then_inc(y_ps, 1)

            def turn(i, peeled):
                pair(i, 0, peeled)
                pair(i, 1, peeled)

            pe.wait_ge(steps_ready, 1)
            turn(0, True)
            with pe.Fori(1, MINTURNS) as i:
                turn(i, False)
            nturns = pe.value_load(turns[0:1, 0:1], min_val=MINTURNS, max_val=TURNS)
            with pe.Fori(MINTURNS, TURNS) as i:
                with pe.If(nturns > i):
                    turn(i, False)


_INS = ["x_prompt", "x_sample", "c_prompt", "c_sample", "state_conv", "state_h", "cache_k", "cache_v", "w_ada", "b_ada",
        "w_in", "conv_w", "conv_b", "w_rg_a", "b_rg_a", "w_rg_x", "b_rg_x", "lru_lambda", "sinks", "g_lru", "g_attn",
        "w_out", "ln1_g", "ln1_b", "w_group", "b_group", "w_router", "b_router", "w_gate", "w_up", "w_down",
        "ln2_g", "ln2_b"]
_OUTS = [(1, T, D), (NS, 1, D), (1, 1, CW - 1, W), (1, 1, W), (1, 1, WIN, NKV, HD), (1, 1, WIN, NKV, HD),
         (1, NS, CW - 1, W), (1, NS, W), (1, NS, WIN, NKV, HD), (1, NS, WIN, NKV, HD)]


def kernel(**inputs):
    import numpy as np
    import concourse.bacc as bacc
    from concourse.bass_utils import run_bass_kernel_spmd

    nc = bacc.Bacc("TRN2", target_bir_lowering=False, num_devices=1)
    arrays, A, O = {}, {}, []
    for name in _INS:
        a = np.ascontiguousarray(inputs[name])
        arrays[f"in_{name}"] = a
        A[name] = nc.dram_tensor(f"in_{name}", a.shape, mybir.dt.from_np(a.dtype), kind="ExternalInput").ap()
    for i, shape in enumerate(_OUTS):
        O.append(nc.dram_tensor(f"out_{i}", shape, F32, kind="ExternalOutput").ap())
    build(nc, A, O)
    r = run_bass_kernel_spmd(nc, [arrays], core_ids=[0])
    return tuple(r.results[0][f"out_{i}"] for i in range(len(_OUTS)))
```

```python
import concourse.bass as bass
from concourse import mybir
from contextlib import ExitStack

F32 = mybir.dt.float32
BF16 = mybir.dt.bfloat16
I32 = mybir.dt.int32
U32 = mybir.dt.uint32
ALU = mybir.AluOpType
ACT = mybir.ActivationFunctionType
AX = mybir.AxisListType

P = 128
D = 1024
KD = D // P
T = 512
NS = 8
NT = T + NS
TT = T // P
HALF = 256
NC = NS + 1
W = 512
FW = W // P
INW = 1792
CW = 4
LB = 64
NH, NKV, HD = 8, 2, 64
G = NH // NKV
WIN = 128
NG, EPG, NE = 4, 8, 32
DE = 256
CAP = 64
NPAIR = NE // 2
MAXSTEP = (2 * NT + (CAP - 1) * NPAIR) // CAP
RING = 4
AHEAD = RING - 1
TURNS = (MAXSTEP + RING - 1) // RING
MINTURNS = NPAIR // RING
NSTEP = RING * TURNS + RING
ALPHA = 2.0 ** 0.25
LN_EPS = 1e-5
RMS_EPS = 1e-6
SCALE = HD ** -0.5
NEG = -1e30
NOWHERE = 1 << 20
CONV = T + CW - 1 + NS * CW
XC = CONV - (CW - 1)
S0 = T + CW - 1
XH = XC // 2


def build(nc, A, O):
    ctx = ExitStack()
    with ctx:
        base = (nc.sbuf_base + 63) // 64 * 64
        size = {"y": 16640, "w": 32768, "x": 20480, "h": 16640, "m": 20480, "r": 98304}
        at, here = {}, base
        for k, v in size.items():
            at[k] = here
            here += v
        small_at = [here]

        def place(name, shape, off, dt=F32):
            return nc.alloc_sbuf_tensor_at(name, shape, dt, offset=off)

        def row(name, shape, region, off, dt=F32):
            return place(name, shape, at[region] + off, dt)

        def small(name, shape, dt=F32):
            n = 1
            for s in shape[1:]:
                n *= s
            n *= 2 if dt == BF16 else 4
            t = place(name, shape, small_at[0], dt)
            small_at[0] += (n + 31) // 32 * 32
            assert small_at[0] <= nc.sbuf_usable_end, small_at
            return t

        late_at = [27648]

        def late(name, shape, dt=F32):
            n = 4
            for d in shape[1:]:
                n *= d
            t = row(name, shape, "w", late_at[0], dt)
            late_at[0] += (n + 31) // 32 * 32
            assert late_at[0] <= size["w"]
            return t

        x_tok = row("x_tok", [P, TT + 1, D], "x", 0)
        hT = row("hT", [P, KD, NT], "h", 0)
        yT = row("yT", [P, 2 * FW, NT], "y", 0)
        xb = row("xb", [P, 2, CONV], "w", 0)
        xc = row("xc", [P, 3, XC], "w", 4384)
        tr = row("tr", [P, XC], "w", 10912)
        ti = row("ti", [P, XC], "w", 13088)
        aa = row("aa", [P, XC], "w", 15264)
        th = row("th", [P, XC], "w", 17440)
        a2 = row("a2", [P, XC], "w", 19616)
        wrg = row("wrg", [P, 2, FW, P], "w", 21792)
        m_sb = row("m_sb", [P, 2, 512], "w", 25888)
        gel = row("gel", [P, FW, NT], "w", 0)
        wout = row("wout", [P, KD, D], "w", 0)
        X = row("X", [P, RING, D], "w", 0)
        XT = row("XT", [P, 2, KD, P], "w", 16384)
        silu_g = row("silu_g", [P, DE], "w", 24576)
        z = row("z", [P, DE], "w", 25600)
        zT = row("zT", [P, 2, P], "w", 26624)
        yo = row("yo", [P, RING, D], "y", 0)
        kc = row("kc", [P, NS, P], "m", 0)
        kbT = row("kbT", [P, NS, WIN + 1], "m", 4096)
        vc = row("vc", [P, NS, P], "m", 8224)
        ps = row("ps", [P, 2, WIN + 1], "m", 12320)
        psT = row("psT", [P, 2, P], "m", 13376)
        qz = row("qz", [P, NS, 32], "m", 14400)
        pnd = row("pnd", [NS, 2, P], "m", 15424)
        pnm = row("pnm", [P, 2, NS], "m", 16448)
        knv = row("knv", [NS, 2, P], "m", 16512)
        klast = row("klast", [P, P], "m", 17536)
        tails = row("tails", [20, FW, P], "m", 18048)
        mod = row("mod", [P, 5, D], "m", 0)
        sq = row("sq", [P, 2 * FW, NT], "h", 0)
        smod = row("smod", [NS, 4, D], "h", 0)
        ada = row("ada", [P, 4, 2048], "r", 0)
        win = row("win", [P, 3, KD, 256], "r", 32768)
        crow = row("crow", [NC, D], "r", 57344)
        csil = row("csil", [NC, D], "r", 61440)
        fill = row("fill", [P, 2 * NSTEP], "r", 65536, I32)
        prm = row("prm", [40, P], "r", 66784)
        stt_in = row("stt_in", [32, W], "r", 67296)
        b_row = row("b_row", [P, 2, 512], "y", 4 * NT * 4)
        m_sb2 = row("m_sb2", [P, 512], "r", 32768)
        b_row2 = row("b_row2", [P, 512], "r", 34816)
        cT = row("cT", [P, KD, 32], "r", 96448)
        mT = row("mT", [P, 2, KD, NC], "r", 97472)
        qT = row("qT", [P, FW, NT], "r", 71744)
        kTz = row("kTz", [P, NKV, 2, T], "r", 57344)
        vtok = row("vtok", [P, TT, P], "r", 65536)
        kvT = row("kvT", [P, 2, NT], "r", 67584)
        PT = row("PT", [P, 2, NKV, G * P], "r", 80064)
        Pm = [row("P0", [P, NH, 2 * P], "r", 88256), row("P1", [P, NH, 2 * P], "h", 4 * NT * 4),
              row("P2", [P, NH, 2 * P], "r", 49152)]
        u = row("u", [P, 2, D], "r", 73728)
        h2 = row("h2", [P, 2, D], "r", 81920)
        h2T = row("h2T", [P, KD, NT], "r", 49152)
        wr = row("wr", [P, KD, NG + NE], "r", 94208)
        LGT = row("LGT", [NG + NE, NT], "r", 90112)
        rs = row("rs", [P, 264], "r", 96448)
        gb = row("gb", [P, D], "r", 67584)
        EXW = 2 * KD * DE + 2 * D
        GU = 2 * KD * DE
        SETS = 3
        wex = [row("wex0", [P, 2, EXW], "r", 0), row("wex1", [P, 2, EXW], "r", 8 * EXW), row("wex2", [P, 2, EXW], "x", 0)]
        yy = row("yy", [P, TT + 1, 2, D], "r", 0)
        wdiag = row("wdiag", [P, TT + 1, 2, P], "r", 65536)
        yout = row("yout", [P, 2, D], "w", 0)

        ident = small("ident", [P, P])
        mask = small("mask", [P, 2, P])
        tri = small("tri", [P, P], BF16)
        ones_bf = small("ones_bf", [P, P], BF16)
        ones = small("ones", [P, 32])
        iota_e = small("iota_e", [P, NE])
        iota_i = small("iota_i", [P, NE], I32)
        pair_id = small("pair_id", [P, TT + 1, 2, 2], I32)
        bsel = small("bsel", [P, 2, NS])
        par = small("par", [P, 40])
        stT = small("stT", [P, FW, 32])
        sp4 = small("sp4", [P, 2, FW])
        spt = small("spt", [P, 6, FW])
        tail_in = small("tail_in", [P, FW, 20])
        sinks8 = small("sinks8", [P, 2, NH])
        sink_s = small("sink_s", [P, 2])
        mx = small("mx", [P, 2, NH])
        nb = small("nb", [P, 2, NH])
        es = small("es", [P, 2, NH])
        sums = small("sums", [P, 2, NH])
        rden = small("rden", [P, 2, NH])
        sv = small("sv", [P, 8, 2])
        rT = small("rT", [P, TT + 1, 2])
        brt = small("brt", [NG + NE, 1])
        bn = small("bn", [P, 2, 6])
        mv = small("mv", [P, 2])
        st1 = small("st1", [P, 4])
        hot = small("hot", [P, TT + 1, NE], BF16)
        wt = small("wt", [P, TT + 1, 2])
        oh = small("oh", [P, TT + 1, 2, NE])
        rank = small("rank", [P, TT + 1, 2])
        slot = small("slot", [P, TT + 1, 2], U32)
        pmax = late("pmax", [P, NPAIR])
        pnum_i = late("pnum_i", [P, 2, NPAIR], I32)
        pnum = late("pnum", [P, NPAIR])
        pend = late("pend", [P, NPAIR])
        pend_i = late("pend_i", [P, NPAIR], I32)
        pbase = late("pbase", [P, NPAIR, 2])
        base_of = late("base_of", [P, TT + 1, 2])
        sgrid_i = row("sgrid_i", [P, NSTEP, NPAIR], "y", 0, I32)
        sgrid = row("sgrid", [P, NSTEP, NPAIR], "y", 4096)
        past = row("past", [P, NSTEP, NPAIR], "y", 8192)
        ohb = row("ohb", [P, (TT + 1) * 2, NE], "y", 10496)
        LG = row("LG", [P, TT + 1, NG + NE], "y", 11776)
        le = row("le", [P, TT + 1, NE], "y", 12512)
        cand = row("cand", [P, TT + 1, NE], "y", 13152)
        eq = row("eq", [P, TT + 1, NE], "y", 13792)
        gt = row("gt", [P, 4, TT + 1, NG], "y", 14432)
        col = late("col", [P, 8, TT + 1])
        rk = late("rk", [P, (TT + 1) * 2, NE])
        spair = late("spair", [P, NSTEP])
        rank_i = late("rank_i", [P, 2, TT + 1, 2], I32)
        third = late("third", [P, NSTEP], I32)
        place_i = late("place_i", [P, NSTEP], I32)
        wneed = late("wneed", [P, 2, NSTEP], I32)
        turns = late("turns", [P, 2], I32)
        idx_all = late("idx_all", [P, NSTEP, 2], I32)
        gidx = late("gidx", [P, RING], I32)
        sidx = late("sidx", [P, RING], I32)
        mark = small("mark", [P, 1])

        B = [ctx.enter_context(nc.psum_tensor(f"B{i}", [P, 512], F32)) for i in range(8)]

        m_dram = nc.dram_tensor("m_dram", (NC, 6, D), F32).ap()
        h_dram = nc.dram_tensor("h_dram", (NT, D), F32).ap()
        x1_dram = nc.dram_tensor("x1_dram", (NT, D), F32).ap()
        y_dram = nc.dram_tensor("y_dram", (2 * NT, D), F32).ap()
        table = nc.dram_tensor("table", (2 * NSTEP * CAP, 2), I32).ap()

        def sem(name):
            return ctx.enter_context(nc.semaphore(name))

        c_in, x_in, small_in, kv_in, brow_in, wrg_in = (sem(n) for n in ("c_in", "x_in", "small_in", "kv_in", "brow_in", "wrg_in"))
        ada_in = [sem(f"ada_in{i}") for i in range(4)]
        ada2_in = [sem(f"ada2_in{i}") for i in range(4)]
        win_in = [sem(f"win_in{i}") for i in range(3)]
        wout_in, mod_in, smod_in, lnp_in, wr_in = (sem(n) for n in ("wout_in", "mod_in", "smod_in", "lnp_in", "wr_in"))
        w_in = [sem(f"w_in{i}") for i in range(SETS)]
        down_in = ada_in[:SETS]
        consts, kz_zero = sem("consts"), sem("kz_zero")
        csil_ready, cT_ps, cT_ready = sem("csil_ready"), sem("cT_ps"), sem("cT_ready")
        xT_ps, xT_v, xT_a, xs_ps = sem("xT_ps"), sem("xT_v"), sem("xT_a"), sem("xs_ps")
        small_ps, small_ready = sem("small_ps"), sem("small_ready")
        ada_used, m_ready, m_stored = sem("ada_used"), sem("m_ready"), sem("m_stored")
        mT_ps, mT_ready = sem("mT_ps"), sem("mT_ready")
        h_v, h_a = sem("h_v"), sem("h_a")
        win_ps, zin_ready = sem("win_ps"), sem("zin_ready")
        xc_ready, gate_ps, gate_tanh, decay_ready = sem("xc_ready"), sem("gate_ps"), sem("gate_tanh"), sem("decay_ready")
        bnorm_ready, broot_ready, lru_done, gelu_ready = sem("bnorm_ready"), sem("broot_ready"), sem("lru_done"), sem("gelu_ready")
        sp_exp, ylru = sem("sp_exp"), sem("ylru")
        kv_ready, q_ready = sem("kv_ready"), sem("q_ready")
        vt_ps, vt_ready = sem("vt_ps"), sem("vt_ready")
        kcT_ps, kcT_ready, qz_ready, ss_ps = sem("kcT_ps"), sem("kcT_ready"), sem("qz_ready"), sem("ss_ps")
        snb_ready, sexp_done, sP_ready, sPT_ps, sPT_ready, sO_ps, sO_stored = (sem(n) for n in (
            "snb_ready", "sexp_done", "sP_ready", "sPT_ps", "sPT_ready", "sO_ps", "sO_stored"))
        S_ps, S_masked, nb_ready, exp_done, rden_ready, P_ready, Pv_ready = (sem(n) for n in (
            "S_ps", "S_masked", "nb_ready", "exp_done", "rden_ready", "P_ready", "Pv_ready"))
        PT_ps, PT_ready, O_ps, O_stored = (sem(n) for n in ("PT_ps", "PT_ready", "O_ps", "O_stored"))
        sq_ready, ss_sum_ps, ms_ready, rs_ready, rT_ready = (sem(n) for n in (
            "sq_ready", "ss_sum_ps", "ms_ready", "rs_ready", "rT_ready"))
        yg_ready, L_ps, A_ps, L_ready, A_used = (sem(n) for n in (
            "yg_ready", "L_ps", "A_ps", "L_ready", "A_used"))
        var_ready, std_ready, norm_ready, xhat_ready, x1_ready, h2_ready = (sem(n) for n in (
            "var_ready", "std_ready", "norm_ready", "xhat_ready", "x1_ready", "h2_ready"))
        h2_stored, x1_stored = [sem("h2_stored0"), sem("h2_stored1")], sem("x1_stored")
        h2T_ps, h2T_v, h2T_a, lgT_ps, lgT_ready, lg_ps = (sem(n) for n in (
            "h2T_ps", "h2T_v", "h2T_a", "lgT_ps", "lgT_ready", "lg_ps"))
        top_ready, top_exp, hot_ready, rank_ps, rows_ready, slot_ready = (sem(n) for n in (
            "top_ready", "top_exp", "hot_ready", "rank_ps", "rows_ready", "slot_ready"))
        tab_init, tab_done, count_ps, steps_ready = (sem(n) for n in (
            "tab_init", "tab_done", "count_ps", "steps_ready"))
        idx_in, idx_ready = sem("idx_in"), sem("idx_ready")
        X_in = [sem(f"X_in{j}") for j in range(RING)]
        XT_ps, XT_v, XT_a, gu_ps, silu_done, z_ready, zT_ps, zT_ready, y_ps, y_v, y_a = (sem(n) for n in (
            "XT_ps", "XT_v", "XT_a", "gu_ps", "silu_done", "z_ready", "zT_ps", "zT_ready", "y_ps", "y_v", "y_a"))
        y_out = [sem(f"y_out{j}") for j in range(RING)]
        experts_done, yy_in, out_ready, out_done = sem("experts_done"), [sem(f"yy_in{i}") for i in range(TT + 1)], sem("out_ready"), [sem("out_done0"), sem("out_done1")]
        wdiag_ready, ysum_ps, gated = (sem(n) for n in ("wdiag_ready", "ysum_ps", "gated"))
        state_done, cache_done = sem("state_done"), sem("cache_done")
        dve_step, act_step, pool_step = sem("dve_step"), sem("act_step"), sem("pool_step")

        ORDER = [0, 8, 1, 9, 2, 10, 3, 11, 12, 13, 4, 5, 6, 7]
        WCH = [0, 4, 1, 5, 6, 2, 3]
        GELU_AT, K_AT = 10, 8
        LAST = [max(q for q in range(len(ORDER)) if ORDER[q] // 2 == c) for c in WCH]
        HALVES = [(0, HALF), (HALF, NT - HALF)]
        TILES = [(t, P) for t in range(TT)] + [(TT, NS)]
        MIX = [(i, t, P if t < TT else NS) for i, t in enumerate([*range(TT - 1), TT, TT - 1])]

        block = ctx.enter_context(nc.Block())

        def pair_rows(ap):
            return ap.rearrange("(p k) n -> p k n", k=KD)

        wg_d = A["w_gate"][0].rearrange("e (p k) f -> e p k f", k=KD)
        wu_d = A["w_up"][0].rearrange("e (p k) f -> e p k f", k=KD)
        wd_d = A["w_down"][0].rearrange("e (p k) d -> e p k d", k=2)

        @block.sync
        def _(sp):
            sp.dma_start(crow[0:NS, :], A["c_sample"][:, :]).then_inc(c_in, 16)
            sp.dma_start(crow[NS:NC, :], A["c_prompt"][:, :]).then_inc(c_in, 16)
            sp.dma_start(x_tok[:, 0:TT, :], A["x_prompt"][0].rearrange("(t p) d -> p t d", p=P)).then_inc(x_in, 16)
            sp.dma_start(x_tok[0:NS, TT, :], A["x_sample"].rearrange("b s d -> (b s) d")).then_inc(x_in, 16)
            wa = A["w_ada"][0].rearrange("(p k) n -> p k n", k=KD)
            for j in range(KD):
                if j >= 4:
                    sp.wait_ge(ada_used, j - 3)
                sp.dma_start(ada[:, j % 4, :], wa[:, j, 0:2048]).then_inc(ada_in[j % 4], 16)
            wi = pair_rows(A["w_in"][0])
            for n, c in enumerate(WCH):
                if n >= 3:
                    sp.wait_ge(win_ps, 2 * (LAST[n - 3] + 1))
                sp.dma_start(win[:, n % 3, :, :], wi[:, :, c * 256:(c + 1) * 256]).then_inc(win_in[n % 3], 16)
                if n == 3:
                    sp.dma_start(kc[:, :, :], A["cache_k"][0].rearrange("b w k d -> w b (k d)")).then_inc(kv_in, 16)
                    sp.dma_start(vc[:, :, :], A["cache_v"][0].rearrange("b w k d -> w b (k d)")).then_inc(kv_in, 16)
                    sp.dma_start(brt[0:NG, :], A["b_group"].rearrange("a g -> g a")).then_inc(kv_in, 16)
                    sp.dma_start(brt[NG:NG + NE, :], A["b_router"][0].rearrange("g (e a) -> (g e) a", a=1)).then_inc(kv_in, 16)
                    for o, a in ((8, "cache_k"), (9, "cache_v")):
                        sp.dma_start(O[o][0, :, 0:WIN - 1].rearrange("b w k d -> b w (k d)"),
                                      A[a][0, :, 1:WIN].rearrange("b w k d -> b w (k d)")).then_inc(cache_done, 16)
                    sp.dma_start(O[6][0, :, 0:CW - 2, :], A["state_conv"][0, :, 1:CW - 1, :]).then_inc(cache_done, 16)

            def load_expert(e, p, q, parts=(True, True)):
                got = w_in[p % SETS]
                to = wex[p % SETS]
                if isinstance(e, int):
                    g, u_, d = (w[e].rearrange("p k f -> p (k f)") for w in (wg_d, wu_d, wd_d))
                else:
                    g, u_, d = (w[bass.ds(e, 1)].rearrange("a p k f -> p (a k f)") for w in (wg_d, wu_d, wd_d))
                if parts[0]:
                    sp.dma_start(to[:, q, 0:KD * DE], g).then_inc(got, 16)
                    sp.dma_start(to[:, q, KD * DE:GU], u_).then_inc(got, 16)
                if parts[1]:
                    sp.dma_start(to[:, q, GU:EXW], d).then_inc(down_in[p % SETS], 16)

            md = m_dram.rearrange("i a n -> i (a n)")

            def store_modulation(r, rows_):
                sp.wait_ge(m_ready, 2 * r)
                for g in range(4):
                    c0 = r * 2048 + g * 512
                    sp.dma_start(md[:, c0:c0 + 512], rows_[32 * g:32 * g + NC, :]).then_inc(m_stored, 16)

            store_modulation(1, m_sb[:, 1, :])
            sp.wait_ge(ylru, FW)
            sp.wait_ge(m_stored, 16 * 4)
            sp.dma_start(wout[:, :, :], A["w_out"][0].rearrange("(f p) n -> p f n", p=P)).then_inc(wout_in, 16)
            for j in range(3 * KD - 4, 3 * KD):
                sp.wait_ge(ada_used, j - 3)
                sp.dma_start(ada[:, j % 4, :], wa[:, j % KD, 4096:6144]).then_inc(ada_in[j % 4], 16)
            store_modulation(2, m_sb2)
            sp.wait_ge(sO_stored, 2)
            sp.wait_ge(state_done, 16 * 8)
            sp.wait_ge(cache_done, 16 * 3)
            sp.wait_ge(m_stored, 16 * 8)
            for n, i in enumerate((2, 4, 3)):
                sp.dma_start(mod[:, n, :], m_dram[NS:NC, i, :].broadcast_to((P, D))).then_inc(mod_in, 16)
            sp.dma_start(mod[:, 3, :], A["ln1_g"].broadcast_to((P, D))).then_inc(mod_in, 16)
            sp.dma_start(mod[:, 4, :], A["ln1_b"].broadcast_to((P, D))).then_inc(mod_in, 16)
            sp.wait_ge(ada_used, 24)
            sp.wait_ge(win_ps, 2 * len(ORDER))
            for q in range(2):
                load_expert(q, 0, q)
            sp.wait_ge(ss_sum_ps, 1)
            for n, i in enumerate((2, 4, 3)):
                sp.dma_start(smod[:, n, :], m_dram[0:NS, i, :]).then_inc(smod_in, 16)
            sp.wait_ge(O_stored, 2 * TT)
            sp.dma_start(wr[:, :, 0:NG], pair_rows(A["w_group"][0])).then_inc(wr_in, 16)
            for g in range(NG):
                sp.dma_start(wr[:, :, NG + g * EPG:NG + (g + 1) * EPG], pair_rows(A["w_router"][0, g])).then_inc(wr_in, 16)
            for i, t, n in MIX:
                sp.wait_ge(h2_ready, i + 1)
                sp.dma_start(h_dram[t * P:t * P + n, :], h2[0:n, i % 2, :]).then_inc(h2_stored[i % 2], 16)
                sp.wait_ge(x1_ready, i + 1)
                sp.dma_start(x1_dram[t * P:t * P + n, :], x_tok[0:n, t, :]).then_inc(x1_stored, 16)
            sp.wait_ge(lgT_ps, 2)
            load_expert(2, 1, 0)
            sp.wait_ge(lg_ps, 1)
            sp.wait_ge(h2_stored[0], 16 * (TT // 2 + 1))
            sp.wait_ge(h2_stored[1], 16 * (TT // 2))
            load_expert(3, 1, 1)
            sp.wait_ge(x1_stored, 16 * (TT + 1))
            load_expert(4, 2, 0, (True, False))
            sp.wait_ge(X_in[AHEAD - 1], 16)
            load_expert(4, 2, 0, (False, True))
            load_expert(5, 2, 1)
            for n, a in ((3, "ln2_g"), (4, "ln2_b")):
                sp.dma_start(mod[:, n, :], A[a].broadcast_to((P, D))).then_inc(lnp_in, 16)
            sp.wait_ge(steps_ready, 1)

            def load_pair(i, j):
                last_step = sp.value_load(pend_i[0:1, bass.ds(SETS * i + (j - SETS), 1)], min_val=1, max_val=MAXSTEP)
                for half, done in enumerate((gu_ps, y_ps)):
                    sp.wait_ge(done, last_step)
                    for q in range(2):
                        load_expert(2 * SETS * i + (2 * j + q), j, q, (half == 0, half == 1))

            with sp.Fori(1, NPAIR // SETS) as i:
                for j in range(SETS):
                    load_pair(i, j)
            for j in range(NPAIR % SETS):
                load_pair(NPAIR // SETS, j)
            last_step = sp.value_load(pend_i[0:1, NPAIR - 2:NPAIR - 1], min_val=1, max_val=MAXSTEP)
            sp.wait_ge(y_ps, last_step)
            sp.dma_start(mod[:, 0, :], m_dram[NS:NC, 5, :].broadcast_to((P, D))).then_inc(lnp_in, 16)
            sp.dma_start(smod[:, 3, :], m_dram[0:NS, 5, :]).then_inc(lnp_in, 16)
            sp.dma_start(x_tok[:, 0:TT, :], x1_dram[0:T, :].rearrange("(t p) d -> p t d", p=P)).then_inc(lnp_in, 16)
            sp.dma_start(x_tok[0:NS, TT, :], x1_dram[T:NT, :]).then_inc(lnp_in, 16)
            sp.wait_ge(experts_done, 1)
            for t, n in TILES:
                for c in range(2):
                    sp.dma_start(yy[0:n, t, c, :], y_dram[c * NT + t * P:c * NT + t * P + n, :]).then_inc(yy_in[t], 16)
            yp = O[0][0].rearrange("(t p) d -> t p d", p=P)
            for t, n in TILES:
                sp.wait_ge(out_ready, t + 1)
                dst = yp[t] if t < TT else O[1].rearrange("b s d -> (b s) d")
                sp.dma_start(dst, yout[0:n, t % 2, :]).then_inc(out_done[t % 2], 16)
            sp.wait_ge(out_done[0], 16 * (TT // 2 + 1))
            sp.wait_ge(out_done[1], 16 * (TT // 2))

        @block.gpsimd
        def _(pool):
            steps = [0]

            def link(ins):
                steps[0] += 1
                ins.then_inc(pool_step, 1)
                pool.wait_ge(pool_step, steps[0])

            def step(ins):
                steps[0] += 1
                ins.then_inc(pool_step, 1)

            step(pool.memset(ident[:, :], 0.0))
            step(pool.memset(cT[:, :, :], 0.0))
            step(pool.memset(b_row[:, :, :], 0.0))
            step(pool.memset(mask[:, :, :], 0.0))
            step(pool.memset(ones[:, :], 1.0))
            step(pool.memset(ones_bf[:, :], 1.0))
            step(pool.memset(tri[:, :], 1.0))
            step(pool.memset(bsel[:, :, :], 1.0))
            step(pool.memset(fill[:, :], NOWHERE))
            pool.memset(sink_s[:, :], 0.0).then_inc(consts, 1)
            step(pool.memset(wrg[:, :, :, :], 0.0))
            step(pool.iota(iota_i[:, :], pattern=[[1, NE]], base=0, channel_multiplier=0))
            for c in range(2):
                step(pool.iota(pair_id[:, :, c, 0], pattern=[[P, TT + 1]], base=0, channel_multiplier=1))
                link(pool.iota(pair_id[:, :, c, 1], pattern=[[P, TT + 1]], base=c * NT, channel_multiplier=1))
            pool.affine_select(out=ident[:, :], in_=ident[:, :], compare_op=ALU.not_equal, fill=1.0, base=0,
                               pattern=[[-1, P]], channel_multiplier=1).then_inc(consts, 1)
            step(pool.affine_select(out=mask[:, 0, :], in_=mask[:, 0, :], compare_op=ALU.is_ge, fill=NEG, base=0,
                                    pattern=[[1, P]], channel_multiplier=-1))
            step(pool.affine_select(out=mask[:, 1, :], in_=mask[:, 1, :], compare_op=ALU.is_ge, fill=NEG, base=0,
                                    pattern=[[-1, P]], channel_multiplier=1))
            step(pool.affine_select(out=tri[:, :], in_=tri[:, :], compare_op=ALU.is_gt, fill=0.0, base=0,
                                    pattern=[[1, P]], channel_multiplier=-1))
            link(pool.affine_select(out=bsel[:, :, :], in_=bsel[:, :, :], compare_op=ALU.is_ge, fill=0.0, base=0,
                                    pattern=[[P, 2], [-32, NS]], channel_multiplier=1))
            step(pool.affine_select(out=bsel[:, :, :], in_=bsel[:, :, :], compare_op=ALU.is_ge, fill=0.0, base=31,
                                    pattern=[[-P, 2], [32, NS]], channel_multiplier=-1))
            pool.wait_ge(pool_step, steps[0])
            pool.tensor_copy(iota_e[:, :], iota_i[:, :]).then_inc(consts, 1)
            pool.dma_start(table.rearrange("(p n) w -> p (n w)", p=P), fill[:, :]).then_inc(tab_init, 16)
            for j in range(4):
                pool.dma_start(b_row[32 * j:32 * j + NC, :, :],
                               A["b_ada"].rearrange("a (r j n) -> a r j n", r=3, j=4)[:, 0:2, j, :].broadcast_to((NC, 2, 512))).then_inc(brow_in, 16)
            wa = A["w_ada"][0].rearrange("(p k) n -> p k n", k=KD)
            for j in range(KD, 3 * KD - 4):
                pool.wait_ge(ada_used, j - 3)
                if j == KD:
                    for g, a in enumerate(("w_rg_a", "w_rg_x")):
                        wv = A[a][0].rearrange("(f n) d e -> n d f e", n=2)
                        for n in range(2):
                            pool.dma_start(wrg[64 * n:64 * n + 64, g, :, 64 * n:64 * n + 64], wv[n]).then_inc(wrg_in, 16)
                pool.dma_start(ada[:, j % 4, :], wa[:, j % KD, (j // KD) * 2048:(j // KD + 1) * 2048]).then_inc(ada2_in[j % 4], 16)
                if j == 2 * KD:
                    pool.wait_ge(tab_init, 16)
                    pool.wait_ge(cT_ps, 1)
                    pool.memset(kTz[:, :, :, :], 0.0).then_inc(kz_zero, 1)
                    pool.memset(qz[:, :, :], 0.0).then_inc(kz_zero, 1)
            def late_bias_and_states():
                pool.wait_ge(win_ps, 2 * len(ORDER))
                link(pool.memset(b_row2[:, :], 0.0))
                for j in range(4):
                    pool.dma_start(b_row2[32 * j:32 * j + NC, :],
                                   A["b_ada"].rearrange("a (r j n) -> a r j n", r=3, j=4)[:, 2, j, :].broadcast_to((NC, 512))).then_inc(brow_in, 16)
                pool.wait_ge(vt_ready, 4)
                rows_ = tails[:, :, :].rearrange("r f p -> r (f p)")
                pool.dma_start(O[2][0, 0], rows_[0:3, :]).then_inc(state_done, 16)
                pool.dma_start(O[6][0, :, CW - 2, :], rows_[3:11, :]).then_inc(state_done, 16)
                pool.dma_start(O[3][0], rows_[11:12, :]).then_inc(state_done, 16)
                pool.dma_start(O[7][0], rows_[12:20, :]).then_inc(state_done, 16)
                pool.wait_ge(vt_ready, 3)
                pool.dma_start(O[4][0, 0].rearrange("w k d -> w (k d)"), klast[:, :]).then_inc(state_done, 16)
                pool.dma_start(O[5][0, 0].rearrange("w k d -> w (k d)"), vtok[:, TT - 1, :]).then_inc(state_done, 16)
                for n in range(2):
                    pool.dma_start(O[8 + n][0, :, WIN - 1].rearrange("b k d -> b (k d)"), knv[:, n, :]).then_inc(state_done, 16)

            for b in range(TT):
                keys = slice(0, 2 * P) if b else slice(P, 2 * P)
                pool.wait_ge(rden_ready, b + 1)
                for h in range(G, NH):
                    pool.tensor_scalar(Pm[b % 3][:, h, keys], Pm[b % 3][:, h, keys], rden[:, b % 2, h:h + 1], None,
                                       ALU.mult).then_inc(P_ready, 1)
                if b == 0:
                    late_bias_and_states()
            pool.wait_ge(mod_in, 16 * 5)
            for rows_, n, got in ((mod, P, None), (smod, NS, smod_in)):
                if got is not None:
                    pool.wait_ge(got, 48)
                link(pool.tensor_tensor(gb[0:n, :], rows_[0:n, 1, :], mod[0:n, 4, :], ALU.mult))
                link(pool.tensor_tensor(rows_[0:n, 2, :], rows_[0:n, 2, :], gb[0:n, :], ALU.add))
                pool.tensor_tensor(rows_[0:n, 1, :], rows_[0:n, 1, :], mod[0:n, 3, :], ALU.mult).then_inc(rows_ready, 1)
            pool.wait_ge(tab_init, 16)
            for i, t, n in MIX:
                pool.wait_ge(xhat_ready, i + 1)
                link(pool.tensor_tensor(x_tok[0:n, t, :], u[0:n, i % 2, :], mod[0:n, 3, :], ALU.mult))
                pool.tensor_tensor(x_tok[0:n, t, :], x_tok[0:n, t, :], mod[0:n, 4, :], ALU.add).then_inc(x1_ready, 1)
            pool.wait_ge(L_ps, TT + 1)
            pool.wait_ge(A_ps, TT)
            step(pool.memset(X[:, :, :], 0.0))
            link(pool.iota(sgrid_i[:, :, :], pattern=[[1, NSTEP], [0, NPAIR]], base=0, channel_multiplier=0))
            pool.tensor_copy(sgrid[:, :, :], sgrid_i[:, :, :]).then_inc(rows_ready, 1)
            pool.wait_ge(slot_ready, 1)
            for t, n in TILES:
                for c in range(2):
                    pool.indirect_dma_start(table[:, :], bass.IndirectOffsetOnAxis(ap=slot[0:n, t, c:c + 1], axis=0),
                                            pair_id[0:n, t, c, :], None, bounds_check=2 * NSTEP * CAP - 1,
                                            oob_is_err=False).then_inc(tab_done, 16)
            pool.wait_ge(tab_done, 16 * 2 * (TT + 1))
            pool.wait_ge(h2_stored[0], 16 * (TT // 2 + 1))
            pool.wait_ge(h2_stored[1], 16 * (TT // 2))
            pool.dma_start(idx_all[:, :, :], table.rearrange("(p s) w -> p s w", s=NSTEP)).then_inc(idx_in, 16)
            pool.wait_ge(idx_in, 16)

            def counted(*values):
                values = [v if isinstance(v, int) else pool.to_reg(v) for v in values]
                pool.wait_ge(tab_init, 16)
                return values if len(values) > 1 else values[0]

            def gather(j, s, n):
                pool.tensor_copy(gidx[:, j:j + 1], idx_all[:, bass.ds(s, 1), 0]).then_inc(idx_ready, 1)
                pool.wait_ge(idx_ready, counted(n + 1))
                pool.indirect_dma_start(X[:, j, :], None, h_dram[:, :],
                                        bass.IndirectOffsetOnAxis(ap=gidx[:, j:j + 1], axis=0),
                                        bounds_check=NT - 1, oob_is_err=False).then_inc(X_in[j], 16)

            def scatter(j, s):
                outputs = counted(s + 1)
                pool.wait_ge(y_v, outputs)
                pool.wait_ge(y_a, outputs)
                pool.tensor_copy(sidx[:, j:j + 1], idx_all[:, bass.ds(s, 1), 1]).then_inc(idx_ready, 1)
                pool.wait_ge(idx_ready, counted(AHEAD + 2 * s + 2))
                pool.indirect_dma_start(y_dram[:, :], bass.IndirectOffsetOnAxis(ap=sidx[:, j:j + 1], axis=0),
                                        yo[:, j, :], None, bounds_check=2 * NT - 1,
                                        oob_is_err=False).then_inc(y_out[j], 16)

            def turn(i, peeled):
                for j in range(RING):
                    s = RING * i + j
                    if not (peeled and j == 0):
                        pool.wait_ge(XT_ps, counted(2 * s))
                    gather((j + AHEAD) % RING, s + AHEAD, AHEAD + 2 * s)
                    scatter(j, s)

            for s in range(AHEAD):
                gather(s, s, s)
            turn(0, True)
            with pool.Fori(1, MINTURNS) as i:
                turn(i, False)
            pool.wait_ge(steps_ready, 1)
            nturns = pool.value_load(turns[0:1, 0:1], min_val=MINTURNS, max_val=TURNS)
            with pool.Fori(MINTURNS, TURNS) as i:
                with pool.If(nturns > i):
                    turn(i, False)
            scattered, gathered = counted(16 * nturns, 16 * nturns + 16)
            for j in range(RING):
                pool.wait_ge(y_out[j], scattered)
                pool.wait_ge(X_in[j], gathered if j < AHEAD else scattered)
            pool.memset(mark[:, :], 0.0).then_inc(experts_done, 1)
            pool.wait_ge(lnp_in, 96)
            for t, n in TILES[:TT]:
                f = yy[0:n, t, 0, :]
                pool.wait_ge(xhat_ready, TT + 2 + t)
                link(pool.tensor_tensor(f, f, mod[0:n, 3, :], ALU.mult))
                if t >= 2:
                    pool.wait_ge(out_done[t % 2], 16 * (t // 2))
                pool.tensor_tensor(yout[0:n, t % 2, :], f, mod[0:n, 4, :], ALU.add).then_inc(out_ready, 1)

        @block.scalar
        def _(act):
            steps = [0]

            def link(ins):
                steps[0] += 1
                ins.then_inc(act_step, 1)
                act.wait_ge(act_step, steps[0])

            act.wait_ge(c_in, 32)
            act.activation(csil[:, :], crow[:, :], ACT.Silu).then_inc(csil_ready, 1)
            act.dma_start(prm[0:16, :], A["conv_w"][0].rearrange("k (f p) -> (k f) p", p=P)).then_inc(small_in, 16)
            for n, a in enumerate(("conv_b", "b_rg_a", "b_rg_x", "lru_lambda", "g_lru", "g_attn")):
                v = A[a][0]
                v = v.rearrange("(f n) e -> f (n e)", n=2) if a in ("b_rg_a", "b_rg_x") else v.rearrange("(f p) -> f p", p=P)
                act.dma_start(prm[16 + 4 * n:20 + 4 * n, :], v).then_inc(small_in, 16)
            act.dma_start(stt_in[0:24, :], A["state_conv"][0].rearrange("b k n -> (b k) n")).then_inc(small_in, 16)
            act.dma_start(stt_in[24:32, :], A["state_h"][0]).then_inc(small_in, 16)
            act.dma_start(sinks8[:, 0, :], A["sinks"].broadcast_to((P, NH))).then_inc(small_in, 16)
            act.wait_ge(consts, 1)
            for j in range(4):
                act.dma_start(sink_s[32 * j:32 * j + NH, 0:1], A["sinks"].rearrange("a h -> h a")).then_inc(small_in, 16)
            for k in range(1, KD, 2):
                act.wait_ge(xT_ps, k + 1)
                act.activation(hT[:, k, 0:T], B[k % 4][:, :], ACT.Copy).then_inc(xT_a, 1)
            act.wait_ge(small_ready, 3)
            act.activation(spt[:, 1, :], spt[:, 0, :], ACT.Exp, scale=-1.0).then_inc(sp_exp, 1)
            act.wait_ge(mT_ready, 4)
            act.wait_ge(xT_a, 4)
            for k in range(1, KD, 2):
                act.activation(hT[:, k, 0:T], hT[:, k, 0:T], ACT.Identity, scale=mT[:, 1, k, NS:NC],
                               bias=mT[:, 0, k, NS:NC]).then_inc(h_a, 1)

            def lru_act(f, g):
                dst = (tr, ti)[g]
                for h in range(2):
                    act.wait_ge(gate_ps, 4 * f + 2 * g + h + 1)
                    if f and g == 0 and h == 0:
                        act.wait_ge(lru_done, f)
                    act.activation(dst[:, h * XH:(h + 1) * XH], B[6 + h][:, 0:XH], ACT.Tanh, scale=0.5,
                                   bias=spt[:, 4 + g, f:f + 1]).then_inc(gate_tanh, 1)
                if g == 0:
                    return
                act.wait_ge(gate_tanh, 4 * (f + 1))
                act.activation(aa[:, :], tr[:, :], ACT.Exp, scale=sp4[:, 1, f:f + 1], bias=sp4[:, 1, f:f + 1]).then_inc(decay_ready, 1)
                act.activation(th[:, :], tr[:, :], ACT.Tanh, scale=sp4[:, 0, f:f + 1], bias=sp4[:, 0, f:f + 1]).then_inc(decay_ready, 1)
                act.wait_ge(bnorm_ready, f + 1)
                act.activation(a2[:, :], a2[:, :], ACT.Sqrt, scale=0.25).then_inc(broot_ready, 1)

            def copy_cached_keys():
                for n in range(2):
                    act.wait_ge(kcT_ps, n + 1)
                    act.activation(kbT[:, 4 * n:4 * n + 4, 0:WIN], B[6 + n][:, :].rearrange("p (b w) -> p b w", w=WIN),
                                   ACT.Copy).then_inc(kcT_ready, 1)

            def sample_exponentials():
                act.wait_ge(snb_ready, 1)
                for n in range(2):
                    act.activation(sv[:, 3, n:n + 1], sink_s[:, 0:1], ACT.Exp, bias=sv[:, 2, n:n + 1]).then_inc(sexp_done, 1)
                for n in range(2):
                    act.activation(ps[:, n, :], ps[:, n, :], ACT.Exp, scale=SCALE, bias=sv[:, 2, n:n + 1],
                                   accum_out=sv[:, 4, n:n + 1]).then_inc(sexp_done, 1)

            for q, f in enumerate(ORDER):
                b0 = (q % 2) * 2
                if q < K_AT and q % 2 == 0:
                    act.wait_ge(win_ps, 2 * q + 1)
                    if f >= 2:
                        act.wait_ge(xc_ready, f - 1)
                    act.activation(xb[:, f % 2, CW - 1:CW - 1 + HALF], B[b0][:, 0:HALF], ACT.Copy).then_inc(zin_ready, 1)
                    act.wait_ge(win_ps, 2 * q + 2)
                    act.activation(xb[:, f % 2, CW - 1 + HALF:CW - 1 + T], B[b0 + 1][:, 0:T - HALF], ACT.Copy).then_inc(zin_ready, 1)
                    act.activation(xb[:, f % 2, S0 + CW - 1:CONV:CW], B[b0 + 1][:, T - HALF:NT - HALF], ACT.Copy).then_inc(zin_ready, 1)
                elif q < K_AT:
                    for h, (c0, cn) in enumerate(HALVES):
                        act.wait_ge(win_ps, 2 * q + h + 1)
                        act.activation(qT[:, f - 8, c0:c0 + cn], B[b0 + h][:, 0:cn], ACT.Copy).then_inc(q_ready, 1)
                elif q < GELU_AT:
                    if q == K_AT:
                        act.wait_ge(kz_zero, 2)
                        act.wait_ge(tab_init, 16)
                    for h, (c0, cn) in enumerate(HALVES):
                        act.wait_ge(win_ps, 2 * q + h + 1)
                        if q == K_AT:
                            cp = min(cn, T - c0)
                            for kv in range(NKV):
                                for half in range(2):
                                    act.activation(kTz[64 * half:64 * half + 64, kv, half, c0:c0 + cp],
                                                   B[b0 + h][64 * kv:64 * kv + 64, 0:cp], ACT.Copy)
                        act.activation(kvT[:, q - K_AT, c0:c0 + cn], B[b0 + h][:, 0:cn], ACT.Copy).then_inc(kv_ready, 1)
                else:
                    if q == GELU_AT:
                        act.wait_ge(lru_done, FW)
                    for h, (c0, cn) in enumerate(HALVES):
                        act.wait_ge(win_ps, 2 * q + h + 1)
                        act.activation(gel[:, q - GELU_AT, c0:c0 + cn], B[b0 + h][:, 0:cn], ACT.Gelu_apprx_tanh).then_inc(gelu_ready, 1)
                if 1 <= q <= K_AT:
                    lru_act((q - 1) // 2, (q - 1) % 2)
                if q == GELU_AT + 1:
                    copy_cached_keys()
                if q == GELU_AT + 2:
                    sample_exponentials()

            act.wait_ge(ylru, FW)
            for f in range(FW):
                act.activation(sq[:, f, :], yT[:, f, :], ACT.Square).then_inc(sq_ready, 1)

            def exps(b):
                keys = slice(0, 2 * P) if b else slice(P, 2 * P)
                act.wait_ge(nb_ready, 2 * (b + 1))
                act.activation(es[:, b % 2, :], es[:, b % 2, :], ACT.Exp).then_inc(exp_done, 1)
                for h in range(NH):
                    act.activation(Pm[b % 3][:, h, keys], Pm[b % 3][:, h, keys], ACT.Exp, scale=SCALE,
                                   bias=nb[:, b % 2, h:h + 1], accum_out=sums[:, b % 2, h:h + 1]).then_inc(exp_done, 1)

            def pt_count(b):
                return 0 if b == 0 else 2 + 4 * (b - 1)

            def evacuate_PT(b):
                first = pt_count(b)
                kbs = (0, 1) if b else (1,)
                for n, (kb, kv) in enumerate((kb, kv) for kv in range(NKV) for kb in kbs):
                    act.wait_ge(PT_ps, first + n + 1)
                    if b and n == 0:
                        act.wait_ge(O_ps, b)
                    act.activation(PT[:, kb, kv, :], B[4 + n % 2][:, :], ACT.Copy).then_inc(PT_ready, 1)

            for b in range(TT + 1):
                if b < TT:
                    exps(b)
                if b >= 1:
                    evacuate_PT(b - 1)
            act.wait_ge(sO_stored, 2)
            act.wait_ge(O_stored, 2 * TT)
            for f in range(FW, 2 * FW):
                act.activation(sq[:, f, :], yT[:, f, :], ACT.Square).then_inc(sq_ready, 1)
            act.wait_ge(ms_ready, 1)
            act.activation(rs[:, :], rs[:, :], ACT.Sqrt).then_inc(rs_ready, 1)

            def mixer_out(i, t, n):
                act.wait_ge(L_ps, i + 1)
                if i >= 2:
                    act.wait_ge(x1_ready, i - 1)
                for c in range(2):
                    src = B[c][:, :] if t < TT else B[7][32 * c:32 * c + n, :]
                    act.activation(u[0:n, i % 2, c * 512:(c + 1) * 512], src, ACT.Copy, scale=rT[0:n, t, 0:1]).then_inc(L_ready, 1)

            def xhat(i, t, n):
                act.wait_ge(var_ready, i + 1)
                act.activation(st1[0:n, 1:2], st1[0:n, 0:1], ACT.Sqrt).then_inc(std_ready, 1)
                act.wait_ge(norm_ready, i + 1)
                act.activation(u[0:n, i % 2, :], u[0:n, i % 2, :], ACT.Identity, scale=st1[0:n, 2:3],
                               bias=st1[0:n, 3:4]).then_inc(xhat_ready, 1)

            def copy_h2T(i, t, n):
                act.wait_ge(h2T_ps, 2 * i + 2)
                act.activation(h2T[:, 4:8, t * P:t * P + n], B[5][:, :].rearrange("p (k m) -> p k m", m=P)[:, :, 0:n], ACT.Copy).then_inc(h2T_a, 1)

            act.wait_ge(rT_ready, 3)
            for i in range(TT + 2):
                if i <= TT:
                    mixer_out(*MIX[i])
                if i >= 1:
                    copy_h2T(*MIX[i - 1])
                if i <= TT:
                    xhat(*MIX[i])
            act.wait_ge(top_ready, 1)
            act.activation(gt[:, 1, :, :], gt[:, 0, :, :], ACT.Exp).then_inc(top_exp, 1)
            act.wait_ge(top_ready, 2)
            act.activation(col[:, 5, :], col[:, 4, :], ACT.Exp).then_inc(top_exp, 1)

            def copy_XT(s, n):
                act.wait_ge(XT_ps, 2 * n + 2)
                act.activation(XT[:, s % 2, 4:8, :], B[1][:, :].rearrange("p (k m) -> p k m", m=P), ACT.Copy).then_inc(XT_a, 1)

            def turn(i, peeled):
                for j in range(RING):
                    n = RING * i + j
                    act.wait_ge(gu_ps, n + 1)
                    act.activation(silu_g[:, :], B[2 + j % 2][:, 0:DE], ACT.Silu).then_inc(silu_done, 1)
                    act.wait_ge(zT_ps, n + 1)
                    act.activation(zT[:, :, :], B[4][:, 0:2 * P].rearrange("p (k m) -> p k m", m=P), ACT.Copy).then_inc(zT_ready, 1)
                    copy_XT(j + 1, n + 1)
                    act.wait_ge(y_ps, n + 1)
                    if not peeled:
                        act.wait_ge(y_out[j], 16 * i)
                    act.activation(yo[:, j, 512:D], B[6][:, :], ACT.Copy).then_inc(y_a, 1)

            copy_XT(0, 0)
            turn(0, True)
            with act.Fori(1, MINTURNS) as i:
                turn(i, False)
            nturns = act.value_load(turns[0:1, 0:1], min_val=MINTURNS, max_val=TURNS)
            with act.Fori(MINTURNS, TURNS) as i:
                with act.If(nturns > i):
                    turn(i, False)

            def xhat2(t, n):
                act.wait_ge(var_ready, TT + 2 + t)
                act.activation(st1[0:n, 1:2], st1[0:n, 0:1], ACT.Sqrt).then_inc(std_ready, 1)
                act.wait_ge(norm_ready, TT + 2 + t)
                act.activation(yy[0:n, t, 0, :], yy[0:n, t, 0, :], ACT.Identity, scale=st1[0:n, 2:3],
                               bias=st1[0:n, 3:4]).then_inc(xhat_ready, 1)

            for t in range(TT + 1):
                xhat2(*TILES[t])

        @block.vector
        def _(dve):
            steps = [0]

            def link(ins):
                steps[0] += 1
                ins.then_inc(dve_step, 1)
                dve.wait_ge(dve_step, steps[0])

            def step(ins):
                steps[0] += 1
                ins.then_inc(dve_step, 1)

            def settle():
                dve.wait_ge(dve_step, steps[0])

            dve.wait_ge(cT_ps, 1)
            dve.wait_ge(consts, 3)
            dve.tensor_copy(cT[:, :, 0:NC], B[7][:, 0:KD * 16].rearrange("p (k c) -> p k c", c=16)[:, :, 0:NC]).then_inc(cT_ready, 1)
            for k in range(0, KD, 2):
                dve.wait_ge(xT_ps, k + 1)
                dve.tensor_copy(hT[:, k, 0:T], B[k % 4][:, :]).then_inc(xT_v, 1)
            dve.wait_ge(xs_ps, 1)
            dve.tensor_copy(hT[:, :, T:NT], B[6][:, 0:KD * NS].rearrange("p (k b) -> p k b", b=NS)).then_inc(xT_v, 1)
            dve.wait_ge(small_ps, 1)
            dve.tensor_copy(par[:, :], B[5][:, 0:40]).then_inc(small_ready, 1)
            dve.tensor_copy(stT[:, :, :], B[5][:, 64:64 + FW * 32].rearrange("p (f c) -> p f c", c=32)).then_inc(small_ready, 1)
            dve.wait_ge(small_ready, 2)
            lam = par[:, 28:32]
            link(dve.tensor_scalar(spt[:, 1, :], lam, -1.0, None, ALU.mult))
            dve.tensor_tensor(spt[:, 0, :], spt[:, 1, :], lam, ALU.max).then_inc(small_ready, 1)
            link(dve.tensor_scalar(spt[:, 2, :], lam, -1.0, 0.0, ALU.mult, ALU.max))
            dve.wait_ge(sp_exp, 1)
            link(dve.tensor_scalar(spt[:, 3, :], spt[:, 1, :], 2.0, None, ALU.add))
            link(dve.reciprocal(spt[:, 3, :], spt[:, 3, :]))
            link(dve.tensor_tensor(spt[:, 3, :], spt[:, 3, :], spt[:, 1, :], ALU.mult))
            link(dve.tensor_tensor(spt[:, 1, :], spt[:, 3, :], spt[:, 3, :], ALU.mult))
            link(dve.tensor_scalar(spt[:, 4, :], spt[:, 1, :], 1.0 / 17, 1.0 / 15, ALU.mult, ALU.add))
            for c in (13, 11, 9, 7, 5, 3, 1):
                link(dve.tensor_tensor(spt[:, 4, :], spt[:, 4, :], spt[:, 1, :], ALU.mult))
                link(dve.tensor_scalar(spt[:, 4, :], spt[:, 4, :], 1.0 / c, None, ALU.add))
            link(dve.tensor_tensor(spt[:, 4, :], spt[:, 4, :], spt[:, 3, :], ALU.mult))
            link(dve.scalar_tensor_tensor(out=spt[:, 4, :], in0=spt[:, 4, :], scalar=2.0, in1=spt[:, 2, :], op0=ALU.mult, op1=ALU.add))
            link(dve.tensor_scalar(sp4[:, 0, :], spt[:, 4, :], 4.0, None, ALU.mult))
            link(dve.tensor_scalar(sp4[:, 1, :], spt[:, 4, :], -4.0, None, ALU.mult))
            step(dve.tensor_scalar(spt[:, 4, :], par[:, 20:24], 0.5, None, ALU.mult))
            step(dve.tensor_scalar(spt[:, 5, :], par[:, 24:28], 0.5, None, ALU.mult))
            dve.wait_ge(small_in, 16 * 14)
            step(dve.tensor_scalar(sinks8[:, 1, :], sinks8[:, 0, :], 1.0 / SCALE, None, ALU.mult))
            step(dve.tensor_scalar(sink_s[:, 1:2], sink_s[:, 0:1], 1.0 / SCALE, None, ALU.mult))

            def modulation(r):
                dve.wait_ge(ada_used, KD * (r + 1))
                if r != 1:
                    dve.wait_ge(brow_in, 16 * (4 if r == 0 else 8))
                bank, bias, to = (B[7], b_row2, m_sb2) if r == 2 else (B[4], b_row[:, r, :], m_sb[:, r, :])
                link(dve.tensor_tensor(to[:, :], bank[:, :], bias[:, :], ALU.add))
                plus = {0: (64, 128), 1: (0, 64), 2: (0, 128)}[r]
                for p0 in range(plus[0], plus[1], 64):
                    dve.tensor_scalar(to[p0:p0 + 64, :], to[p0:p0 + 64, :], 1.0, None, ALU.add).then_inc(m_ready, 1)

            modulation(0)
            for g in range(4):
                if g == 0:
                    dve.wait_ge(mT_ps, 1)
                for kk in range(2):
                    i = dve.tensor_copy(mT[64 * (g % 2):64 * (g % 2) + 64, g // 2, 4 * kk:4 * kk + 4, :],
                                        B[5 + 2 * kk][0:64, :].rearrange("p (k c) -> p k c", c=P)[:, :, 32 * g:32 * g + NC])
                    if kk:
                        i.then_inc(mT_ready, 1)
                    else:
                        step(i)
            dve.wait_ge(mT_ready, 4)
            dve.wait_ge(xT_v, 5)
            for k in range(0, KD, 2):
                dve.tensor_scalar(hT[:, k, 0:T], hT[:, k, 0:T], mT[:, 1, k, NS:NC], mT[:, 0, k, NS:NC], ALU.mult, ALU.add).then_inc(h_v, 1)
            link(dve.tensor_tensor(hT[:, :, T:NT], hT[:, :, T:NT], mT[:, 1, :, 0:NS], ALU.mult))
            dve.tensor_tensor(hT[:, :, T:NT], hT[:, :, T:NT], mT[:, 0, :, 0:NS], ALU.add).then_inc(h_v, 1)
            step(dve.memset(xb[:, :, 0:CW - 1], 0.0))

            def conv(f):
                v = xb[:, f % 2, :]
                o = xc[:, f % 3, :]
                step(dve.tensor_copy(xb[:, f % 2, S0:CONV].rearrange("p (b k) -> p b k", k=CW)[:, :, 0:CW - 1],
                                     stT[:, f, 0:24].rearrange("p (b k) -> p b k", k=CW - 1)))
                dve.wait_ge(zin_ready, 3 * (f + 1))
                settle()
                if f >= 3:
                    dve.wait_ge(gate_ps, 4 * (f - 2))
                step(dve.tensor_copy(tail_in[:, f, 0:3], v[:, T:T + 3]))
                step(dve.tensor_copy(tail_in[:, f, 3:11], v[:, S0 + CW - 1:CONV:CW]))
                link(dve.tensor_scalar(o, v[:, 0:XC], par[:, f:f + 1], par[:, 16 + f:17 + f], ALU.mult, ALU.add))
                for k in range(1, CW):
                    i = dve.scalar_tensor_tensor(out=o, in0=v[:, k:k + XC], scalar=par[:, 4 * k + f:4 * k + f + 1], in1=o,
                                                 op0=ALU.mult, op1=ALU.add)
                    if k < CW - 1:
                        link(i)
                    else:
                        i.then_inc(xc_ready, 1)

            def lru(f):
                o = xc[:, f % 3, :]
                dve.wait_ge(decay_ready, 2 * f + 1)
                link(dve.tensor_tensor(a2[:, :], aa[:, :], aa[:, :], ALU.mult))
                dve.wait_ge(decay_ready, 2 * f + 2)
                link(dve.scalar_tensor_tensor(out=a2[:, :], in0=a2[:, :], scalar=1.0, in1=th[:, :], op0=ALU.add, op1=ALU.mult))
                dve.tensor_scalar(a2[:, :], a2[:, :], 1e-30, None, ALU.max).then_inc(bnorm_ready, 1)
                link(dve.scalar_tensor_tensor(out=ti[:, :], in0=ti[:, :], scalar=1.0, in1=o, op0=ALU.add, op1=ALU.mult))
                dve.wait_ge(broot_ready, f + 1)
                link(dve.tensor_tensor(ti[:, :], ti[:, :], a2[:, :], ALU.mult))
                link(dve.tensor_tensor_scan(yT[:, f, 0:T], aa[:, 0:T], ti[:, 0:T], 0.0, ALU.mult, ALU.add))
                link(dve.tensor_tensor(yT[:, f, T:NT], aa[:, S0:XC:CW], stT[:, f, 24:32], ALU.mult))
                link(dve.tensor_tensor(yT[:, f, T:NT], yT[:, f, T:NT], ti[:, S0:XC:CW], ALU.add))
                dve.tensor_copy(tail_in[:, f, 11:20], yT[:, f, T - 1:NT]).then_inc(lru_done, 1)

            conv(0)
            for f in range(1, FW):
                conv(f)
                lru(f - 1)
            lru(FW - 1)
            modulation(1)

            def times_gate(f):
                dve.wait_ge(gelu_ready, 2 * (f + 1))
                dve.tensor_tensor(yT[:, f, :], yT[:, f, :], gel[:, f, :], ALU.mult).then_inc(ylru, 1)

            dve.wait_ge(vt_ps, 1)
            dve.tensor_copy(vtok[:, :, :], B[5][:, :].rearrange("p (t d) -> p t d", d=P)).then_inc(vt_ready, 1)
            dve.tensor_copy(klast[:, :], B[6][:, 0:P]).then_inc(vt_ready, 1)
            dve.tensor_copy(knv[:, :, :], B[6][0:NS, P:3 * P].rearrange("p (c d) -> p c d", d=P)).then_inc(vt_ready, 1)
            dve.wait_ge(vt_ps, 2)
            dve.tensor_copy(tails[:, :, :], B[7][0:20, :].rearrange("p (f d) -> p f d", d=P)).then_inc(vt_ready, 1)
            dve.wait_ge(kz_zero, 2)
            dve.wait_ge(q_ready, 2 * FW)
            for kv in range(NKV):
                for half in range(2):
                    dve.tensor_copy(qz[64 * kv:64 * kv + 64, :, kv * G + half:(kv + 1) * G:2].rearrange("p b i -> p i b"),
                                    qT[64 * half:64 * half + 64, 2 * kv:2 * kv + 2, T:NT]).then_inc(qz_ready, 1)
            dve.wait_ge(kv_ready, 2)
            dve.tensor_copy(kbT[:, :, WIN:WIN + 1], kvT[:, 0, T:NT].rearrange("p (b a) -> p b a", a=1)).then_inc(qz_ready, 1)
            times_gate(0)
            times_gate(1)
            dve.wait_ge(ss_ps, 1)
            sc = B[5][:, 0:2 * (WIN + 1)].rearrange("p (n w) -> p n w", w=WIN + 1)
            step(dve.tensor_copy(ps[:, :, :], sc))
            link(dve.tensor_reduce(sv[:, 0, :], sc, AX.X, ALU.max))
            link(dve.tensor_scalar(sv[:, 1, :], sv[:, 0, :], sink_s[:, 1:2], None, ALU.max))
            dve.tensor_scalar(sv[:, 2, :], sv[:, 1, :], -SCALE, None, ALU.mult).then_inc(snb_ready, 1)
            times_gate(2)
            dve.wait_ge(sexp_done, 4)
            link(dve.tensor_tensor(sv[:, 5, :], sv[:, 4, :], sv[:, 3, :], ALU.add))
            link(dve.reciprocal(sv[:, 6, :], sv[:, 5, :]))
            for n in range(2):
                link(dve.tensor_scalar(ps[:, n, :], ps[:, n, :], sv[:, 6, n:n + 1], None, ALU.mult))
                dve.tensor_scalar(pnm[:, n, :], bsel[:, n, :], ps[:, n, WIN:WIN + 1], None, ALU.mult).then_inc(sP_ready, 1)
            times_gate(3)

            def mask_rows(b):
                keys = slice(0, 2 * P) if b else slice(P, 2 * P)
                kn = 2 * P if b else P
                if b >= 3:
                    dve.wait_ge(PT_ps, 2 + 4 * (b - 3))
                for h in range(NH):
                    if h % 2 == 0:
                        dve.wait_ge(S_ps, 4 * b + h // 2 + 1)
                    dve.tensor_tensor_reduce(out=Pm[b % 3][:, h, keys], in0=B[h // 2][:, (h % 2) * kn:(h % 2 + 1) * kn],
                                             in1=mask[:, :, :].rearrange("p a k -> p (a k)")[:, keys], scale=1.0, scalar=NEG,
                                             op0=ALU.add, op1=ALU.max, accum_out=mx[:, b % 2, h:h + 1]).then_inc(S_masked, 1)
                dve.wait_ge(S_masked, NH * (b + 1))
                link(dve.tensor_tensor(mx[:, b % 2, :], mx[:, b % 2, :], sinks8[:, 1, :], ALU.max))
                dve.tensor_scalar(nb[:, b % 2, :], mx[:, b % 2, :], -SCALE, None, ALU.mult).then_inc(nb_ready, 1)
                dve.wait_ge(nb_ready, 2 * b + 1)
                dve.tensor_tensor(es[:, b % 2, :], sinks8[:, 0, :], nb[:, b % 2, :], ALU.add).then_inc(nb_ready, 1)

            def denominators(b):
                dve.wait_ge(exp_done, (NH + 1) * (b + 1))
                if b >= 2:
                    dve.wait_ge(P_ready, G * (b - 1))
                link(dve.tensor_tensor(sums[:, b % 2, :], sums[:, b % 2, :], es[:, b % 2, :], ALU.add))
                dve.reciprocal(rden[:, b % 2, :], sums[:, b % 2, :]).then_inc(rden_ready, 1)
                dve.wait_ge(rden_ready, b + 1)
                keys = slice(0, 2 * P) if b else slice(P, 2 * P)
                for h in range(G):
                    dve.tensor_scalar(Pm[b % 3][:, h, keys], Pm[b % 3][:, h, keys], rden[:, b % 2, h:h + 1], None,
                                      ALU.mult).then_inc(Pv_ready, 1)

            def store_O(b):
                dve.wait_ge(O_ps, b + 1)
                for kv in range(NKV):
                    for half in range(2):
                        i = dve.tensor_copy(yT[64 * half:64 * half + 64, FW + 2 * kv:FW + 2 * kv + 2, b * P:(b + 1) * P],
                                            B[6][64 * kv:64 * kv + 64, :].rearrange("p (g q) -> p g q", q=P)[:, half::2, :])
                        if half:
                            i.then_inc(O_stored, 1)
                        else:
                            step(i)

            for b in range(TT + 2):
                if b < TT:
                    mask_rows(b)
                if b == 0:
                    dve.wait_ge(sPT_ps, 1)
                    dve.tensor_copy(psT[:, :, :], B[6][:, 0:2 * P].rearrange("p (n m) -> p n m", m=P)).then_inc(sPT_ready, 1)
                    dve.tensor_copy(pnd[:, :, :], B[7][0:NS, 0:2 * P].rearrange("p (n m) -> p n m", m=P)).then_inc(sPT_ready, 1)
                if 1 <= b <= TT:
                    denominators(b - 1)
                if b == 1:
                    dve.wait_ge(sO_ps, 1)
                    for kv in range(NKV):
                        for half in range(2):
                            i = dve.tensor_copy(yT[64 * half:64 * half + 64, FW + 2 * kv:FW + 2 * kv + 2, T:NT].rearrange("p i b -> p b i"),
                                                B[5][64 * kv:64 * kv + 64, 0:NS * 32].rearrange("p (b h) -> p b h", h=32)[:, :, kv * G + half:(kv + 1) * G:2])
                            if half:
                                i.then_inc(sO_stored, 1)
                            else:
                                step(i)
                if b == 2:
                    dve.wait_ge(sq_ready, FW)
                    for f in range(FW):
                        dve.tensor_scalar(yT[:, f, :], yT[:, f, :], par[:, 32 + f:33 + f], None, ALU.mult).then_inc(yg_ready, 1)
                if b >= 2:
                    store_O(b - 2)
                if b == 3:
                    modulation(2)
            dve.wait_ge(ss_sum_ps, 1)
            dve.tensor_scalar(rs[:, :], B[4][:, 0:264], 1.0 / W, RMS_EPS, ALU.mult, ALU.add).then_inc(ms_ready, 1)
            for f in range(FW, 2 * FW):
                dve.tensor_scalar(yT[:, f, :], yT[:, f, :], par[:, 32 + f:33 + f], None, ALU.mult).then_inc(yg_ready, 1)
            dve.wait_ge(rs_ready, 1)
            dve.reciprocal(rs[:, :], rs[:, :]).then_inc(rs_ready, 1)
            dve.wait_ge(ss_sum_ps, 2)
            for c in range(2):
                dve.tensor_copy(rT[:, 0:TT, :].rearrange("p (h c) g -> p h c g", c=2)[:, :, c, :],
                                B[5][:, c * P:(c + 1) * P].rearrange("p (g h x) -> p h g x", g=2, h=2)[:, :, :, 0]).then_inc(rT_ready, 1)
            dve.tensor_copy(rT[0:NS, TT, :], B[5][0:NS, 2 * P:3 * P].rearrange("p (g h x) -> p g h x", g=2, h=2)[:, :, 1, 0]).then_inc(rT_ready, 1)
            dve.wait_ge(rT_ready, 3)
            dve.wait_ge(mod_in, 16 * 5)

            def layer_norm_stats(src, n, i):
                for c in range(2):
                    step(dve.bn_stats(bn[0:n, c, :], src[:, c * 512:(c + 1) * 512]))
                settle()
                link(dve.bn_aggr(mv[0:n, :], bn[0:n, :, :].rearrange("p a b -> p (a b)")))
                dve.tensor_scalar(st1[0:n, 0:1], mv[0:n, 1:2], LN_EPS, None, ALU.add).then_inc(var_ready, 1)
                dve.wait_ge(std_ready, i + 1)
                link(dve.reciprocal(st1[0:n, 2:3], st1[0:n, 1:2]))
                dve.scalar_tensor_tensor(out=st1[0:n, 3:4], in0=mv[0:n, 0:1], scalar=-1.0, in1=st1[0:n, 2:3],
                                         op0=ALU.mult, op1=ALU.mult).then_inc(norm_ready, 1)

            def copy_h2T(i, t, n):
                dve.wait_ge(h2T_ps, 2 * i + 1)
                dve.tensor_copy(h2T[:, 0:4, t * P:t * P + n], B[4][:, :].rearrange("p (k m) -> p k m", m=P)[:, :, 0:n]).then_inc(h2T_v, 1)

            def residual(i, t, n):
                gate = mod[:, 0, :] if t < TT else smod[0:NS, 0, :]
                dve.wait_ge(A_ps, min(i + 1, TT - 1) if i < TT else TT)
                dve.wait_ge(L_ready, 2 * (i + 1))
                for c in range(2):
                    src = B[2 + c][:, :] if t < TT else B[7][64 + 32 * c:64 + 32 * c + n, :]
                    dve.scalar_tensor_tensor(out=u[0:n, i % 2, c * 512:(c + 1) * 512], in0=src, scalar=rT[0:n, t, 1:2],
                                             in1=u[0:n, i % 2, c * 512:(c + 1) * 512], op0=ALU.mult, op1=ALU.add).then_inc(A_used, 1)
                if i >= 1:
                    copy_h2T(*MIX[i - 1])
                dve.wait_ge(A_used, 2 * (i + 1))
                link(dve.tensor_tensor(u[0:n, i % 2, :], u[0:n, i % 2, :], gate, ALU.mult))
                link(dve.scalar_tensor_tensor(out=u[0:n, i % 2, :], in0=x_tok[0:n, t, :], scalar=ALPHA, in1=u[0:n, i % 2, :],
                                              op0=ALU.mult, op1=ALU.add))
                layer_norm_stats(u[0:n, i % 2, :], n, i)

            def modulate2(i, t, n):
                scale = mod[:, 1, :] if t < TT else smod[0:NS, 1, :]
                shift = mod[:, 2, :] if t < TT else smod[0:NS, 2, :]
                dve.wait_ge(xhat_ready, i + 1)
                if i >= 2:
                    dve.wait_ge(h2_stored[i % 2], 16 * (i // 2))
                    dve.wait_ge(h2T_ps, 2 * (i - 1))
                link(dve.tensor_tensor(h2[0:n, i % 2, :], u[0:n, i % 2, :], scale, ALU.mult))
                dve.tensor_tensor(h2[0:n, i % 2, :], h2[0:n, i % 2, :], shift, ALU.add).then_inc(h2_ready, 1)

            dve.wait_ge(rows_ready, 1)
            for i in range(TT + 2):
                if i == TT - 1:
                    dve.wait_ge(rows_ready, 2)
                if i <= TT:
                    residual(*MIX[i])
                    modulate2(*MIX[i])
                else:
                    copy_h2T(*MIX[TT])
            dve.wait_ge(lgT_ps, 1)
            dve.tensor_scalar(LGT[:, 0:T - P], B[6][0:NG + NE, 0:T - P], brt[:, 0:1], None, ALU.add).then_inc(lgT_ready, 1)
            dve.wait_ge(lgT_ps, 2)
            dve.tensor_scalar(LGT[:, T - P:NT], B[7][0:NG + NE, 0:P + NS], brt[:, 0:1], None, ALU.add).then_inc(lgT_ready, 1)

            def per_tile(v, n):
                return v.rearrange("p (t a) -> p t a", a=1).broadcast_to((P, TT + 1, n))

            def numbers(n):
                return iota_e[:, 0:n].rearrange("p (a n) -> p a n", a=1).broadcast_to((P, TT + 1, n))

            def first_of(value, best, n, out):
                e_, c_ = eq[:, :, 0:n], cand[:, :, 0:n]
                link(dve.tensor_tensor(e_, value, per_tile(best, n), ALU.is_equal))
                link(dve.scalar_tensor_tensor(out=c_, in0=e_, scalar=-1024.0, in1=numbers(n), op0=ALU.mult, op1=ALU.add))
                link(dve.tensor_reduce(col[:, 6, :], c_, AX.X, ALU.min))
                link(dve.tensor_tensor(out, c_, per_tile(col[:, 6, :], n), ALU.is_equal))

            link(dve.memset(LG[:, TT, :], 0.0))
            dve.wait_ge(lg_ps, 1)
            step(dve.tensor_copy(LG[:, 0:TT, :], B[6][:, 0:TT * (NG + NE)].rearrange("p (t e) -> p t e", e=NG + NE)))
            step(dve.tensor_copy(LG[0:NS, TT, :], B[6][0:NS, TT * (NG + NE):(TT + 1) * (NG + NE)]))
            settle()
            link(dve.tensor_reduce(col[:, 0, :], LG[:, :, 0:NG], AX.X, ALU.max))
            dve.tensor_tensor(gt[:, 0, :, :], LG[:, :, 0:NG], per_tile(col[:, 0, :], NG), ALU.subtract).then_inc(top_ready, 1)
            first_of(LG[:, :, 0:NG], col[:, 0, :], NG, gt[:, 2, :, :])
            link(dve.tensor_scalar(gt[:, 3, :, :], gt[:, 2, :, :], 1.0, -NEG, ALU.subtract, ALU.mult))
            for e in range(EPG):
                step(dve.tensor_tensor(le[:, :, e::EPG], LG[:, :, NG + e::EPG], gt[:, 3, :, :], ALU.add))
            settle()
            link(dve.tensor_reduce(col[:, 1, :], le[:, :, :], AX.X, ALU.max))
            first_of(le[:, :, :], col[:, 1, :], NE, oh[:, :, 0, :])
            link(dve.scalar_tensor_tensor(out=le[:, :, :], in0=oh[:, :, 0, :], scalar=2 * NEG, in1=le[:, :, :], op0=ALU.mult, op1=ALU.add))
            link(dve.tensor_reduce(col[:, 2, :], le[:, :, :], AX.X, ALU.max))
            first_of(le[:, :, :], col[:, 2, :], NE, oh[:, :, 1, :])
            dve.tensor_tensor(hot[:, :, :], oh[:, :, 0, :], oh[:, :, 1, :], ALU.add).then_inc(hot_ready, 1)
            dve.tensor_tensor(col[:, 4, :], col[:, 2, :], col[:, 1, :], ALU.subtract).then_inc(top_ready, 1)

            dve.wait_ge(count_ps, 1)
            link(dve.tensor_reduce(pmax[:, :], B[5][:, 0:NE].rearrange("p (a b) -> p a b", b=2), AX.X, ALU.max))
            link(dve.tensor_scalar(pnum_i[:, 0, :], pmax[:, :], 1.0, float(CAP - 1), ALU.max, ALU.add))
            link(dve.tensor_scalar(pnum_i[:, 1, :], pnum_i[:, 0, :], 6, None, ALU.arith_shift_right))
            link(dve.tensor_copy(pnum[:, :], pnum_i[:, 1, :]))
            link(dve.tensor_tensor_scan(pend[:, :], ones[:, 0:NPAIR], pnum[:, :], 0.0, ALU.mult, ALU.add))
            step(dve.tensor_copy(pend_i[:, :], pend[:, :]))
            link(dve.tensor_tensor(pmax[:, :], pend[:, :], pnum[:, :], ALU.subtract))
            for h in range(2):
                step(dve.tensor_scalar(pbase[:, :, h], pmax[:, :], float(h * NSTEP * CAP), None, ALU.add))
            settle()
            link(dve.tensor_tensor(ohb[:, :, :], oh[:, :, :, :].rearrange("p t c e -> p (t c) e"),
                                   pbase[:, :, :].rearrange("p (a n) h -> p a (n h)", a=1).broadcast_to((P, (TT + 1) * 2, NE)), ALU.mult))
            link(dve.tensor_reduce(base_of[:, :, :].rearrange("p t c -> p (t c)"), ohb[:, :, :], AX.X, ALU.add))
            dve.wait_ge(rank_ps, 1)
            for c in range(2):
                step(dve.tensor_tensor(rk[:, c::2, :], oh[:, :, c, :], B[7][:, 0:(TT + 1) * NE].rearrange("p (t e) -> p t e", e=NE), ALU.mult))
            settle()
            link(dve.tensor_reduce(rank[:, :, :].rearrange("p t c -> p (t c)"), rk[:, :, :], AX.X, ALU.add))
            link(dve.tensor_copy(rank_i[:, 0, :, :], rank[:, :, :]))
            link(dve.tensor_scalar(rank_i[:, 1, :, :], rank_i[:, 0, :, :], 6, None, ALU.arith_shift_right))
            link(dve.scalar_tensor_tensor(out=base_of[:, :, :], in0=rank[:, :, :], scalar=float(NSTEP), in1=base_of[:, :, :],
                                          op0=ALU.mult, op1=ALU.add))
            dve.scalar_tensor_tensor(out=slot[:, :, :], in0=rank_i[:, 1, :, :], scalar=float(1 - CAP * NSTEP), in1=base_of[:, :, :],
                                     op0=ALU.mult, op1=ALU.add).then_inc(slot_ready, 1)
            dve.wait_ge(top_exp, 2)
            link(dve.tensor_reduce(col[:, 3, :], gt[:, 1, :, :], AX.X, ALU.add))
            link(dve.scalar_tensor_tensor(out=col[:, 7, :], in0=col[:, 5, :], scalar=1.0, in1=col[:, 3, :], op0=ALU.add, op1=ALU.mult))
            link(dve.reciprocal(wt[:, :, 0], col[:, 7, :]))
            step(dve.tensor_tensor(wt[:, :, 1], wt[:, :, 0], col[:, 5, :], ALU.mult))
            dve.wait_ge(rows_ready, 3)
            link(dve.tensor_tensor(past[:, :, :], sgrid[:, :, :],
                                   pend[:, :].rearrange("p (a n) -> p a n", a=1).broadcast_to((P, NSTEP, NPAIR)), ALU.is_ge))
            link(dve.tensor_reduce(spair[:, :], past[:, :, :], AX.X, ALU.add))
            link(dve.tensor_scalar(spair[:, :], spair[:, :], float(NPAIR - 1), None, ALU.min))
            link(dve.tensor_scalar(third[:, :], spair[:, :], 11.0, None, ALU.mult))
            link(dve.tensor_scalar(third[:, :], third[:, :], 5, None, ALU.arith_shift_right))
            step(dve.scalar_tensor_tensor(out=place_i[:, :], in0=third[:, :], scalar=float(-SETS), in1=spair[:, :],
                                          op0=ALU.mult, op1=ALU.add))
            step(dve.tensor_scalar(wneed[:, 0, :], third[:, :], 64.0, 64.0, ALU.mult, ALU.add))
            step(dve.tensor_scalar(wneed[:, 1, :], third[:, :], 32.0, 80.0, ALU.mult, ALU.add))
            link(dve.tensor_scalar(turns[:, 1:2], pend[:, NPAIR - 1:NPAIR], float(RING - 1), None, ALU.add))
            dve.tensor_scalar(turns[:, 0:1], turns[:, 1:2], 2, None, ALU.arith_shift_right).then_inc(steps_ready, 1)
            dve.wait_ge(steps_ready, 1)

            def copy_XT(s, n):
                dve.wait_ge(XT_ps, 2 * n + 1)
                dve.tensor_copy(XT[:, s % 2, 0:4, :], B[0][:, :].rearrange("p (k m) -> p k m", m=P)).then_inc(XT_v, 1)

            def turn(i, peeled):
                for j in range(RING):
                    n = RING * i + j
                    dve.wait_ge(silu_done, n + 1)
                    if not (peeled and j == 0):
                        dve.wait_ge(zT_ps, n)
                    dve.tensor_tensor(z[:, :], silu_g[:, :], B[2 + j % 2][:, DE:2 * DE], ALU.mult).then_inc(z_ready, 1)
                    copy_XT(j + 1, n + 1)
                    dve.wait_ge(y_ps, n + 1)
                    if not peeled:
                        dve.wait_ge(y_out[j], 16 * i)
                    dve.tensor_copy(yo[:, j, 0:512], B[5][:, :]).then_inc(y_v, 1)

            copy_XT(0, 0)
            turn(0, True)
            with dve.Fori(1, MINTURNS) as i:
                turn(i, False)
            nturns = dve.value_load(turns[0:1, 0:1], min_val=MINTURNS, max_val=TURNS)
            with dve.Fori(MINTURNS, TURNS) as i:
                with dve.If(nturns > i):
                    turn(i, False)
            for t, n in TILES:
                for c in range(2):
                    dve.tensor_scalar(wdiag[0:n, t, c, 0:n], ident[0:n, 0:n], wt[0:n, t, c:c + 1], None, ALU.mult).then_inc(wdiag_ready, 1)
            dve.wait_ge(lnp_in, 96)
            for t, n in TILES:
                f = yy[0:n, t, 0, :]
                for c in range(2):
                    dve.wait_ge(ysum_ps, 2 * t + c + 1)
                    gate = mod[:, 0, c * 512:(c + 1) * 512] if t < TT else smod[0:NS, 3, c * 512:(c + 1) * 512]
                    dve.tensor_tensor(f[:, c * 512:(c + 1) * 512], B[2 * (t % 2) + c][0:n, :], gate, ALU.mult).then_inc(gated, 1)
                dve.wait_ge(gated, 2 * (t + 1))
                link(dve.scalar_tensor_tensor(out=f, in0=x_tok[0:n, t, :], scalar=ALPHA, in1=f, op0=ALU.mult, op1=ALU.add))
                layer_norm_stats(f, n, TT + 1 + t)
            dve.wait_ge(xhat_ready, 2 * (TT + 1))
            link(dve.tensor_tensor(f, f, mod[0:NS, 3, :], ALU.mult))
            dve.wait_ge(out_done[0], 16 * (TT // 2))
            dve.wait_ge(out_ready, TT)
            dve.tensor_tensor(yout[0:NS, 0, :], f, mod[0:NS, 4, :], ALU.add).then_inc(out_ready, 1)

        @block.tensor
        def _(pe):
            pe.wait_ge(consts, 2)
            pe.wait_ge(csil_ready, 1)
            for k in range(KD):
                last = pe.transpose(B[7][:, 16 * k:16 * k + NC], csil[:, k::KD], ident[0:NC, 0:NC])
            last.then_inc(cT_ps, 1)
            def modulation(chunks):
                for j in chunks:
                    r, k = j // KD, j % KD
                    if r == 1 and k == 0:
                        pe.wait_ge(m_ready, r)
                    if j >= 3 * KD - 4:
                        pe.wait_ge(ada_in[j % 4], 48)
                    elif r:
                        pe.wait_ge(ada2_in[j % 4], 16 * ((j - KD) // 4 + 1))
                    else:
                        pe.wait_ge(ada_in[j % 4], 16 * (j // 4 + 1))
                    for g in range(4):
                        last = pe.matmul(B[7 if r == 2 else 4][32 * g:32 * g + 32, :], cT[:, k, :], ada[:, j % 4, g * 512:(g + 1) * 512],
                                         start=(k == 0), stop=(k == KD - 1))
                    last.then_inc(ada_used, 1)

            pe.wait_ge(cT_ready, 1)
            for k in range(KD):
                if k % 3 == 0:
                    modulation([k // 3])
                if k == 0:
                    pe.wait_ge(x_in, 32)
                if k >= 4:
                    if k % 2:
                        pe.wait_ge(xT_a, (k - 4) // 2 + 1)
                    else:
                        pe.wait_ge(xT_v, (k - 4) // 2 + 1)
                for t in range(TT):
                    last = pe.transpose(B[k % 4][:, t * P:(t + 1) * P], x_tok[:, t, k::KD], ident[:, :])
                last.then_inc(xT_ps, 1)
            for k in range(KD):
                last = pe.transpose(B[6][:, NS * k:NS * k + NS], x_tok[0:NS, TT, k::KD], ident[0:NS, 0:NS])
            last.then_inc(xs_ps, 1)
            modulation([3])
            pe.wait_ge(small_in, 16 * 14)
            pe.transpose(B[5][:, 0:40], prm[:, :], ident[0:40, 0:40])
            for f in range(FW):
                last = pe.transpose(B[5][:, 64 + 32 * f:96 + 32 * f], stt_in[:, f * P:(f + 1) * P], ident[0:32, 0:32])
            last.then_inc(small_ps, 1)

            modulation(range(4, KD))
            pe.wait_ge(m_ready, 1)
            pe.wait_ge(small_ready, 2)
            for k in range(KD):
                last = pe.transpose(B[5 + 2 * (k // 4)][0:64, (k % 4) * P:(k % 4 + 1) * P], m_sb[:, 0, k::KD], ident[:, :])
            last.then_inc(mT_ps, 1)

            def evacuated(q):
                if q < K_AT and q % 2 == 0:
                    pe.wait_ge(zin_ready, 3 * (q // 2 + 1))
                elif q < K_AT:
                    pe.wait_ge(q_ready, 2 * (q // 2 + 1))
                elif q < GELU_AT:
                    pe.wait_ge(kv_ready, 2 * (q - K_AT + 1))
                else:
                    pe.wait_ge(gelu_ready, 2 * (q - GELU_AT + 1))

            def project_in(q):
                n = WCH.index(ORDER[q] // 2)
                pe.wait_ge(win_in[n % 3], 16 * (n // 3 + 1))
                if q >= 2:
                    evacuated(q - 2)
                col = (ORDER[q] % 2) * P
                for h, (c0, cn) in enumerate(HALVES):
                    for k in range(KD):
                        if q == 0 and h == 0:
                            if k % 2:
                                pe.wait_ge(h_a, k // 2 + 1)
                            else:
                                pe.wait_ge(h_v, k // 2 + 1)
                        if q == 0 and h == 1 and k == 0:
                            pe.wait_ge(h_v, 5)
                        last = pe.matmul(B[(q % 2) * 2 + h][:, 0:cn], win[:, n % 3, k, col:col + P], hT[:, k, c0:c0 + cn],
                                         start=(k == 0), stop=(k == KD - 1))
                    last.then_inc(win_ps, 1)

            def lru_gate(f, g):
                pe.wait_ge(xc_ready, f + 1)
                if f == 0:
                    pe.wait_ge(wrg_in, 16 * 4)
                    pe.wait_ge(mT_ready, 4)
                for h in range(2):
                    if 2 * f + g:
                        pe.wait_ge(gate_tanh, 4 * f + 2 * (g - 1) + h + 1)
                    pe.matmul(B[6 + h][:, 0:XH], wrg[:, g, f, :], xc[:, f % 3, h * XH:(h + 1) * XH],
                              start=True, stop=True).then_inc(gate_ps, 1)

            def token_major():
                pe.wait_ge(kv_ready, 4)
                pe.wait_ge(gate_tanh, 4 * FW)
                for t in range(TT):
                    pe.transpose(B[5][:, t * P:(t + 1) * P], kvT[:, 1, t * P:(t + 1) * P], ident[:, :])
                pe.transpose(B[6][:, 0:P], kvT[:, 0, T - P:T], ident[:, :])
                for n in range(2):
                    last = pe.transpose(B[6][0:NS, (1 + n) * P:(2 + n) * P], kvT[:, n, T:NT], ident[:, :])
                last.then_inc(vt_ps, 1)
                pe.wait_ge(lru_done, FW)
                for f in range(FW):
                    last = pe.transpose(B[7][0:20, f * P:(f + 1) * P], tail_in[:, f, :], ident[:, :])
                last.then_inc(vt_ps, 1)

            def cached_keys():
                pe.wait_ge(vt_ready, 4)
                pe.wait_ge(kv_in, 16 * 4)
                for b in range(NS):
                    last = pe.transpose(B[6 + b // 4][:, (b % 4) * P:(b % 4 + 1) * P], kc[:, b, :], ident[:, :])
                    if b % 4 == 3:
                        last.then_inc(kcT_ps, 1)

            def sample_scores():
                pe.wait_ge(kcT_ready, 2)
                pe.wait_ge(qz_ready, 5)
                for b in range(NS):
                    j = b % 4
                    c0 = (b // 4) * (WIN + 1)
                    last = pe.matmul(B[5][32 * j:32 * j + 32, c0:c0 + WIN + 1], qz[:, b, :], kbT[:, b, :], start=True, stop=True)
                last.then_inc(ss_ps, 1)

            for q in range(len(ORDER)):
                project_in(q)
                if q == GELU_AT:
                    token_major()
                if q == GELU_AT + 1:
                    cached_keys()
                if q == GELU_AT + 2:
                    sample_scores()
                if 1 <= q <= K_AT:
                    lru_gate((q - 1) // 2, (q - 1) % 2)
                if 1 <= q <= KD:
                    modulation([KD + q - 1])

            def scores(b):
                k0 = max(0, b - 1) * P
                kn = (b + 1) * P - k0
                for p in range(NH // 2):
                    if b:
                        pe.wait_ge(S_masked, NH * (b - 1) + 2 * p + 2)
                    pe.matmul(B[p][:, 0:2 * kn], qT[:, p, b * P:(b + 1) * P], kTz[:, p // 2, :, k0:k0 + kn],
                              start=True, stop=True).then_inc(S_ps, 1)

            def pt_count(b):
                return 0 if b == 0 else 2 + 4 * (b - 1)

            def weigh(b):
                first = pt_count(b)
                kbs = (0, 1) if b else (1,)
                n = 0
                for kv in range(NKV):
                    pe.wait_ge(P_ready if kv else Pv_ready, G * (b + 1))
                    for kb in kbs:
                        if first + n >= 2:
                            pe.wait_ge(PT_ready, first + n - 1)
                        for g in range(G):
                            last = pe.transpose(B[4 + n % 2][:, g * P:(g + 1) * P],
                                                Pm[b % 3][:, kv * G + g, kb * P:(kb + 1) * P], ident[:, :])
                        last.then_inc(PT_ps, 1)
                        n += 1
                if b:
                    pe.wait_ge(O_stored, 2 * b)
                pe.wait_ge(PT_ready, first + n)
                for kb in kbs:
                    for kv in range(NKV):
                        last = pe.matmul(B[6][64 * kv:64 * kv + 64, :], vtok[:, b - 1 + kb, 64 * kv:64 * kv + 64],
                                         PT[:, kb, kv, :], start=(kb == kbs[0]), stop=(kb == 1))
                last.then_inc(O_ps, 1)

            evacuated(GELU_AT + 2)
            evacuated(GELU_AT + 3)
            scores(0)
            pe.wait_ge(sP_ready, 2)
            for n in range(2):
                pe.transpose(B[6][:, n * P:(n + 1) * P], ps[:, n, 0:WIN], ident[:, :])
            for n in range(2):
                last = pe.transpose(B[7][0:NS, n * P:(n + 1) * P], pnm[:, n, :], ident[:, :])
            last.then_inc(sPT_ps, 1)
            scores(1)
            pe.wait_ge(sPT_ready, 2)
            for b in range(NS):
                pe.matmul(B[5][:, 32 * b:32 * b + 32], knv[:, 1, :], pnd[:, b // 4, 32 * (b % 4):32 * (b % 4) + 32], start=True, stop=False)
                last = pe.matmul(B[5][:, 32 * b:32 * b + 32], vc[:, b, :], psT[:, b // 4, 32 * (b % 4):32 * (b % 4) + 32],
                                 start=False, stop=True)
            last.then_inc(sO_ps, 1)
            pe.wait_ge(m_ready, 2)
            pe.wait_ge(sO_stored, 2)
            for b in range(TT):
                if b < 3:
                    modulation(range(2 * KD + (0, 4, 6)[b], 2 * KD + (4, 6, 8)[b]))
                if b + 2 < TT:
                    scores(b + 2)
                weigh(b)

            def first_lru_part(c):
                for f in range(FW):
                    last = pe.matmul(B[c][:, :], yT[:, f, 0:P], wout[:, f, c * 512:(c + 1) * 512], start=(f == 0), stop=(f == FW - 1))
                if c:
                    last.then_inc(L_ps, 1)

            pe.wait_ge(S_masked, NH * TT)
            pe.wait_ge(yg_ready, FW)
            pe.wait_ge(wout_in, 16)
            first_lru_part(0)
            pe.wait_ge(PT_ready, pt_count(TT))
            for f in range(FW):
                for g in range(2):
                    pe.wait_ge(sq_ready, 4 * g + f + 1 if g == 0 else 2 * FW)
                    for h in range(2):
                        j = 2 * g + h
                        last = pe.matmul(B[4][32 * j:32 * j + 32, 0:264], ones[:, :], sq[:, 4 * g + f, h * HALF:h * HALF + 264],
                                         start=(f == 0), stop=(f == FW - 1))
            last.then_inc(ss_sum_ps, 1)
            first_lru_part(1)
            pe.wait_ge(rs_ready, 2)
            for c in range(2):
                pe.transpose(B[5][:, c * P:(c + 1) * P], rs[:, c * P:(c + 1) * P], ident[:, :])
            pe.transpose(B[5][0:NS, 2 * P:3 * P], rs[:, 2 * P:2 * P + NS], ident[:, :]).then_inc(ss_sum_ps, 1)

            def project_out(i, t, n, groups=(0, 1)):
                if t == 0:
                    pe.wait_ge(yg_ready, 2 * FW)
                if t < TT:
                    for g in groups:
                        if i:
                            pe.wait_ge(A_used if g else L_ready, 2 * (i if i < TT else i - 1))
                        for f in range(FW):
                            for c in range(2):
                                last = pe.matmul(B[2 * g + c][:, :], yT[:, FW * g + f, t * P:(t + 1) * P],
                                                 wout[:, FW * g + f, c * 512:(c + 1) * 512], start=(f == 0), stop=(f == FW - 1))
                        last.then_inc(A_ps if g else L_ps, 1)
                else:
                    pe.wait_ge(m_ready, 4)
                    for f in range(FW):
                        for g in range(2):
                            for c in range(2):
                                j = 2 * g + c
                                last = pe.matmul(B[7][32 * j:32 * j + n, :], yT[:, FW * g + f, T:NT],
                                                 wout[:, FW * g + f, c * 512:(c + 1) * 512], start=(f == 0), stop=(f == FW - 1))
                    last.then_inc(L_ps, 1)

            def transpose_h2(i, t, n):
                pe.wait_ge(h2_ready, i + 1)
                if i == 0:
                    pe.wait_ge(rT_ready, 3)
                else:
                    pe.wait_ge(h2T_v, i)
                    pe.wait_ge(h2T_a, i)
                for k in range(KD):
                    last = pe.transpose(B[4 + k // 4][:, (k % 4) * P:(k % 4) * P + n], h2[0:n, i % 2, k::KD], ident[0:n, 0:n])
                    if k % 4 == 3:
                        last.then_inc(h2T_ps, 1)

            def logits(bank, c0, cn):
                for k in range(KD):
                    last = pe.matmul(B[bank][0:NG + NE, 0:cn], wr[:, k, :], h2T[:, k, c0:c0 + cn], start=(k == 0), stop=(k == KD - 1))
                last.then_inc(lgT_ps, 1)

            project_out(*MIX[0], groups=(1,))
            for i in range(1, TT):
                project_out(*MIX[i])
                if i < TT - 1:
                    transpose_h2(*MIX[i - 1])
            project_out(*MIX[TT], groups=(0,))
            transpose_h2(*MIX[TT - 2])
            project_out(*MIX[TT], groups=(1,))
            transpose_h2(*MIX[TT - 1])
            pe.wait_ge(wr_in, 16 * 5)
            logits(6, 0, T - P)
            transpose_h2(*MIX[TT])
            pe.wait_ge(h2T_v, TT + 1)
            pe.wait_ge(h2T_a, TT + 1)
            logits(7, T - P, P + NS)
            pe.wait_ge(lgT_ready, 2)
            for t, n in TILES:
                last = pe.transpose(B[6][0:n, t * (NG + NE):(t + 1) * (NG + NE)], LGT[:, t * P:t * P + n], ident[0:NG + NE, 0:NG + NE])
            last.then_inc(lg_ps, 1)
            pe.wait_ge(hot_ready, 1)
            for t, n in TILES:
                last = pe.matmul(B[5][:, 0:NE], ones_bf[0:n, :], hot[0:n, t, :], start=(t == 0), stop=(t == TT))
            last.then_inc(count_ps, 1)
            for t in range(TT + 1):
                for t2 in range(t):
                    pe.matmul(B[7][:, t * NE:(t + 1) * NE], ones_bf[:, :], hot[:, t2, :], start=(t2 == 0), stop=False)
                last = pe.matmul(B[7][:, t * NE:(t + 1) * NE], tri[:, :], hot[:, t, :], start=(t == 0), stop=True)
            last.then_inc(rank_ps, 1)

            def transpose_X(j, i, half):
                for k in range(4 * half, 4 * half + 4):
                    last = pe.transpose(B[half][:, (k % 4) * P:(k % 4 + 1) * P], X[:, j, k::KD], ident[:, :])
                last.then_inc(XT_ps, 1)

            def turn(i, peeled):
                for j in range(RING):
                    n = RING * i + j
                    place = pe.value_load(place_i[0:1, bass.ds(n, 1)], min_val=0, max_val=SETS - 1)
                    need = pe.value_load(wneed[0:1, 0, bass.ds(n, 1)], min_val=64, max_val=64 * NPAIR)
                    need_down = pe.value_load(wneed[0:1, 1, bass.ds(n, 1)], min_val=80, max_val=32 * NPAIR + 48)
                    for pl in range(SETS):
                        with pe.If(place == pl):
                            pe.wait_ge(XT_v, n + 1)
                            pe.wait_ge(XT_a, n + 1)
                            pe.wait_ge(w_in[pl], need)
                            for k in range(KD):
                                for q in range(2):
                                    gu = wex[pl][:, q, 0:GU].rearrange("p (c k f) -> p c k f", c=2, k=KD)
                                    last = pe.matmul(B[2 + j % 2][64 * q:64 * q + 64, :], XT[:, j % 2, k, 64 * q:64 * q + 64],
                                                     gu[:, :, k, :], start=(k == 0), stop=(k == KD - 1))
                            last.then_inc(gu_ps, 1)
                            pe.wait_ge(X_in[(j + 1) % RING], 16 * i + 16 + (16 if j == RING - 1 else 0))
                            transpose_X((j + 1) % RING, i, 0)
                            pe.wait_ge(z_ready, n + 1)
                            for k in range(2):
                                last = pe.transpose(B[4][:, k * P:(k + 1) * P], z[:, k::2], ident[:, :])
                            last.then_inc(zT_ps, 1)
                            transpose_X((j + 1) % RING, i, 1)
                            pe.wait_ge(zT_ready, n + 1)
                            if not (peeled and j == 0):
                                pe.wait_ge(y_v, n)
                                pe.wait_ge(y_a, n)
                            pe.wait_ge(down_in[pl], need_down)
                            for k in range(2):
                                for c in range(2):
                                    for q in range(2):
                                        dn = GU + k * D + c * 512
                                        last = pe.matmul(B[5 + c][64 * q:64 * q + 64, :], zT[:, k, 64 * q:64 * q + 64],
                                                         wex[pl][:, q, dn:dn + 512], start=(k == 0), stop=(k == 1))
                            last.then_inc(y_ps, 1)

            pe.wait_ge(steps_ready, 1)
            pe.wait_ge(X_in[0], 16)
            transpose_X(0, 0, 0)
            transpose_X(0, 0, 1)
            turn(0, True)
            with pe.Fori(1, MINTURNS) as i:
                turn(i, False)
            nturns = pe.value_load(turns[0:1, 0:1], min_val=MINTURNS, max_val=TURNS)
            with pe.Fori(MINTURNS, TURNS) as i:
                with pe.If(nturns > i):
                    turn(i, False)
            pe.wait_ge(wdiag_ready, 2 * (TT + 1))
            for t, n in TILES:
                pe.wait_ge(yy_in[t], 32)
                if t >= 2:
                    pe.wait_ge(gated, 2 * (t - 1))
                for c in range(2):
                    for e in range(2):
                        last = pe.matmul(B[2 * (t % 2) + c][0:n, :], wdiag[0:n, t, e, 0:n], yy[0:n, t, e, c * 512:(c + 1) * 512],
                                         start=(e == 0), stop=(e == 1))
                    last.then_inc(ysum_ps, 1)


_INS = ["x_prompt", "x_sample", "c_prompt", "c_sample", "state_conv", "state_h", "cache_k", "cache_v", "w_ada", "b_ada",
        "w_in", "conv_w", "conv_b", "w_rg_a", "b_rg_a", "w_rg_x", "b_rg_x", "lru_lambda", "sinks", "g_lru", "g_attn",
        "w_out", "ln1_g", "ln1_b", "w_group", "b_group", "w_router", "b_router", "w_gate", "w_up", "w_down",
        "ln2_g", "ln2_b"]
_OUTS = [(1, T, D), (NS, 1, D), (1, 1, CW - 1, W), (1, 1, W), (1, 1, WIN, NKV, HD), (1, 1, WIN, NKV, HD),
         (1, NS, CW - 1, W), (1, NS, W), (1, NS, WIN, NKV, HD), (1, NS, WIN, NKV, HD)]


def kernel(**inputs):
    import numpy as np
    import concourse.bacc as bacc
    from concourse.bass_utils import run_bass_kernel_spmd

    nc = bacc.Bacc("TRN2", target_bir_lowering=False, num_devices=1)
    arrays, A, O = {}, {}, []
    for name in _INS:
        a = np.ascontiguousarray(inputs[name])
        arrays[f"in_{name}"] = a
        A[name] = nc.dram_tensor(f"in_{name}", a.shape, mybir.dt.from_np(a.dtype), kind="ExternalInput").ap()
    for i, shape in enumerate(_OUTS):
        O.append(nc.dram_tensor(f"out_{i}", shape, F32, kind="ExternalOutput").ap())
    build(nc, A, O)
    r = run_bass_kernel_spmd(nc, [arrays], core_ids=[0])
    return tuple(r.results[0][f"out_{i}"] for i in range(len(_OUTS)))
```
